# Optimizing a Trainium2 kernel written in Bass

```python
import math
import jax, jax.numpy as jnp
from jax import lax
import numpy as np

D_MODEL = 1024
BATCH = 1
SEQ = 1024
DEPTH = 1
DEC_BATCH = 8
DEC_SEQ = 8
PAST_LEN = 2048
PAGE_SIZE = 128

HEAD_DIM = 64
N_HEADS = 8
N_KV_HEADS = 2
ATTN_WIDTH = N_HEADS * HEAD_DIM
KV_WIDTH = N_KV_HEADS * HEAD_DIM
ROPE_DIM = HEAD_DIM // 4
ROPE_THETA = 500000.0
IDX_HEADS = 8
IDX_DIM = 64
TOPK_MAX = 256
QBLK = 128
POOL_WIDTH = D_MODEL - ATTN_WIDTH
POOL_WINDOWS = (2, 4, 8, 16)
POOL_GROUP = POOL_WIDTH // len(POOL_WINDOWS)
POOL_STATE = max(POOL_WINDOWS) - 1
MIX_WIDTH = POOL_WIDTH + ATTN_WIDTH
IN_SPLITS = (POOL_WIDTH, ATTN_WIDTH, KV_WIDTH, KV_WIDTH, IDX_HEADS * IDX_DIM, IDX_DIM, IDX_HEADS)
IN_WIDTH = POOL_WIDTH + ATTN_WIDTH + 2 * KV_WIDTH + IDX_HEADS * IDX_DIM + IDX_DIM + IDX_HEADS
N_GROUPS = 4
EXPERTS_PER_GROUP = 8
N_EXPERTS = N_GROUPS * EXPERTS_PER_GROUP
EXPERT_TOPK = 2
EXPERT_HIDDEN = 256
MOE_BLOCK = 128
NORM_EPS = 1e-6

kernel_name = 'hybrid_pool_dsa_hmoe_step'

def rms_norm(x, g):
    xf = x.astype(jnp.float32)
    y = xf * lax.rsqrt(jnp.mean(xf * xf, axis=-1, keepdims=True) + NORM_EPS)
    return (y * g.astype(jnp.float32)).astype(x.dtype)

def rope(x, pos):
    half = ROPE_DIM // 2
    inv = jnp.power(jnp.float32(ROPE_THETA), -jnp.arange(half, dtype=jnp.float32) / half)
    ang = pos.astype(jnp.float32)[:, None] * inv[None, :]
    cos = jnp.cos(ang)[None, :, None, :]
    sin = jnp.sin(ang)[None, :, None, :]
    xr = x[..., :ROPE_DIM].astype(jnp.float32)
    x1, x2 = xr[..., :half], xr[..., half:]
    rot = jnp.concatenate([x1 * cos - x2 * sin, x2 * cos + x1 * sin], axis=-1).astype(x.dtype)
    return jnp.concatenate([rot, x[..., ROPE_DIM:]], axis=-1)

def project(xn, w_in):
    z = xn @ w_in
    B, T, _ = z.shape
    cuts = np.cumsum(np.array(IN_SPLITS))[:-1].tolist()
    u, q, k, v, qi, ki, wi = jnp.split(z, cuts, axis=-1)
    q = q.reshape(B, T, N_HEADS, HEAD_DIM)
    k = k.reshape(B, T, N_KV_HEADS, HEAD_DIM)
    v = v.reshape(B, T, N_KV_HEADS, HEAD_DIM)
    qi = qi.reshape(B, T, IDX_HEADS, IDX_DIM)
    wi = wi * (IDX_HEADS ** -0.5)
    return u, q, k, v, qi, ki, wi

def pool_mix(u_ext, pos0, w_pool, scale):
    P = POOL_STATE
    T = u_ext.shape[1] - P
    csum = jnp.cumsum(u_ext.astype(jnp.float32), axis=1)
    csum = jnp.pad(csum, ((0, 0), (1, 0), (0, 0)))
    pos = pos0 + jnp.arange(T, dtype=jnp.int32)
    cur = u_ext[:, P:].astype(jnp.float32)
    outs = []
    for g, w in enumerate(POOL_WINDOWS):
        c = slice(g * POOL_GROUP, (g + 1) * POOL_GROUP)
        win = csum[:, P + 1:P + 1 + T, c] - csum[:, P + 1 - w:P + 1 - w + T, c]
        cnt = jnp.minimum(pos + 1, w).astype(jnp.float32)[None, :, None]
        d = (win / cnt - cur[..., c]).astype(u_ext.dtype)
        outs.append(d @ w_pool[g])
    return jnp.concatenate(outs, axis=-1) * scale

def indexer_select(qi, wi, ki, qpos, kpos, topk):
    s = jnp.einsum('bthd,bsd->bths', qi, ki, preferred_element_type=jnp.float32) * (IDX_DIM ** -0.5)
    score = jnp.einsum('bths,bth->bts', jax.nn.relu(s), wi.astype(jnp.float32))
    score = jnp.where(kpos[None, None, :] <= qpos[None, :, None], score, -jnp.inf)
    _, sel = lax.top_k(score, topk)
    valid = sel <= qpos[None, :, None]
    return sel, valid

def sparse_attend(q, ksel, vsel, valid):
    B, T, H, Dh = q.shape
    qg = q.reshape(B, T, N_KV_HEADS, H // N_KV_HEADS, Dh)
    s = jnp.einsum('btkgd,btnkd->btkgn', qg, ksel, preferred_element_type=jnp.float32) * (HEAD_DIM ** -0.5)
    s = jnp.where(valid[:, :, None, None, :], s, -jnp.inf)
    p = jax.nn.softmax(s, axis=-1)
    o = jnp.einsum('btkgn,btnkd->btkgd', p.astype(vsel.dtype), vsel)
    return o.reshape(B, T, H * Dh)

def take_rows(rows, idx):
    return jax.vmap(lambda r, i: r[i])(rows, idx)

def dsa_prompt(q, k, v, qi, ki, wi):
    B, S = q.shape[:2]
    nb = S // QBLK
    topk = min(TOPK_MAX, S // 4)
    kpos = jnp.arange(S, dtype=jnp.int32)

    def one_block(args):
        qb, qib, wib, qpos = args
        sel, valid = indexer_select(qib, wib, ki, qpos, kpos, topk)
        return sparse_attend(qb, take_rows(k, sel), take_rows(v, sel), valid)

    to_blocks = lambda t: t.reshape(B, nb, QBLK, *t.shape[2:]).swapaxes(0, 1)
    out = lax.map(one_block, (to_blocks(q), to_blocks(qi), to_blocks(wi), kpos.reshape(nb, QBLK)))
    return out.swapaxes(0, 1).reshape(B, S, ATTN_WIDTH)

def gather_paged(cache, l, page_table, sel, new_rows, past_len):
    DB, T, n = sel.shape
    logical = jnp.minimum(sel, past_len - 1) // PAGE_SIZE
    phys = jnp.take_along_axis(page_table, logical.reshape(DB, T * n), axis=1).reshape(DB, T, n)
    past_rows = cache[l, phys, sel % PAGE_SIZE].astype(new_rows.dtype)
    new_sel = take_rows(new_rows, jnp.clip(sel - past_len, 0, new_rows.shape[1] - 1))
    is_past = (sel < past_len)[..., None, None]
    return jnp.where(is_past, past_rows, new_sel)

def dsa_sample(q, k, v, qi, ki, wi, cache_k, cache_v, cache_idx_k, l, page_table, past_len):
    DB, T = q.shape[:2]
    ki_past = cache_idx_k[l, page_table].reshape(DB, past_len, IDX_DIM).astype(ki.dtype)
    ki_all = jnp.concatenate([ki_past, ki], axis=1)
    qpos = past_len + jnp.arange(T, dtype=jnp.int32)
    kpos = jnp.arange(past_len + T, dtype=jnp.int32)
    topk = min(TOPK_MAX, (past_len + T) // 4)
    sel, valid = indexer_select(qi, wi, ki_all, qpos, kpos, topk)
    ksel = gather_paged(cache_k, l, page_table, sel, k, past_len)
    vsel = gather_paged(cache_v, l, page_table, sel, v, past_len)
    return sparse_attend(q, ksel, vsel, valid)

def hier_moe(h, rg_w, rg_b, re_w, re_b, w_gate, w_up, w_down):
    B, T, D = h.shape
    x = h.reshape(B * T, D)
    N = x.shape[0]
    g_logits = (x @ rg_w).astype(jnp.float32) + rg_b.astype(jnp.float32)
    g_prob = jax.nn.softmax(g_logits, axis=-1)
    g_sel = jnp.argmax(g_logits, axis=-1)
    g_w = jnp.max(g_prob, axis=-1)
    e_logits = ((x @ re_w).astype(jnp.float32) + re_b.astype(jnp.float32)).reshape(N, N_GROUPS, EXPERTS_PER_GROUP)
    e_in = e_logits[jnp.arange(N), g_sel]
    top_w, top_i = lax.top_k(jax.nn.softmax(e_in, axis=-1), EXPERT_TOPK)
    comb = g_w[:, None] * top_w / jnp.sum(top_w, axis=-1, keepdims=True)
    eid = (g_sel[:, None] * EXPERTS_PER_GROUP + top_i).reshape(-1)
    tok = jnp.repeat(jnp.arange(N, dtype=jnp.int32), EXPERT_TOPK)
    wts = comb.reshape(-1)
    M = eid.shape[0]
    order = jnp.argsort(eid)
    se, st, sw = eid[order], tok[order], wts[order]
    counts = jnp.bincount(eid, length=N_EXPERTS)
    starts = jnp.cumsum(counts) - counts
    padded = ((counts + MOE_BLOCK - 1) // MOE_BLOCK) * MOE_BLOCK
    pends = jnp.cumsum(padded)
    pstarts = pends - padded
    dest = pstarts[se] + (jnp.arange(M) - starts[se])
    n_blk = -(-M // MOE_BLOCK) + N_EXPERTS
    row_tok = jnp.full((n_blk * MOE_BLOCK,), N, jnp.int32).at[dest].set(st)
    blk_e = jnp.minimum(jnp.searchsorted(pends, jnp.arange(n_blk) * MOE_BLOCK, side='right'), N_EXPERTS - 1)
    x_pad = jnp.concatenate([x, jnp.zeros((1, D), x.dtype)], axis=0)

    def run_block(args):
        toks, e = args
        xb = x_pad[toks]
        return (jax.nn.silu(xb @ w_gate[e]) * (xb @ w_up[e])) @ w_down[e]

    out = lax.map(run_block, (row_tok.reshape(n_blk, MOE_BLOCK), blk_e)).reshape(n_blk * MOE_BLOCK, D)
    y = jnp.zeros((N, D), jnp.float32).at[st].add(out[dest].astype(jnp.float32) * sw[:, None])
    return y.astype(h.dtype).reshape(B, T, D)

def setup_inputs(seed: int = 0) -> dict:
    key = jax.random.key(seed)
    ks = jax.random.split(key, 24)
    n_pages = PAST_LEN // PAGE_SIZE
    n_pool = (DEC_BATCH * n_pages * 5) // 4
    f32 = jnp.float32
    nrm = lambda k, shape, s: jax.random.normal(k, shape, f32) * s
    page_table = jax.random.permutation(ks[6], n_pool)[:DEC_BATCH * n_pages].reshape(DEC_BATCH, n_pages).astype(jnp.int32)
    return {
        'x_prompt': nrm(ks[0], (BATCH, SEQ, D_MODEL), 1.0),
        'x_sample': nrm(ks[1], (DEC_BATCH, DEC_SEQ, D_MODEL), 1.0),
        'cache_k': nrm(ks[2], (DEPTH, n_pool, PAGE_SIZE, N_KV_HEADS, HEAD_DIM), 1.0),
        'cache_v': nrm(ks[3], (DEPTH, n_pool, PAGE_SIZE, N_KV_HEADS, HEAD_DIM), 1.0),
        'cache_idx_k': nrm(ks[4], (DEPTH, n_pool, PAGE_SIZE, IDX_DIM), 1.0),
        'state_pool': nrm(ks[5], (DEPTH, DEC_BATCH, POOL_STATE, POOL_WIDTH), 1.0),
        'page_table': page_table,
        'norm_mix_g': 1.0 + nrm(ks[7], (DEPTH, D_MODEL), 0.05),
        'w_in': nrm(ks[8], (DEPTH, D_MODEL, IN_WIDTH), D_MODEL ** -0.5),
        'pool_w': nrm(ks[9], (DEPTH, len(POOL_WINDOWS), POOL_GROUP, POOL_GROUP), POOL_GROUP ** -0.5),
        'pool_scale': 1.0 + nrm(ks[10], (DEPTH, POOL_WIDTH), 0.1),
        'w_out': nrm(ks[11], (DEPTH, MIX_WIDTH, D_MODEL), MIX_WIDTH ** -0.5),
        'norm_ffn_g': 1.0 + nrm(ks[12], (DEPTH, D_MODEL), 0.05),
        'router_group_w': nrm(ks[13], (DEPTH, D_MODEL, N_GROUPS), D_MODEL ** -0.5),
        'router_group_b': nrm(ks[14], (DEPTH, N_GROUPS), 0.01),
        'router_expert_w': nrm(ks[15], (DEPTH, D_MODEL, N_EXPERTS), D_MODEL ** -0.5),
        'router_expert_b': nrm(ks[16], (DEPTH, N_EXPERTS), 0.01),
        'expert_w_gate': nrm(ks[17], (DEPTH, N_EXPERTS, D_MODEL, EXPERT_HIDDEN), D_MODEL ** -0.5),
        'expert_w_up': nrm(ks[18], (DEPTH, N_EXPERTS, D_MODEL, EXPERT_HIDDEN), D_MODEL ** -0.5),
        'expert_w_down': nrm(ks[19], (DEPTH, N_EXPERTS, EXPERT_HIDDEN, D_MODEL), EXPERT_HIDDEN ** -0.5),
        'final_norm_g': 1.0 + nrm(ks[20], (D_MODEL,), 0.05),
    }

def reference(x_prompt, x_sample, cache_k, cache_v, cache_idx_k, state_pool, page_table,
              norm_mix_g, w_in, pool_w, pool_scale, w_out, norm_ffn_g,
              router_group_w, router_group_b, router_expert_w, router_expert_b,
              expert_w_gate, expert_w_up, expert_w_down, final_norm_g):
    past_len = page_table.shape[1] * PAGE_SIZE
    hp, hs = x_prompt, x_sample
    kp_l, vp_l, ikp_l, pp_l = [], [], [], []
    ks_l, vs_l, iks_l, ps_l = [], [], [], []
    for l in range(DEPTH):
        moe_args = (router_group_w[l], router_group_b[l], router_expert_w[l], router_expert_b[l],
                    expert_w_gate[l], expert_w_up[l], expert_w_down[l])
        B, S, _ = hp.shape
        u, q, k, v, qi, ki, wi = project(rms_norm(hp, norm_mix_g[l]), w_in[l])
        pos = jnp.arange(S, dtype=jnp.int32)
        q, k, qi = rope(q, pos), rope(k, pos), rope(qi, pos)
        ki = rope(ki[:, :, None, :], pos)[:, :, 0, :]
        u_ext = jnp.concatenate([jnp.zeros((B, POOL_STATE, POOL_WIDTH), u.dtype), u], axis=1)
        pool_o = pool_mix(u_ext, 0, pool_w[l], pool_scale[l])
        attn_o = dsa_prompt(q, k, v, qi, ki, wi)
        hp = hp + jnp.concatenate([pool_o, attn_o], axis=-1) @ w_out[l]
        hp = hp + hier_moe(rms_norm(hp, norm_ffn_g[l]), *moe_args)
        kp_l.append(k); vp_l.append(v); ikp_l.append(ki); pp_l.append(u_ext[:, -POOL_STATE:])
        T = hs.shape[1]
        u, q, k, v, qi, ki, wi = project(rms_norm(hs, norm_mix_g[l]), w_in[l])
        pos = past_len + jnp.arange(T, dtype=jnp.int32)
        q, k, qi = rope(q, pos), rope(k, pos), rope(qi, pos)
        ki = rope(ki[:, :, None, :], pos)[:, :, 0, :]
        u_ext = jnp.concatenate([state_pool[l].astype(u.dtype), u], axis=1)
        pool_o = pool_mix(u_ext, past_len, pool_w[l], pool_scale[l])
        attn_o = dsa_sample(q, k, v, qi, ki, wi, cache_k, cache_v, cache_idx_k, l, page_table, past_len)
        hs = hs + jnp.concatenate([pool_o, attn_o], axis=-1) @ w_out[l]
        hs = hs + hier_moe(rms_norm(hs, norm_ffn_g[l]), *moe_args)
        ks_l.append(k); vs_l.append(v); iks_l.append(ki); ps_l.append(u_ext[:, -POOL_STATE:])
    y_prompt = rms_norm(hp, final_norm_g)
    y_sample = rms_norm(hs, final_norm_g)
    k_prompt, v_prompt = jnp.stack(kp_l), jnp.stack(vp_l)
    idx_k_prompt, pool_prompt = jnp.stack(ikp_l), jnp.stack(pp_l)
    k_sample, v_sample = jnp.stack(ks_l), jnp.stack(vs_l)
    idx_k_sample, pool_sample = jnp.stack(iks_l), jnp.stack(ps_l)
    return (y_prompt, y_sample, k_prompt, v_prompt, idx_k_prompt, pool_prompt,
            k_sample, v_sample, idx_k_sample, pool_sample)


_drawn_inputs = setup_inputs


def setup_inputs(seed=0):
    import zlib

    import numpy as np

    out = dict(_drawn_inputs(seed))
    spreads = {}
    factors = {'router_group_b': 3.865, 'router_expert_b': 3.827}
    for name, (base, spread) in spreads.items():
        noise = np.random.default_rng([zlib.crc32(name.encode()), seed]).standard_normal(out[name].shape)
        drawn = base * np.exp(spread * noise) if base else spread * noise
        out[name] = __import__('jax').numpy.asarray(drawn.astype(out[name].dtype))
    for name, factor in factors.items():
        out[name] = (out[name] * factor).astype(out[name].dtype)
    return out
```

```python
from contextlib import ExitStack

import numpy as np

import concourse.bass as bass
from concourse import mybir

F32 = mybir.dt.float32
BF16 = mybir.dt.bfloat16
U32 = mybir.dt.uint32
I32 = mybir.dt.int32
ALU = mybir.AluOpType
ACT = mybir.ActivationFunctionType
AX = mybir.AxisListType

P = 128
D = 1024
KC = D // P
SEQ = 1024
NT = SEQ // P
SB, ST = 8, 8
SR = SB * ST
NTOK = SEQ + SR
TILES = NT + 1
PAST, PAGE = 2048, 128
NPG = PAST // PAGE
SLOTS = PAST // P
LS = PAST + ST
HD, NH, NKV = 64, 8, 2
GH = NH // NKV
ROPE = 16
TOPK = 256
NIN = 1864
CU, CQ, CK, CV, CQI, CKI, CWI = 0, 512, 1024, 1152, 1280, 1792, 1856
WINDOWS = (2, 4, 8, 16)
HALO = 15
NG, EPG = 4, 8
NE = NG * EPG
HID = 256
CAP = 128
OVB = 16
NBLK = NE + OVB
EPS = 1e-6
SCALE = HD ** -0.5
BIG = 1e30
ITERS = 26
ZS = 20
ORDER = [NT] + list(range(NT))
SEL_GROUPS = [[2, 3], [4, 5], [6, 7]]

CC = {}
_at = 0
for _n, _w in (("ident", P), ("dmask", P), ("tri", P), ("ones", P), ("cos", TILES * ROPE), ("sin", TILES * ROPE),
               ("pinv", 4 * 16), ("iota", NE), ("tailmask", ST), ("diag", ST), ("tokid", TILES), ("pmod", 1), ("eps", 1), ("z", 1)):
    CC[_n] = (_at, _at + _w)
    _at += _w
NCONST = _at


def constants():
    c = np.zeros((P, NCONST), np.float32)

    def put(name, a):
        lo, hi = CC[name]
        a = np.asarray(a, np.float32)
        c[:a.shape[0], lo:hi] = a.reshape(a.shape[0], -1)

    r = np.arange(P)
    put("ident", np.eye(P))
    put("dmask", np.where(r[None, :] <= r[:, None], 0.0, -BIG))
    put("tri", (r[:, None] < r[None, :]))
    put("ones", np.ones((P, P)))
    half = ROPE // 2
    inv = np.power(np.float32(500000.0), -np.arange(half, dtype=np.float32) / np.float32(half)).astype(np.float32)
    pos = np.zeros((TILES, P), np.float32)
    pos[:NT] = np.arange(SEQ).reshape(NT, P)
    pos[NT, :SR] = PAST + np.arange(SR) % ST
    ang = (pos[:, :, None] * inv).astype(np.float32)
    co, si = np.cos(ang), np.sin(ang)
    put("cos", np.concatenate([co, co], -1).transpose(1, 0, 2))
    put("sin", np.concatenate([-si, si], -1).transpose(1, 0, 2))
    put("pinv", np.tile(np.stack([1.0 / np.minimum(np.arange(16) + 1, w) for w in WINDOWS]).reshape(1, -1), (P, 1)))
    put("iota", np.tile(np.arange(NE)[None], (P, 1)))
    rs = np.arange(SR)
    put("tailmask", np.where(np.arange(ST)[None] <= (rs % ST)[:, None], 0.0, -BIG))
    put("diag", ((rs % ST)[:, None] == np.arange(ST)[None]))
    tok = np.arange(TILES)[None] * P + r[:, None]
    put("tokid", np.minimum(tok, NTOK - 1))
    put("pmod", (r % (P // NPG))[:, None])
    put("eps", np.full((P, 1), EPS))
    s = np.zeros((SR, SB, NH, ST), np.float32)
    for b in range(SB):
        for t in range(ST):
            s[b * ST + t, b, :, t] = 1.0
    return c, s.reshape(SR, SB * SR)


def mask_at(i):
    return P * (i * (i + 1) // 2)


def program(nc, x_prompt, x_sample, cache_k, cache_v, cache_idx_k, state_pool, page_table, norm_mix_g, w_in,
            pool_w, pool_scale, w_out, norm_ffn_g, router_group_w, router_group_b, router_expert_w,
            router_expert_b, expert_w_gate, expert_w_up, expert_w_down, final_norm_g, const_table, head_select,
            y_prompt, y_sample, k_prompt, v_prompt, idx_k_prompt, pool_prompt,
            k_sample, v_sample, idx_k_sample, pool_sample):
    ctx = ExitStack()
    with ctx:
        def sem(name):
            return ctx.enter_context(nc.semaphore(name))

        TOTAL = 53200
        mem = ctx.enter_context(nc.sbuf_tensor("mem", [P, TOTAL], F32))
        ps = ctx.enter_context(nc.psum_tensor("ps", [P, 8, 512], F32))
        at = [0]

        def cut(n, shape=None, dt=F32):
            lo = at[0]
            at[0] += n
            assert at[0] <= TOTAL, at[0]
            v = mem[:, lo:lo + n]
            if dt is not F32:
                v = v.bitcast(dt)
            if shape:
                names = "abcd"[:len(shape)]
                v = v.rearrange(f"p ({' '.join(names)}) -> p {' '.join(names)}", **dict(zip(names, shape)))
            return v

        con = cut(NCONST)
        selb = cut(SB * SR // 2, (SB, SR), BF16)
        stat = cut(256)
        gb = cut(D)
        psc = cut(4)
        early = at[0]
        qT = cut(4 * NTOK, (4, NTOK))
        kiT = cut(NTOK)
        kT = cut(NTOK)
        V = cut(TILES * P, (TILES, P))
        mixP = cut(4 * NTOK, (4, NTOK))
        mask = cut(36 * P // 2, None, BF16)
        SC = cut(33 * P)
        junk = cut(512, None, BF16)
        selG = cut(512, None, BF16)
        selT = cut(512, None, BF16)
        rl = cut(2 * 512, (2, 512))
        W = cut(TILES * 8, (TILES, 8))
        QS = cut(NH * SR, (SB, NH, ST))
        uC = SC[:, 0:4 * SR].rearrange("p (g t) -> p g t", g=4)
        Ztwice = SC[:, 1024:2048].rearrange("p (h a d) -> p h a d", h=NH, a=2)
        WS = cut(SB * SR, (SB, SR))
        QB = cut(SB * SR, (SB, 2, GH, ST))
        persistent = at[0]

        win = cut(KC * NIN, (KC, NIN))
        qiT = cut(2 * 512, (2, 4, P))
        u2 = cut(2 * 4 * (P + HALO), (2, 4, P + HALO))
        uS = cut(4 * SB * (ST + HALO), (4, SB, ST + HALO))
        xb = cut(3 * D, (3, D))
        xnT = cut(2 * D, (2, KC, P))
        Z = cut(ZS * HD, (ZS, HD))
        sumA = cut(736)
        sumB = cut(736)
        dT = cut(4 * P)
        rt1 = cut(19 * ROPE, (19, ROPE))
        rt2 = cut(19 * ROPE, (19, ROPE))
        pw = cut(4 * P, (4, P))
        stt_in = cut(512)

        at[0] = persistent
        rt = cut(1400)
        rw = cut(KC * 36, (KC, 36))
        wout = cut(8 * D, (8, D))
        SCs = cut(LS)
        sG = cut(LS // 2, None, BF16)
        sT = cut(LS // 2, None, BF16)
        sJ = cut(LS // 2, None, BF16)
        smask = cut(LS // 2, None, BF16)
        region = at[0]
        kin = cut(2 * 1024, (2, SLOTS, HD))
        kiTs = cut(2 * 1024, (2, 8, P))
        rs = cut(2 * LS, (2, LS))
        zslots = cut(NBLK * 16, None, I32)
        at[0] = region
        Sm = cut(2 * 1024, (2, 1024))
        PT = cut(2 * 1024, (2, 8, P))
        hb = cut(2 * D, (2, D))
        x2 = cut(2 * D, (2, D))
        x2T = cut(D, (KC, P))
        Osb = cut(512)
        mixA = cut(512, (4, P))
        at[0] = region
        mixS = cut(4 * SR, (4, SR))
        KTs = cut(LS)
        Ps = cut(LS)
        PTs = cut((SLOTS + 1) * SR, (SLOTS + 1, SR))
        Kin = [cut(2048, (SLOTS, P))]
        Vin = [cut(2048, (SLOTS, P))]
        Kin.append(SC[:, 0:2048].rearrange("p (s d) -> p s d", d=P))
        Vin.append(SC[:, 2048:4096].rearrange("p (s d) -> p s d", d=P))
        Vnew = rl[:, :, :].rearrange("p a n -> p (a n)")[0:ST, :].rearrange("t (b n) -> t b n", b=SB)
        assert at[0] <= TOTAL

        at[0] = early
        wgu = cut(2 * KC * 512, (2, KC, 512))
        wdn = cut(2 * 2 * D, (2, 2, D))
        xg = cut(2 * D, (2, D))
        xgT = cut(2 * D, (2, KC, P))
        sg = cut(2 * HID, (2, HID))
        hid = cut(HID)
        hT = cut(HID, (2, P))
        ob = cut(2 * D, (2, D))
        assert at[0] <= persistent
        at[0] = early
        o1 = cut(2 * D, (2, D))
        o2 = cut(2 * D, (2, D))
        hc = cut(2 * D, (2, D))
        yc = cut(2 * D, (2, D))
        sq = cut(D)
        def const(name, rows=P):
            lo, hi = CC[name]
            return con[0:rows, lo:hi]

        def ident(n):
            return con[0:n, CC["ident"][0]:CC["ident"][0] + n]

        def cs(name, i, rows):
            lo = CC[name][0] + i * ROPE
            return con[0:rows, lo:lo + ROPE]

        def rows(i):
            return SR if i == NT else P

        ssq, std, rstd = stat[:, 0:9], stat[:, 9:18], stat[:, 18:27]
        lo_, hi_, mid_, cnt_, t1_, t2_ = (stat[:, 30 + 4 * j:34 + 4 * j] for j in range(6))
        need_ = stat[:, 54:58]
        mx, nb = stat[:, 60:68], stat[:, 68:76]
        esum, einv = stat[:, 76:92], stat[:, 92:108]
        ssq2, std2, rstd2 = stat[:, 108:117], stat[:, 117:126], stat[:, 126:135]
        wsc = stat[0:SR, 135:143]
        pt_i = stat[:, 143:151].bitcast(I32)
        pidx = stat[:, 151:159].bitcast(U32)
        smx, snb, sesum, seinv = (stat[0:SR, 160 + 8 * j:168 + 8 * j] for j in range(4))
        ssq3, std3, rstd3 = stat[:, 192:201], stat[:, 201:210], stat[:, 210:219]

        rt_at = [0]

        def rcut(n, dt=F32):
            rt_at[0] += n
            v = rt[:, rt_at[0] - n:rt_at[0]]
            return v if dt is F32 else v.bitcast(dt)

        bias36 = rcut(36)
        L = rcut(36)
        G8 = rcut(8)
        gm8, gi8 = rcut(8), rcut(8, U32)
        E32 = rcut(NE)
        em8, ei8 = rcut(8), rcut(8, U32)
        r1 = rcut(8)
        gexp = rcut(4)
        oh4 = rcut(4)
        OH = rcut(2 * NE).rearrange("p (k e) -> p k e", k=2)
        A = rcut(NE)
        ASUM = rcut(NE)
        rkt = rcut(NE)
        RK = rcut(2 * TILES).rearrange("p (i k) -> p i k", k=2)
        EF = rcut(2 * TILES).rearrange("p (i k) -> p i k", k=2)
        CW = rcut(2 * TILES).rearrange("p (i k) -> p i k", k=2)
        dest = rcut(2 * TILES, U32).rearrange("p (i k) -> p i k", k=2)
        cntE, ovE, ovS, ovX, ovT = (rcut(NE) for _ in range(5))
        OS, DB, DF = (rcut(2 * TILES) for _ in range(3))
        toki = rcut(16 * TILES, I32).rearrange("p (i k) -> p i k", k=16)
        ovb = rcut(OVB + 1, I32)
        ovf = rcut(OVB + 1)
        slot_tok = rcut(NBLK, U32)
        assert rt_at[0] <= 1400

        def scv(i):
            lo = mask_at(i) - mask_at(2)
            return SC[:, lo:lo + P * (i + 1)]

        def maskv(i):
            return mask[:, mask_at(i):mask_at(i) + P * (i + 1)]

        def bank(b, r=P, n=512):
            return ps[0:r, b, 0:n]

        def rowsof(ap, i):
            return ap[0][i * P:(i + 1) * P] if i < NT else ap[1]

        x_rows = (x_prompt[0], x_sample.rearrange("b t d -> (b t) d"))
        k_rows = (k_prompt[0, 0].rearrange("t g d -> t (g d)"), k_sample[0].rearrange("b t g d -> (b t) (g d)"))
        v_rows = (v_prompt[0, 0].rearrange("t g d -> t (g d)"), v_sample[0].rearrange("b t g d -> (b t) (g d)"))
        ik_rows = (idx_k_prompt[0, 0], idx_k_sample[0].rearrange("b t d -> (b t) d"))
        y_rows = (y_prompt[0], y_sample.rearrange("b t d -> (b t) d"))
        h_dram = nc.dram_tensor("h_rows", (NTOK, D), F32, kind="Internal").ap()
        xn_dram = nc.dram_tensor("xn_rows", (NTOK, D), F32, kind="Internal").ap()
        w_dram = nc.dram_tensor("index_weights", (SR, NH), F32, kind="Internal").ap()
        slot_dram = nc.dram_tensor("slot_tokens", (NBLK * P, 16), I32, kind="Internal").ap()
        eo_dram = nc.dram_tensor("expert_rows", (NBLK * P, D), F32, kind="Internal").ap()
        w_in_k = w_in[0].rearrange("(p c) n -> p c n", c=KC)
        gate_k = expert_w_gate[0].rearrange("e (p c) n -> e p c n", c=KC)
        up_k = expert_w_up[0].rearrange("e (p c) n -> e p c n", c=KC)
        down_k = expert_w_down[0].rearrange("e (p c) n -> e p c n", c=2)
        SPP = PAGE // SLOTS
        ci_rows = cache_idx_k[0].rearrange("n (c s) d -> (n c) (s d)", c=SPP)
        ck_rows = cache_k[0].rearrange("n (c s) g d -> (n c) (s g d)", c=SPP)
        cv_rows = cache_v[0].rearrange("n (c s) g d -> (n c) (s g d)", c=SPP)

        PART = {"T0": 0, "T1": 1, "U": 2, "Q": 3, "QI": 4, "KV": 5, "S0": 6, "S1": 7}
        order = [("T0", "state"), ("T0", ("x", 0)), ("T1", ("x", 0))]
        score_steps = {}
        m = 0
        for n in range(TILES + 1):
            if n < TILES:
                order += [(q, n) for q in ("U", "Q", "KV", "QI")]
            if n + 1 < TILES:
                order += [("T0", ("x", n + 1)), ("T1", ("x", n + 1))]
            if n:
                order += [("T0", ("q", n - 1)), ("T1", ("qi", n - 1)), ("T0", ("k", n - 1)), ("T1", ("pool", n - 1))]
                if n - 1 in (0, TILES - 1):
                    order += [("T0", ("u", n - 1))]
                i = ORDER[n - 1]
                score_steps[n - 1] = []
                if 2 <= i < NT:
                    for lo in range(0, P * (i + 1), 512):
                        for h in range(NH):
                            score_steps[n - 1].append((m, lo, min(512, P * (i + 1) - lo), h))
                            order += [(f"S{m % 2}", ("s", m))]
                            m += 1
        n_scores = m
        P2A = {"ACC": 0, "TR": 5, "PS0": 6, "PS1": 7}
        orderA = [("TR", (0, 0)), ("TR", (0, 1))]
        for b in range(SB):
            orderA += [(f"PS{(5 * b + q) % 2}", (b, q)) for q in range(5)]
            if b + 1 < SB:
                orderA += [("TR", (b + 1, 0)), ("TR", (b + 1, 1))]
        orderA += [("ACC", 0)]
        P2B = {"A0": 0, "A1": 2, "PT0": 4, "PT1": 5, "O": 6, "M": 7}

        def tail_tasks(i):
            return ([("OT", i)] if i < NT else []) + [("OP", i, 0), ("OP", i, 1), ("XR", i, 0), ("XR", i, 1), ("LG", i), ("RK", i)]

        tasks = []
        for i in range(NT):
            rest = tail_tasks(i - 1) if i else []
            tasks.append(("S", i, 0))
            for h in range(NH):
                if h + 1 < NH:
                    tasks.append(("S", i, h + 1))
                if h >= 1 and rest:
                    tasks.append(rest.pop(0))
                tasks += [("T", i, h), ("V", i, h)]
            assert not rest
        tasks += tail_tasks(NT - 1)
        orderB = []
        npt = 0
        pt_use = {}
        for t in tasks + tail_tasks(NT):
            if t[0] == "S":
                orderB.append((f"A{t[2] % 2}", t))
            elif t[0] == "T":
                for c in range(0, t[1] + 1, 4):
                    pt_use[t + (c,)] = npt % 2
                    orderB.append((f"PT{npt % 2}", t + (c,)))
                    npt += 1
            elif t[0] == "V":
                if t[2] == 0:
                    orderB.append(("O", ("V", t[1])))
            else:
                orderB.append(("M", t))
        orderB.append(("M", "count"))
        P2C = {"SS": 0, "TK0": 5, "TK1": 6, "PV": 7}
        orderC = []
        ntk = 0
        tk_use = {}

        def tk(key):
            nonlocal ntk
            tk_use[key] = ntk % 2
            orderC.append((f"TK{ntk % 2}", key))
            ntk += 1

        for b in range(SB):
            for c in range(4):
                tk(("k", b, c))
            orderC.append(("SS", b))
            for c in range(3):
                tk(("p", b, c))
            orderC.append(("PV", b))

        filled, emptied, use = {}, {}, {}
        for tag, parts, seq in (("1", PART, order), ("2a", P2A, orderA), ("2b", P2B, orderB), ("2c", P2C, orderC)):
            for q in parts:
                filled[tag + q], emptied[tag + q] = sem(f"filled_{tag}_{q}"), sem(f"emptied_{tag}_{q}")
            seen = {}
            for q, key in seq:
                use[tag, q, key] = seen.get(q, 0)
                seen[q] = seen.get(q, 0) + 1
            use[tag] = seen

        def claim(pe, tag, q, key):
            if use[tag, q, key]:
                pe.wait_ge(emptied[tag + q], use[tag, q, key])

        def settle(pe, tag):
            for q, n in use[tag].items():
                pe.wait_ge(emptied[tag + q], n)

        def take(eng, tag, q, key):
            eng.wait_ge(filled[tag + q], use[tag, q, key] + 1)

        def copied(eng, tag, q, key):
            eng.wait_ge(emptied[tag + q], use[tag, q, key] + 1)

        consts_in = sem("consts_in")
        small_in = sem("small_in")
        w_in_in = [sem(f"w_in_in{c}") for c in range(4)]
        x_in = [sem(f"x_in{s}") for s in range(3)]
        state_in = sem("state_in")
        act_step, dve_step, pool_step = sem("act_step"), sem("dve_step"), sem("pool_step")
        init_done = sem("init_done")
        ssq_ready, std_ready, rstd_ready, xs_ready, xn_ready = sem("ssq_ready"), sem("std_ready"), sem("rstd_ready"), sem("xs_ready"), sem("xn_ready")
        z_ready, kv_out, d_ready, u_out, score_added = sem("z_ready"), sem("kv_out"), sem("d_ready"), sem("u_out"), sem("score_added")
        head_select_in = sem("head_select_in")
        phase1 = sem("phase1_done")
        state_out = sem("state_out")
        wscr_out, wsc_in, pt_in = sem("index_weights_out"), sem("index_weights_in"), sem("page_table_in")
        pidx_ready, WS_ready, QB_ready = sem("page_rows_ready"), sem("WS_ready"), sem("QB_ready")
        ki_in = [sem(f"ki_in{s}") for s in range(2)]
        sec_done, smask_ready = sem("weighted_done"), sem("smask_ready")
        phase2a = sem("phase2a_done")
        wout_in, rw_in, gb_in = sem("wout_in"), sem("router_in"), sem("ffn_norm_in")
        s_masked, s_exp, av_done = sem("scores_masked"), sem("probs_ready"), sem("values_summed")
        xr_in, h_out, x2_out = ([sem(f"{n}{s}") for s in range(2)] for n in ("residual_in", "h_out", "x2_out"))
        ssq2_ready, std2_ready, x2_ready, A_ready, ASUM_ready = (
            sem("ssq2_ready"), sem("std2_ready"), sem("x2_ready"), sem("A_ready"), sem("ASUM_ready"))
        logits_split, gexp_ready = sem("logits_split"), sem("gexp_ready")
        prompts_done = sem("prompt_tiles_done")
        KV_in = [sem(f"KV_in{s}") for s in range(2)]
        Vnew_in = sem("Vnew_in")
        smax_ready, snorm_ready = sem("smax_ready"), sem("snorm_ready")
        toki_ready, slots_cleared, dest_ready, slots_out, slots_in = (
            sem("toki_ready"), sem("slots_cleared"), sem("dest_ready"), sem("slots_out"), sem("slots_in"))
        phase2 = sem("phase2_done")
        wgu_in, wdn_in, xg_in, eo_out = ([sem(f"{n}{s}") for s in range(2)] for n in ("wgu_in", "wdn_in", "xg_in", "eo_out"))
        xT_filled, xT_emptied = [sem(f"xT_filled{c}") for c in range(2)], [sem(f"xT_emptied{c}") for c in range(2)]
        gu_filled, hid_ready = sem("gate_up_filled"), sem("hidden_ready")
        silu_ready, hT_filled, hT_ready = sem("silu_ready"), sem("hT_filled"), sem("hT_ready")
        dn_filled, dn_emptied = [sem(f"down_filled{c}") for c in range(2)], [sem(f"down_emptied{c}") for c in range(2)]
        ov_w, ov_x, ov_pe, ov_act, ov_dve, ov_out = (sem(f"overflow_{n}") for n in ("weights_in", "rows_in", "pe", "act", "dve", "out"))
        experts_done = sem("experts_done")
        o_in, hc_in, y_ready, y_out = ([sem(f"{n}{s}") for s in range(2)] for n in ("o_in", "hc_in", "y_ready", "y_out"))
        ysum_ready, ssq3_ready, std3_ready = sem("ysum_ready"), sem("ssq3_ready"), sem("std3_ready")
        fin_norm_in = sem("fin_norm_in")

        block = ctx.enter_context(nc.Block())

        def tiles_out(eng, sems, n):
            for s in range(2):
                eng.wait_ge(sems[s], 16 * ((n + 1 - s) // 2))

        def rowsof_dram(ap, i):
            return ap[i * P:i * P + rows(i)]

        def dyn(ap, e):
            return ap[e] if isinstance(e, int) else ap[bass.ds(e, 1)].rearrange("a p c n -> (a p) c n")

        def block_rows(e):
            v = eo_dram.rearrange("(b p) n -> b p n", p=P)
            return v[e] if isinstance(e, int) else v[bass.ds(e, 1)].rearrange("a p n -> (a p) n")

        def store_y(eng, i):
            r, s = rows(i), i % 2
            eng.wait_ge(y_ready[s], i // 2 + 1)
            eng.dma_start(rowsof(y_rows, i), yc[0:r, s, :]).then_inc(y_out[s], 16)

        @block.sync
        def _(sp):
            sp.dma_start(con[:, :], const_table).then_inc(consts_in, 16)
            sp.dma_start(gb[:, :], norm_mix_g[0:1, :].partition_broadcast(P)).then_inc(consts_in, 16)
            sp.dma_start(sumA[0:SR, 0:SB * SR], head_select).then_inc(head_select_in, 16)
            sp.dma_start(stt_in[0:SB * HALO, :], state_pool[0].rearrange("b t c -> (b t) c")).then_inc(state_in, 16)
            for n in range(2):
                r = rows(ORDER[n])
                sp.dma_start(xb[0:r, n % 3, :], rowsof(x_rows, ORDER[n])).then_inc(x_in[n % 3], 16)
            for c in range(4):
                sp.dma_start(win[:, 2 * c:2 * c + 2, :], w_in_k[:, 2 * c:2 * c + 2, :]).then_inc(w_in_in[c], 16)
            sp.dma_start(pw[:, :, :], pool_w[0].rearrange("g c n -> c g n")).then_inc(small_in, 16)
            sp.dma_start(psc[:, :], pool_scale[0].rearrange("(g c) -> c g", g=4),
                         allow_slow_non_contiguous=True).then_inc(small_in, 16)
            for c in range(SPP):
                sp.dma_start(pt_i[c:P:SPP, :], page_table.rearrange("b j -> j b"),
                             allow_slow_non_contiguous=True).then_inc(pt_in, 16)
            sp.dma_start(pool_sample[0, :, 0:HALO - ST, :], state_pool[0, :, ST:HALO, :]).then_inc(state_out, 16)
            for n in range(2, TILES):
                if n >= 3:
                    take(sp, "1", "T1", ("x", n - 3))
                r = rows(ORDER[n])
                sp.dma_start(xb[0:r, n % 3, :], rowsof(x_rows, ORDER[n])).then_inc(x_in[n % 3], 16)
                if n == 2:
                    copied(sp, "1", "KV", 0)
                    sp.dma_start(w_dram, W[0:SR, NT, :]).then_inc(wscr_out, 16)
                    sp.wait_ge(wscr_out, 16)
                    for h in range(NH):
                        sp.dma_start(wsc[h * ST:(h + 1) * ST, :], w_dram.rearrange("(b t) h -> h t b", t=ST)[h],
                                     allow_slow_non_contiguous=True).then_inc(wsc_in, 16)
            sp.wait_ge(phase1, 4)
            sp.dma_start(wout[:, 0:4, :], w_out[0, 0:512, :].rearrange("(g c) n -> c g n", c=P)).then_inc(wout_in, 16)
            for g in range(NKV):
                src = w_out[0, 512 + 256 * g:512 + 256 * g + 256, :].rearrange("(h d) n -> d h n", d=HD)
                sp.dma_start(wout[HD * g:HD * g + HD, 4:8, :], src).then_inc(wout_in, 16)
            sp.dma_start(rw[:, :, 0:NG], router_group_w[0].rearrange("(c p) n -> p c n", p=P)).then_inc(rw_in, 16)
            sp.dma_start(rw[:, :, NG:36], router_expert_w[0].rearrange("(c p) n -> p c n", p=P)).then_inc(rw_in, 16)
            sp.dma_start(bias36[:, 0:NG], router_group_b[0:1, :].partition_broadcast(P)).then_inc(rw_in, 16)
            sp.dma_start(bias36[:, NG:36], router_expert_b[0:1, :].partition_broadcast(P)).then_inc(rw_in, 16)
            sp.dma_start(gb[:, :], norm_ffn_g[0:1, :].partition_broadcast(P)).then_inc(gb_in, 16)
            sp.wait_ge(phase2a, 3)

            def tail(i):
                s, r = i % 2, rows(i)
                copied(sp, "2b", "M", ("OP", i, 1))
                sp.dma_start(rowsof_dram(h_dram, i), hb[0:r, s, :]).then_inc(h_out[s], 16)
                sp.wait_ge(x2_ready, i + 1)
                sp.dma_start(rowsof_dram(xn_dram, i), x2[0:r, s, :]).then_inc(x2_out[s], 16)

            def residual(i):
                s, r = i % 2, rows(i)
                if 2 <= i:
                    sp.wait_ge(h_out[s], 16 * (i // 2))
                    sp.wait_ge(x2_ready, i - 1)
                sp.dma_start(hb[0:r, s, :], rowsof(x_rows, i)).then_inc(xr_in[s], 16)

            residual(0)
            residual(1)
            for i in range(NT):
                tail(i)
                if i + 2 < NT:
                    residual(i + 2)
            sp.wait_ge(kv_out, 48 * TILES)
            sp.dma_start(Vnew, v_sample[0].rearrange("b t g d -> t b (g d)")).then_inc(Vnew_in, 16)
            copied(sp, "2c", "PV", SB - 1)
            residual(NT)
            tail(NT)
            sp.wait_ge(phase2, 4)

            def weights(e, q, s):
                sp.dma_start(wgu[:, s, :, 0:HID], dyn(gate_k, e)).then_inc(wgu_in[s], 16)
                sp.dma_start(wgu[:, s, :, HID:2 * HID], dyn(up_k, e)).then_inc(wgu_in[s], 16)
                sp.dma_start(wdn[:, s, :, :], dyn(down_k, e)).then_inc(wdn_in[s], 16)

            weights(0, 0, 0)
            weights(1, 0, 1)
            with sp.Fori(1, NE // 2) as q:
                for s in range(2):
                    sp.wait_ge(dn_filled[1], q * 2 + (s - 1))
                    weights(q * 2 + s, q, s)
            sp.wait_ge(dn_filled[1], NE)
            sp.wait_ge(slots_in, 16)
            some = sp.value_load(ovb[0:1, OVB:OVB + 1], min_val=0, max_val=OVB)
            with sp.If(some > 0):
                with sp.Fori(0, OVB) as j:
                    sp.wait_ge(ov_pe, j * 4 + 4)
                    e = sp.value_load(ovb[0:1, bass.ds(j, 1)], min_val=0, max_val=NE - 1)
                    sp.dma_start(wgu[:, 0, :, 0:HID], dyn(gate_k, e)).then_inc(ov_w, 16)
                    sp.dma_start(wgu[:, 0, :, HID:2 * HID], dyn(up_k, e)).then_inc(ov_w, 16)
                    sp.dma_start(wdn[:, 0, :, :], dyn(down_k, e)).then_inc(ov_w, 16)
                sp.nop()
            with sp.Else():
                sp.nop()
            sp.wait_ge(experts_done, 4)
            tiles_out(sp, h_out, TILES)
            sp.dma_start(gb[:, :], final_norm_g.rearrange("(a n) -> a n", a=1).partition_broadcast(P)).then_inc(fin_norm_in, 16)
            for i in range(TILES):
                s, r = i % 2, rows(i)
                if i >= 2:
                    sp.wait_ge(ysum_ready, 2 * (i - 1))
                sp.dma_start(hc[0:r, s, :], rowsof_dram(h_dram, i)).then_inc(hc_in[s], 16)
                if i >= 1:
                    store_y(sp, i - 1)
            store_y(sp, TILES - 1)
            for s in range(2):
                sp.wait_ge(y_out[s], 16 * ((TILES + 1 - s) // 2))
            sp.wait_ge(state_out, 16)
            sp.wait_ge(u_out, 16 * (SB + 1))

        @block.gpsimd
        def _(pool):
            steps = [0]

            def link(ins):
                steps[0] += 1
                ins.then_inc(pool_step, 1)
                pool.wait_ge(pool_step, steps[0])

            pool.memset(u2[:, 0, :, 0:HALO], 0.0).then_inc(init_done, 1)
            pool.memset(WS[:, :, :], 0.0).then_inc(init_done, 1)
            pool.memset(QB[:, :, :, :, :], 0.0).then_inc(init_done, 1)
            pool.memset(mask[:, 0:3 * P], 0.0).then_inc(init_done, 1)
            pool.wait_ge(consts_in, 32)
            pool.wait_ge(init_done, 4)
            pool.wait_ge(head_select_in, 16)
            link(pool.tensor_copy(selb[0:SR].rearrange("p b r -> p (b r)"), sumA[0:SR, 0:SB * SR]))
            pool.tensor_copy(mask[:, 0:P], const("dmask")).then_inc(init_done, 1)
            pool.tensor_copy(mask[:, 2 * P:3 * P], const("dmask")).then_inc(init_done, 1)

            def norm_weight(n):
                r = rows(ORDER[n])
                pool.wait_ge(xs_ready, n + 1)
                pool.tensor_tensor(xb[0:r, n % 3, :], xb[0:r, n % 3, :], gb[0:r, :], ALU.mult).then_inc(xn_ready, 1)

            def rope(n):
                i = ORDER[n]
                r = rows(i)
                copied(pool, "1", "QI", n)
                z = Z[0:r, 0:19, :]
                c = cs("cos", i, r).unsqueeze(1).broadcast_to([r, 19, ROPE])
                s = cs("sin", i, r).unsqueeze(1).broadcast_to([r, 19, ROPE])
                hf = ROPE // 2
                link(pool.tensor_tensor(rt1[0:r], z[:, :, 0:ROPE], c, ALU.mult))
                link(pool.tensor_tensor(rt2[0:r, :, 0:hf], z[:, :, hf:ROPE], s[:, :, 0:hf], ALU.mult))
                link(pool.tensor_tensor(rt2[0:r, :, hf:ROPE], z[:, :, 0:hf], s[:, :, hf:ROPE], ALU.mult))
                link(pool.tensor_tensor(z[:, :, 0:ROPE], rt1[0:r], rt2[0:r], ALU.add))
                if i == NT:
                    link(pool.tensor_copy(Ztwice[0:r, :, 0, :], Z[0:r, 10:18, :]))
                    link(pool.tensor_copy(Ztwice[0:r, :, 1, :], Z[0:r, 10:18, :]))
                pool.tensor_copy(Z[0:r, 19, :], Z[0:r, 18, :]).then_inc(z_ready, 1)
                pool.dma_start(rowsof(k_rows, i), Z[0:r, 8:10, :].rearrange("p a d -> p (a d)")).then_inc(kv_out, 16)
                pool.dma_start(rowsof(ik_rows, i), Z[0:r, 18, :]).then_inc(kv_out, 16)
                pool.dma_start(rowsof(v_rows, i), V[0:r, i, :]).then_inc(kv_out, 16)

            def pooling(n):
                i = ORDER[n]
                copied(pool, "1", "U", n)
                if i == NT:
                    T = ST + HALO
                    u = uS
                    sa = sumA[:, :].rearrange("p (g b t) -> p g b t", g=4, b=SB)
                    sb_ = sumB[:, :].rearrange("p (g b t) -> p g b t", g=4, b=SB)
                    d = dT[:, 0:4 * SR].rearrange("p (g b t) -> p g b t", g=4, b=SB)
                else:
                    T = P + HALO
                    u = u2[:, i % 2]
                    sa = sumA[:, 0:4 * T].rearrange("p (g t) -> p g t", g=4)
                    sb_ = sumB[:, 0:4 * T].rearrange("p (g t) -> p g t", g=4)
                    d = dT[:, 0:4 * P].rearrange("p (g t) -> p g t", g=4)

                def cutv(v, g, a, b):
                    return v[:, g, :, a:b] if i == NT else v[:, g, a:b]

                g4 = slice(0, 4)
                link(pool.tensor_tensor(cutv(sa, g4, 1, T), cutv(u, g4, 1, T), cutv(u, g4, 0, T - 1), ALU.add))
                g3 = slice(1, 4)
                link(pool.tensor_tensor(cutv(sb_, g3, 3, T), cutv(sa, g3, 3, T), cutv(sa, g3, 1, T - 2), ALU.add))
                g2 = slice(2, 4)
                link(pool.tensor_tensor(cutv(sa, g2, 7, T), cutv(sb_, g2, 7, T), cutv(sb_, g2, 3, T - 4), ALU.add))
                link(pool.tensor_tensor(cutv(sb_, 3, 15, T), cutv(sa, 3, 15, T), cutv(sa, 3, 7, T - 8), ALU.add))
                if n:
                    take(pool, "1", "T1", ("pool", n - 1))
                for g, w in enumerate(WINDOWS):
                    src = (sa, sb_, sa, sb_)[g]
                    if i == NT:
                        link(pool.tensor_scalar(d[:, g], cutv(src, g, HALO, T), 1.0 / w, None, ALU.mult))
                    elif i:
                        link(pool.tensor_scalar(d[:, g, :], src[:, g, HALO:T], 1.0 / w, None, ALU.mult))
                    else:
                        lo = CC["pinv"][0] + 16 * g
                        pool.tensor_tensor(d[:, g, 0:16], src[:, g, HALO:HALO + 16], con[:, lo:lo + 16], ALU.mult)
                        link(pool.tensor_scalar(d[:, g, 16:P], src[:, g, HALO + 16:T], 1.0 / w, None, ALU.mult))
                pool.tensor_tensor(d, d, cutv(u, g4, HALO, T), ALU.subtract).then_inc(d_ready, 1)

            norm_weight(0)
            norm_weight(1)
            for n in range(TILES):
                rope(n)
                pooling(n)
                if n + 2 < TILES:
                    norm_weight(n + 2)
                if n == 0:
                    pool.wait_ge(pt_in, 16 * SPP)
                    pool.tensor_scalar(pidx, pt_i, float(SPP), const("pmod")[:, 0:1], ALU.mult, ALU.add).then_inc(pidx_ready, 1)
            pool.wait_ge(wsc_in, 16 * NH)
            for b in range(SB):
                link(pool.tensor_scalar(WS[0:SR, b, b * ST:(b + 1) * ST], const("diag", SR), wsc[:, b:b + 1], None, ALU.mult))
            for g in range(NKV):
                q0 = qT[HD * g:HD * (g + 1), :, SEQ:NTOK].rearrange("p h (b t) -> p b h t", b=SB)
                link(pool.tensor_copy(QB[HD * g:HD * (g + 1), :, g, :, :], q0))
            pool.wait_ge(kv_out, 48 * TILES)
            pool.drain().then_inc(phase1, 1)

            pool.wait_ge(phase1, 4)
            pool.wait_ge(pidx_ready, 1)
            zero = zslots
            link(pool.memset(zero, 0))
            pool.dma_start(slot_dram.rearrange("(p c) k -> p (c k)", p=P), zero).then_inc(slots_cleared, 16)
            per = OVB * D // 512
            pool.dma_start(eo_dram[NE * P:NBLK * P, :].rearrange("(p c) n -> p (c n)", p=P).rearrange("p (c n) -> p c n", c=per),
                           zslots.bitcast(F32)[:, 0:512].unsqueeze(1).broadcast_to([P, per, 512])).then_inc(slots_cleared, 16)
            for b in range(SB):
                s = b % 2
                if b >= 2:
                    take(pool, "2a", "TR", (b - 2, 1))
                pool.indirect_dma_start(kin[:, s].rearrange("p s d -> p (s d)"), None, ci_rows,
                                        bass.IndirectOffsetOnAxis(ap=pidx[:, b:b + 1], axis=0)).then_inc(ki_in[s], 16)
            pool.iota(toki[:, :, :], pattern=[[P, TILES], [0, 16]], base=0, channel_multiplier=1).then_inc(toki_ready, 1)
            pool.wait_ge(slots_cleared, 32)
            for s in range(2):
                pool.wait_ge(ki_in[s], 16 * SB // 2)
            pool.drain().then_inc(phase2a, 1)
            pool.wait_ge(prompts_done, 3)
            tiles_out(pool, h_out, NT)
            tiles_out(pool, x2_out, NT)
            for b in range(SB):
                s = b % 2
                if b >= 2:
                    take(pool, "2c", "PV", b - 2)
                for buf, src in ((Kin[s], ck_rows), (Vin[s], cv_rows)):
                    pool.indirect_dma_start(buf.rearrange("p s d -> p (s d)"), None, src,
                                            bass.IndirectOffsetOnAxis(ap=pidx[:, b:b + 1], axis=0)).then_inc(KV_in[s], 16)
            pool.wait_ge(dest_ready, 1)
            for i in range(TILES):
                r = rows(i)
                for k in range(2):
                    pool.indirect_dma_start(slot_dram, bass.IndirectOffsetOnAxis(ap=dest[0:r, i, k:k + 1], axis=0),
                                            toki[0:r, i, :], None).then_inc(slots_out, 16)
            pool.wait_ge(slots_out, 16 * 2 * TILES)
            pool.dma_start(slot_tok.bitcast(I32), slot_dram[:, 0:1].rearrange("(c p) k -> p (c k)", p=P),
                           allow_slow_non_contiguous=True).then_inc(slots_in, 16)
            pool.wait_ge(slots_in, 16)
            tiles_out(pool, x2_out, TILES)
            pool.drain().then_inc(phase2, 1)
            pool.wait_ge(phase2, 4)

            for e in range(NE):
                s = e % 2
                if e >= 2:
                    pool.wait_ge(xT_filled[1], e - 1)
                pool.indirect_dma_start(xg[:, s, :], None, xn_dram,
                                        bass.IndirectOffsetOnAxis(ap=slot_tok[:, e:e + 1], axis=0)).then_inc(xg_in[s], 16)
            pool.wait_ge(dn_filled[1], NE)
            some = pool.value_load(ovb[0:1, OVB:OVB + 1], min_val=0, max_val=OVB)
            with pool.If(some > 0):
                for j in range(OVB):
                    if j:
                        pool.wait_ge(ov_pe, 4 * j + 4)
                    pool.indirect_dma_start(xg[:, 0, :], None, xn_dram,
                                            bass.IndirectOffsetOnAxis(ap=slot_tok[:, NE + j:NE + j + 1], axis=0)).then_inc(ov_x, 16)
                pool.nop()
            with pool.Else():
                pool.nop()
            pool.drain().then_inc(experts_done, 1)
            pool.wait_ge(experts_done, 4)
            for i in range(TILES):
                s, r = i % 2, rows(i)
                if i >= 2:
                    pool.wait_ge(ysum_ready, 2 * (i - 1))
                for k, o in ((0, o1), (1, o2)):
                    pool.indirect_dma_start(o[0:r, s, :], None, eo_dram,
                                            bass.IndirectOffsetOnAxis(ap=dest[0:r, i, k:k + 1], axis=0)).then_inc(o_in[s], 16)

        @block.tensor
        def _(pe):
            mm = nc.tensor.matmul
            tr = nc.tensor.transpose

            def x_turn(n):
                r = rows(ORDER[n])
                pe.wait_ge(xn_ready, n + 1)
                for c in range(2):
                    claim(pe, "1", f"T{c}", ("x", n))
                    for j in range(4):
                        ins = tr(ps[:, c, j * P:j * P + r], xb[0:r, n % 3, 4 * c + j:D:KC], ident(r))
                    ins.then_inc(filled[f"1T{c}"], 1)

            def project(n):
                i = ORDER[n]
                r = rows(i)
                s = n % 2
                for c in range(2):
                    copied(pe, "1", f"T{c}", ("x", n))
                claim(pe, "1", "U", n)
                for g in range(4):
                    for k in range(KC):
                        if n == 0 and g == 0 and k % 2 == 0:
                            pe.wait_ge(w_in_in[k // 2], 16)
                        ins = mm(ps[:, PART["U"], g * r:(g + 1) * r], win[:, k, g * P:(g + 1) * P], xnT[:, s, k, 0:r],
                                 start=(k == 0), stop=(k == KC - 1))
                ins.then_inc(filled["1U"], 1)
                for part, spans in (("Q", ((CQ, CK, 0),)), ("KV", ((CK, CQI, 0), (CKI, NIN, CQI - CK))), ("QI", ((CQI, CKI, 0),))):
                    claim(pe, "1", part, n)
                    for a, b, o in spans:
                        for k in range(KC):
                            ins = mm(ps[0:r, PART[part], o:o + b - a], xnT[:, s, k, 0:r], win[:, k, a:b],
                                     start=(k == 0), stop=(k == KC - 1))
                    ins.then_inc(filled["1" + part], 1)

            def z_turn(n):
                i = ORDER[n]
                r = rows(i)
                pe.wait_ge(z_ready, n + 1)
                claim(pe, "1", "T0", ("q", n))
                for c in range(4):
                    ins = tr(ps[:, 0, c * r:(c + 1) * r], Z[0:r, 2 * c:2 * c + 2, :].rearrange("p a d -> p (a d)"), ident(r))
                ins.then_inc(filled["1T0"], 1)
                claim(pe, "1", "T1", ("qi", n))
                if i == NT:
                    for h in range(NH):
                        ins = tr(ps[:, 1, h * r:(h + 1) * r], Ztwice[0:r, h].rearrange("p a d -> p (a d)"), ident(r))
                else:
                    for c in range(4):
                        ins = tr(ps[:, 1, c * r:(c + 1) * r], Z[0:r, 10 + 2 * c:12 + 2 * c, :].rearrange("p a d -> p (a d)"), ident(r))
                ins.then_inc(filled["1T1"], 1)
                claim(pe, "1", "T0", ("k", n))
                for c, z0 in ((0, 8), (1, 18)):
                    ins = tr(ps[:, 0, c * r:(c + 1) * r], Z[0:r, z0:z0 + 2, :].rearrange("p a d -> p (a d)"), ident(r))
                ins.then_inc(filled["1T0"], 1)

            def pool_out(n):
                r = rows(ORDER[n])
                if n == 0:
                    pe.wait_ge(small_in, 32)
                pe.wait_ge(d_ready, n + 1)
                claim(pe, "1", "T1", ("pool", n))
                for g in range(4):
                    ins = mm(ps[:, 1, g * r:(g + 1) * r], pw[:, g, :], dT[:, g * r:(g + 1) * r], start=True, stop=True)
                ins.then_inc(filled["1T1"], 1)

            def u_turn(n):
                claim(pe, "1", "T0", ("u", n))
                for g in range(4):
                    if ORDER[n] == NT:
                        ins = tr(ps[0:SR, 0, g * P:(g + 1) * P], uC[:, g, :], ident(P))
                    else:
                        ins = tr(ps[0:HALO, 0, g * P:(g + 1) * P], u2[:, ORDER[n] % 2, g, P:P + HALO], ident(P))
                ins.then_inc(filled["1T0"], 1)

            def scores(n):
                i = ORDER[n]
                copied(pe, "1", "T1", ("qi", n))
                copied(pe, "1", "T0", ("k", n))
                for m, lo, w, h in score_steps[n]:
                    hf = HD * (h % 2)
                    claim(pe, "1", f"S{m % 2}", ("s", m))
                    mm(ps[:, 6 + m % 2, 0:w], qiT[hf:hf + HD, i % 2, h // 2, :], kiT[hf:hf + HD, lo:lo + w],
                       start=True, stop=True).then_inc(filled[f"1S{m % 2}"], 1)

            pe.wait_ge(consts_in, 32)
            pe.wait_ge(state_in, 16)
            claim(pe, "1", "T0", "state")
            for g in range(4):
                ins = tr(ps[:, 0, g * SB * HALO:(g + 1) * SB * HALO], stt_in[0:SB * HALO, g * P:(g + 1) * P], ident(SB * HALO))
            ins.then_inc(filled["1T0"], 1)
            x_turn(0)
            for n in range(TILES + 1):
                if n < TILES:
                    project(n)
                if n + 1 < TILES:
                    x_turn(n + 1)
                if n:
                    z_turn(n - 1)
                    pool_out(n - 1)
                    if n - 1 in (0, TILES - 1):
                        u_turn(n - 1)
                    if score_steps[n - 1]:
                        scores(n - 1)
            settle(pe, "1")
            pe.drain().then_inc(phase1, 1)
            pe.wait_ge(phase1, 4)


            def ki_turn(b):
                pe.wait_ge(ki_in[b % 2], 16 * (b // 2 + 1))
                for c in range(2):
                    claim(pe, "2a", "TR", (b, c))
                    for j in range(4):
                        a = 2 * (4 * c + j)
                        ins = tr(ps[:, 5, j * P:(j + 1) * P], kin[:, b % 2, a:a + 2, :].rearrange("p s d -> p (s d)"), ident(P))
                    ins.then_inc(filled["2aTR"], 1)

            def s_scores(b):
                copied(pe, "2a", "TR", (b, 1))
                for q in range(5):
                    part = (5 * b + q) % 2
                    claim(pe, "2a", f"PS{part}", (b, q))
                    if q < 4:
                        c, sp_ = q // 2, q % 2
                        hf = HD * sp_
                        mm(ps[0:SR, 6 + part, :], QS[hf:hf + HD, b].rearrange("p h t -> p (h t)"),
                           kiTs[hf:hf + HD, b % 2, 4 * c:4 * c + 4, :].rearrange("p j k -> p (j k)"),
                           start=True, stop=True).then_inc(filled[f"2aPS{part}"], 1)
                    else:
                        mm(ps[0:SR, 6 + part, 0:ST], QS[0:HD, b].rearrange("p h t -> p (h t)"),
                           kiT[0:HD, SEQ + b * ST:SEQ + (b + 1) * ST], start=True, stop=True).then_inc(filled[f"2aPS{part}"], 1)

            def weighted(b):
                for q in range(5):
                    copied(pe, "2a", f"PS{(5 * b + q) % 2}", (b, q))
                for q in range(5):
                    w = 512 if q < 4 else ST
                    ins = mm(ps[0:SR, q, 0:w], WS[0:SR, b, :], rs[0:SR, b % 2, 512 * q:512 * q + w],
                             start=(b == 0), stop=(b == SB - 1))
                ins.then_inc(sec_done, 1)
                if b == SB - 1:
                    pe.wait_ge(sec_done, SB)
                    pe.nop().then_inc(filled["2aACC"], 1)

            ki_turn(0)
            for b in range(SB):
                s_scores(b)
                if b + 1 < SB:
                    ki_turn(b + 1)
                if b:
                    weighted(b - 1)
            weighted(SB - 1)
            settle(pe, "2a")
            pe.drain().then_inc(phase2a, 1)
            pe.wait_ge(phase2a, 3)

            def q_k(i, h):
                part = h % 2
                g, w = h // GH, P * (i + 1)
                claim(pe, "2b", f"A{part}", ("S", i, h))
                for lo in range(0, w, 512):
                    e = min(512, w - lo)
                    ins = mm(ps[:, 2 * part + lo // 512, 0:e], qT[HD * g:HD * (g + 1), h % GH, i * P:(i + 1) * P],
                             kT[HD * g:HD * (g + 1), lo:lo + e], start=True, stop=True)
                ins.then_inc(filled[f"2bA{part}"], 1)

            def p_turn(i, h):
                pe.wait_ge(s_exp, i * NH + h + 1)
                for c in range(0, i + 1, 4):
                    part = pt_use["T", i, h, c]
                    claim(pe, "2b", f"PT{part}", ("T", i, h, c))
                    for j in range(c, min(c + 4, i + 1)):
                        ins = tr(ps[:, 4 + part, (j - c) * P:(j - c + 1) * P], Sm[:, h % 2, j * P:(j + 1) * P], ident(P))
                    ins.then_inc(filled[f"2bPT{part}"], 1)

            def p_v(i, h):
                if h == 0:
                    claim(pe, "2b", "O", ("V", i))
                g = h // GH
                for c in range(0, i + 1, 4):
                    copied(pe, "2b", f"PT{pt_use['T', i, h, c]}", ("T", i, h, c))
                for j in range(i + 1):
                    ins = mm(ps[:, 6, h * HD:(h + 1) * HD], PT[:, h % 2, j, :], V[:, j, g * HD:(g + 1) * HD],
                             start=(j == 0), stop=(j == i))
                ins.then_inc(av_done, 1)
                if h == NH - 1:
                    pe.wait_ge(av_done, (i + 1) * NH)
                    pe.nop().then_inc(filled["2bO"], 1)

            def tail(t):
                kind, i = t[0], t[1]
                r = rows(i)
                tok = slice(i * P, i * P + r)
                claim(pe, "2b", "M", t)
                if kind == "OT":
                    copied(pe, "2b", "O", ("V", i))
                    for c in range(4):
                        ins = tr(ps[:, 7, c * P:(c + 1) * P], Osb[:, c * P:(c + 1) * P], ident(P))
                elif kind == "OP":
                    if t[2] == 0:
                        if i < NT:
                            copied(pe, "2b", "M", ("OT", i))
                        if i == 0:
                            pe.wait_ge(wout_in, 48)
                    for k in range(8):
                        if k < 4:
                            lhs = mixP[:, k, tok]
                        else:
                            lhs = mixS[:, k - 4, :] if i == NT else mixA[:, k - 4, :]
                        ins = mm(ps[0:r, 7, :], lhs, wout[:, k, 512 * t[2]:512 * t[2] + 512], start=(k == 0), stop=(k == 7))
                elif kind == "XR":
                    pe.wait_ge(x2_ready, i + 1)
                    for j in range(4):
                        c = 4 * t[2] + j
                        ins = tr(ps[:, 7, j * r:(j + 1) * r], x2[0:r, i % 2, c * P:(c + 1) * P], ident(r))
                elif kind == "LG":
                    copied(pe, "2b", "M", ("XR", i, 1))
                    if i == 0:
                        pe.wait_ge(rw_in, 64)
                    for k in range(KC):
                        ins = mm(ps[0:r, 7, 0:36], x2T[:, k, 0:r], rw[:, k, :], start=(k == 0), stop=(k == KC - 1))
                elif kind == "RK":
                    pe.wait_ge(A_ready, i + 1)
                    mm(ps[0:r, 7, 0:NE], const("tri")[0:r, 0:r], A[0:r, :], start=True, stop=False)
                    ins = mm(ps[0:r, 7, 0:NE], const("ones")[:, 0:r], ASUM[:, :], start=False, stop=True)
                ins.then_inc(filled["2bM"], 1)

            for t in tasks:
                if t[0] == "S":
                    q_k(t[1], t[2])
                elif t[0] == "T":
                    p_turn(t[1], t[2])
                elif t[0] == "V":
                    p_v(t[1], t[2])
                else:
                    tail(t)
            for q in ("A0", "A1", "PT0", "PT1", "O"):
                pe.wait_ge(emptied["2b" + q], use["2b"][q])
            pe.wait_ge(emptied["2bM"], use["2b", "M", ("OP", NT, 0)])
            pe.drain().then_inc(prompts_done, 1)
            pe.wait_ge(prompts_done, 3)

            pe.wait_ge(smask_ready, 1)
            pe.wait_ge(Vnew_in, 16)
            for b in range(SB):
                s = b % 2
                pe.wait_ge(KV_in[s], 32 * (b // 2 + 1))
                for c in range(4):
                    part = tk_use["k", b, c]
                    claim(pe, "2c", f"TK{part}", ("k", b, c))
                    for j in range(4):
                        ins = tr(ps[:, 5 + part, j * P:(j + 1) * P], Kin[s][:, 4 * c + j, :], ident(P))
                    ins.then_inc(filled[f"2cTK{part}"], 1)
                claim(pe, "2c", "SS", b)
                smv = smask[0:SR, 0:PAST].rearrange("r (p s) -> r s p", s=SLOTS)
                for q in range(5):
                    c = min(q, 3)
                    copied(pe, "2c", f"TK{tk_use['k', b, c]}", ("k", b, c))
                    lhs = QB[:, b].rearrange("p g h t -> p (g h t)")
                    if q < 4:
                        mm(ps[0:SR, q, :], lhs, KTs[:, 512 * q:512 * (q + 1)], start=True, stop=False)
                        mm(ps[0:SR, q, :], selb[0:SR, b, :], smv[:, 4 * q:4 * q + 4, :], start=False, stop=True)
                    else:
                        mm(ps[0:SR, 4, 0:ST], lhs, kT[:, SEQ + b * ST:SEQ + (b + 1) * ST], start=True, stop=False)
                        ins = mm(ps[0:SR, 4, 0:ST], selb[0:SR, b, :], smask[0:SR, PAST:LS], start=False, stop=True)
                ins.then_inc(filled["2cSS"], 1)
                pe.wait_ge(snorm_ready, b + 1)
                for c in range(3):
                    part = tk_use["p", b, c]
                    claim(pe, "2c", f"TK{part}", ("p", b, c))
                    if c < 2:
                        for j in range(8):
                            a = 8 * c + j
                            ins = tr(ps[:, 5 + part, j * SR:(j + 1) * SR], Ps[0:SR, a * P:(a + 1) * P], ident(SR))
                    else:
                        ins = tr(ps[0:ST, 5 + part, 0:SR], Ps[0:SR, PAST:LS], ident(SR))
                    ins.then_inc(filled[f"2cTK{part}"], 1)
                claim(pe, "2c", "PV", b)
                for c in range(3):
                    copied(pe, "2c", f"TK{tk_use['p', b, c]}", ("p", b, c))
                for a in range(SLOTS):
                    mm(ps[:, 7, 0:SR], Vin[s][:, a, :], PTs[:, a, :], start=(a == 0), stop=False)
                mm(ps[:, 7, 0:SR], Vnew[:, b, :], PTs[0:ST, SLOTS, :], start=False, stop=True).then_inc(filled["2cPV"], 1)
            settle(pe, "2c")
            for t in tail_tasks(NT):
                tail(t)
            claim(pe, "2b", "M", "count")
            pe.wait_ge(ASUM_ready, TILES)
            mm(ps[:, 7, 0:NE], const("ones"), ASUM[:, :], start=True, stop=True).then_inc(filled["2bM"], 1)
            settle(pe, "2b")
            pe.drain().then_inc(phase2, 1)
            pe.wait_ge(phase2, 4)

            def rows_turn(e, q, s, first):
                pe.wait_ge(xg_in[s], q * 16 + 16)
                for c in range(2):
                    if not first:
                        pe.wait_ge(xT_emptied[c], e)
                    for j in range(4):
                        ins = tr(ps[:, c, j * P:(j + 1) * P], xg[:, s, 4 * c + j:D:KC], ident(P))
                    ins.then_inc(xT_filled[c], 1)

            def gate_up(e, q, s, first):
                pe.wait_ge(wgu_in[s], q * 32 + 32)
                for c in range(2):
                    pe.wait_ge(xT_emptied[c], e + 1)
                if not first:
                    pe.wait_ge(hid_ready, e - 1)
                for k in range(KC):
                    ins = mm(ps[:, 2 + s, :], xgT[:, s, k, :], wgu[:, s, k, :], start=(k == 0), stop=(k == KC - 1))
                ins.then_inc(gu_filled, 1)

            def down(e, q, s, first):
                pe.wait_ge(hid_ready, e + 1)
                if not first:
                    pe.wait_ge(hT_ready, e)
                for c in range(2):
                    ins = tr(ps[:, 4, c * P:(c + 1) * P], hid[:, c:HID:2], ident(P))
                ins.then_inc(hT_filled, 1)
                pe.wait_ge(hT_ready, e + 1)
                pe.wait_ge(wdn_in[s], q * 16 + 16)
                for c in range(2):
                    if not first:
                        pe.wait_ge(dn_emptied[c], e)
                    for k in range(2):
                        ins = mm(ps[:, 5 + c, :], hT[:, k, :], wdn[:, s, k, 512 * c:512 * (c + 1)], start=(k == 0), stop=(k == 1))
                    ins.then_inc(dn_filled[c], 1)

            rows_turn(0, 0, 0, True)
            gate_up(0, 0, 0, True)
            rows_turn(1, 0, 1, False)
            down(0, 0, 0, True)
            gate_up(1, 0, 1, True)
            rows_turn(2, 1, 0, False)
            down(1, 0, 1, False)
            with pe.Fori(1, NE // 2 - 1) as q:
                gate_up(q * 2, q, 0, False)
                rows_turn(q * 2 + 1, q, 1, False)
                down(q * 2, q, 0, False)
                gate_up(q * 2 + 1, q, 1, False)
                rows_turn(q * 2 + 2, q + 1, 0, False)
                down(q * 2 + 1, q, 1, False)
            gate_up(NE - 2, NE // 2 - 1, 0, False)
            rows_turn(NE - 1, NE // 2 - 1, 1, False)
            down(NE - 2, NE // 2 - 1, 0, False)
            gate_up(NE - 1, NE // 2 - 1, 1, False)
            down(NE - 1, NE // 2 - 1, 1, False)

            pe.wait_ge(dn_emptied[0], NE)
            pe.wait_ge(dn_emptied[1], NE)
            some = pe.value_load(ovb[0:1, OVB:OVB + 1], min_val=0, max_val=OVB)
            with pe.If(some > 0):
                pe.nop().then_inc(ov_pe, 4)
                with pe.Fori(0, OVB) as j:
                    pe.wait_ge(ov_x, j * 16 + 16)
                    pe.wait_ge(ov_dve, j * 4 + 4)
                    for c in range(8):
                        ins = tr(ps[:, c // 4, (c % 4) * P:(c % 4 + 1) * P], xg[:, 0, c:D:KC], ident(P))
                    ins.then_inc(ov_pe, 1)
                    pe.wait_ge(ov_w, j * 48 + 48)
                    pe.wait_ge(ov_dve, j * 4 + 5)
                    for k in range(KC):
                        ins = mm(ps[:, 2, :], xgT[:, 0, k, :], wgu[:, 0, k, :], start=(k == 0), stop=(k == KC - 1))
                    ins.then_inc(ov_pe, 1)
                    pe.wait_ge(ov_dve, j * 4 + 6)
                    for c in range(2):
                        ins = tr(ps[:, 4, c * P:(c + 1) * P], hid[:, c:HID:2], ident(P))
                    ins.then_inc(ov_pe, 1)
                    pe.wait_ge(ov_dve, j * 4 + 7)
                    for c in range(2):
                        for k in range(2):
                            ins = mm(ps[:, 5 + c, :], hT[:, k, :], wdn[:, 0, k, 512 * c:512 * (c + 1)], start=(k == 0), stop=(k == 1))
                    ins.then_inc(ov_pe, 1)
                pe.nop()
            with pe.Else():
                pe.nop()
            pe.drain().then_inc(experts_done, 1)

        @block.scalar
        def _(act):
            fn = nc.scalar.activation

            def copy(out, in_, scale=1.0):
                return fn(out, in_, ACT.Copy, scale=scale)

            def four(v, r):
                return v[:, 0:4 * r].rearrange("p (g t) -> p g t", g=4)

            def root(n):
                r = rows(ORDER[n])
                act.wait_ge(ssq_ready, n + 1)
                fn(std[0:r, n:n + 1], ssq[0:r, n:n + 1], ACT.Sqrt, scale=1.0 / D, bias=const("eps", r)).then_inc(std_ready, 1)

            def scale_rows(n):
                r = rows(ORDER[n])
                act.wait_ge(rstd_ready, n + 1)
                copy(xb[0:r, n % 3, :], xb[0:r, n % 3, :], scale=rstd[0:r, n:n + 1]).then_inc(xs_ready, 1)

            def keep_xT(n):
                r = rows(ORDER[n])
                for c in range(2):
                    take(act, "1", f"T{c}", ("x", n))
                    copy(xnT[:, n % 2, 4 * c:4 * c + 4, 0:r], ps[:, c, :].rearrange("p (g t) -> p g t", g=4)[:, :, 0:r])\
                        .then_inc(emptied[f"1T{c}"], 1)

            def keep_rows(n):
                i = ORDER[n]
                r = rows(i)
                take(act, "1", "U", n)
                if n >= 2:
                    act.wait_ge(d_ready, n - 1)
                u = four(ps[:, PART["U"], :], r)
                if i == NT:
                    copy(uC, u)
                    copy(uS[:, :, :, HALO:HALO + ST], u.rearrange("p g (b t) -> p g b t", b=SB)).then_inc(emptied["1U"], 1)
                else:
                    if i:
                        act.wait_ge(emptied["1U"], n)
                        copy(u2[:, i % 2, :, 0:HALO], u2[:, (i - 1) % 2, :, P:P + HALO])
                    else:
                        act.wait_ge(init_done, 4)
                    copy(u2[:, i % 2, :, HALO:HALO + P], u).then_inc(emptied["1U"], 1)
                if n:
                    act.wait_ge(kv_out, 48 * n)
                    take(act, "1", "T0", ("k", n - 1))
                take(act, "1", "Q", n)
                copy(Z[0:r, 0:8, :].rearrange("p (b g) d -> p g b d", g=NKV),
                     ps[0:r, PART["Q"], :].rearrange("p (g b d) -> p g b d", g=NKV, b=GH)).then_inc(emptied["1Q"], 1)
                take(act, "1", "KV", n)
                kv = ps[0:r, PART["KV"], :]
                copy(Z[0:r, 8:10, :].rearrange("p a d -> p (a d)"), kv[:, 0:P])
                copy(V[0:r, i, :], kv[:, P:2 * P])
                copy(Z[0:r, 18, :], kv[:, 2 * P:2 * P + HD])
                copy(W[0:r, i, :], kv[:, 2 * P + HD:2 * P + HD + NH], scale=(NH ** -0.5) * (HD ** -0.5)).then_inc(emptied["1KV"], 1)
                take(act, "1", "QI", n)
                copy(Z[0:r, 10:18, :].rearrange("p a d -> p (a d)"), ps[0:r, PART["QI"], :]).then_inc(emptied["1QI"], 1)

            def keep_z(n):
                i = ORDER[n]
                r = rows(i)
                tok = slice(i * P, i * P + r)
                take(act, "1", "T0", ("q", n))
                copy(qT[:, :, tok], four(ps[:, 0, :], r)).then_inc(emptied["1T0"], 1)
                take(act, "1", "T1", ("qi", n))
                if i == NT:
                    copy(QS[:, :, :, :].rearrange("p b h t -> p h b t"), ps[:, 1, :].rearrange("p (h b t) -> p h b t", h=NH, b=SB)).then_inc(emptied["1T1"], 1)
                else:
                    copy(qiT[:, i % 2], four(ps[:, 1, :], r)).then_inc(emptied["1T1"], 1)
                take(act, "1", "T0", ("k", n))
                copy(kT[:, tok], ps[:, 0, 0:r])
                copy(kiT[:, tok], ps[:, 0, r:2 * r]).then_inc(emptied["1T0"], 1)
                take(act, "1", "T1", ("pool", n))
                for g in range(4):
                    ins = copy(mixP[:, g, tok], ps[:, 1, g * r:(g + 1) * r], scale=psc[:, g:g + 1])
                ins.then_inc(emptied["1T1"], 1)
                if n == 0:
                    take(act, "1", "T0", ("u", n))
                    copy(stt_in[0:SR, :], ps[0:SR, 0, :]).then_inc(emptied["1T0"], 1)
                    copied(act, "1", "T0", ("u", n))
                    for b in range(SB):
                        act.dma_start(pool_sample[0, b, HALO - ST:HALO, :], stt_in[b * ST:(b + 1) * ST, :]).then_inc(u_out, 16)
                if n == TILES - 1:
                    take(act, "1", "T0", ("u", n))
                    act.wait_ge(u_out, 16 * SB)
                    copy(stt_in[0:HALO, :], ps[0:HALO, 0, :]).then_inc(emptied["1T0"], 1)
                    copied(act, "1", "T0", ("u", n))
                    act.dma_start(pool_prompt[0, 0], stt_in[0:HALO, :]).then_inc(u_out, 16)
                    act.wait_ge(u_out, 16 * (SB + 1))

            def relus(n):
                for m, lo, w, h in score_steps[n]:
                    take(act, "1", f"S{m % 2}", ("s", m))
                    if m >= 2:
                        act.wait_ge(score_added, m - 1)
                    fn(rl[:, m % 2, 0:w], ps[:, 6 + m % 2, 0:w], ACT.Relu).then_inc(emptied[f"1S{m % 2}"], 1)

            act.wait_ge(consts_in, 32)
            act.wait_ge(small_in, 32)
            take(act, "1", "T0", "state")
            copy(uS[:, :, :, 0:HALO], ps[:, 0, 0:4 * SB * HALO].rearrange("p (g b t) -> p g b t", g=4, b=SB))\
                .then_inc(emptied["1T0"], 1)
            for n in range(2):
                root(n)
                scale_rows(n)
            keep_xT(0)
            for n in range(TILES + 1):
                if n + 2 < TILES:
                    root(n + 2)
                if n + 1 < TILES:
                    keep_xT(n + 1)
                if n + 2 < TILES:
                    scale_rows(n + 2)
                if n:
                    keep_z(n - 1)
                if n < TILES:
                    keep_rows(n)
                if n:
                    relus(n - 1)
            act.drain().then_inc(phase1, 1)
            act.wait_ge(phase1, 4)

            def keep_ki(b):
                for c in range(2):
                    take(act, "2a", "TR", (b, c))
                    copy(kiTs[:, b % 2, 4 * c:4 * c + 4, :], four(ps[:, 5, :], P)).then_inc(emptied["2aTR"], 1)

            keep_ki(0)
            for b in range(SB):
                for q in range(5):
                    part, w = (5 * b + q) % 2, 512 if q < 4 else ST
                    take(act, "2a", f"PS{part}", (b, q))
                    if b >= 2 and q == 0:
                        act.wait_ge(sec_done, b - 1)
                    fn(rs[0:SR, b % 2, 512 * q:512 * q + w], ps[0:SR, 6 + part, 0:w], ACT.Relu).then_inc(emptied[f"2aPS{part}"], 1)
                if b + 1 < SB:
                    keep_ki(b + 1)
            take(act, "2a", "ACC", 0)
            inorder = SCs[0:SR, 0:PAST].rearrange("r (p s) -> r s p", s=SLOTS)
            for q in range(4):
                a = 8 * (q // 2) + q % 2
                copy(inorder[:, a:a + 7:2, :], ps[0:SR, q, :].rearrange("r (s p) -> r s p", s=4))
            copy(SCs[0:SR, PAST:LS], ps[0:SR, 4, 0:ST]).then_inc(emptied["2aACC"], 1)
            act.drain().then_inc(phase2a, 1)
            act.wait_ge(phase2a, 3)

            def tail(t):
                kind, i = t[0], t[1]
                r, s = rows(i), i % 2
                if kind == "OT":
                    take(act, "2b", "M", t)
                    copy(mixA[:, :, :], four(ps[:, 7, :], P)).then_inc(emptied["2bM"], 1)
                elif kind == "OP" and t[2] == 1:
                    copied(act, "2b", "M", t)
                    if i >= 2:
                        act.wait_ge(x2_out[s], 16 * (i // 2))
                        take(act, "2b", "M", ("XR", i - 2, 1))
                    fn(x2[0:r, s, :], hb[0:r, s, :], ACT.Square, accum_out=ssq2[0:r, i:i + 1]).then_inc(ssq2_ready, 1)
                    act.wait_ge(ssq2_ready, i + 1)
                    fn(std2[0:r, i:i + 1], ssq2[0:r, i:i + 1], ACT.Sqrt, scale=1.0 / D, bias=const("eps", r)).then_inc(std2_ready, 1)
                elif kind == "XR":
                    take(act, "2b", "M", t)
                    copy(x2T[:, 4 * t[2]:4 * t[2] + 4, 0:r], four(ps[:, 7, :], r)).then_inc(emptied["2bM"], 1)
                elif kind == "LG":
                    act.wait_ge(logits_split, i + 1)
                    fn(gexp[0:r, :], G8[0:r, 0:NG], ACT.Exp, bias=r1[0:r, 0:1], accum_out=r1[0:r, 2:3])
                    fn(r1[0:r, 3:4], r1[0:r, 1:2], ACT.Exp).then_inc(gexp_ready, 1)

            for t in tasks:
                kind, i = t[0], t[1]
                if kind == "S":
                    h, w = t[2], P * (i + 1)
                    act.wait_ge(s_masked, i * NH + h + 1)
                    fn(Sm[:, h % 2, 0:w], Sm[:, h % 2, 0:w], ACT.Exp, bias=nb[:, h:h + 1], scale=SCALE,
                       accum_out=esum[:, 8 * (i % 2) + h:8 * (i % 2) + h + 1]).then_inc(s_exp, 1)
                elif kind == "T":
                    h = t[2]
                    part = pt_use[t + (0,)]
                    n = min(4, i + 1)
                    take(act, "2b", f"PT{part}", t + (0,))
                    if i * NH + h >= 2:
                        act.wait_ge(av_done, i * NH + h - 1)
                    copy(PT[:, h % 2, 0:n, :], ps[:, 4 + part, 0:n * P].rearrange("p (j q) -> p j q", q=P))\
                        .then_inc(emptied[f"2bPT{part}"], 1)
                elif kind != "V":
                    tail(t)
            act.drain().then_inc(prompts_done, 1)
            act.wait_ge(prompts_done, 3)
            tiles_out(act, h_out, NT)
            tiles_out(act, x2_out, NT)

            flat = ps[:, :, :].rearrange("p b n -> p (b n)")
            for b in range(SB):
                for c in range(4):
                    part = tk_use["k", b, c]
                    take(act, "2c", f"TK{part}", ("k", b, c))
                    copy(KTs[:, 512 * c:512 * (c + 1)], ps[:, 5 + part, :]).then_inc(emptied[f"2cTK{part}"], 1)
                act.wait_ge(smax_ready, b + 1)
                fn(Ps[0:SR, :], flat[0:SR, 0:LS], ACT.Exp, bias=snb[:, b:b + 1], scale=SCALE,
                   accum_out=sesum[:, b:b + 1]).then_inc(emptied["2cSS"], 1)
                for c in (0, 2):
                    part = tk_use["p", b, c]
                    take(act, "2c", f"TK{part}", ("p", b, c))
                    if c == 0:
                        copy(PTs[:, 0:8, :], ps[:, 5 + part, :].rearrange("p (a t) -> p a t", a=8)).then_inc(emptied[f"2cTK{part}"], 1)
                    else:
                        copy(PTs[0:ST, SLOTS, :], ps[0:ST, 5 + part, 0:SR]).then_inc(emptied[f"2cTK{part}"], 1)
                take(act, "2c", "PV", b)
                for g in range(NKV):
                    pv = ps[HD * g:HD * (g + 1), 7, 32 * g:32 * g + 32].rearrange("p (h t) -> p h t", h=GH)
                    ins = copy(mixS[HD * g:HD * (g + 1), :, b * ST:(b + 1) * ST], pv)
                ins.then_inc(emptied["2cPV"], 1)
            for t in tail_tasks(NT):
                tail(t)
            act.drain().then_inc(phase2, 1)
            act.wait_ge(phase2, 4)

            def silu(e, s, first):
                act.wait_ge(gu_filled, e + 1)
                if not first:
                    act.wait_ge(hid_ready, e - 1)
                fn(sg[:, s, :], ps[:, 2 + s, 0:HID], ACT.Silu).then_inc(silu_ready, 1)

            def keep_xgT(e, s):
                act.wait_ge(xT_filled[0], e + 1)
                copy(xgT[:, s, 0:4, :], four(ps[:, 0, :], P)).then_inc(xT_emptied[0], 1)

            def keep_out(e, q, s, first):
                act.wait_ge(dn_filled[0], e + 1)
                if not first:
                    act.wait_ge(eo_out[s], q * 16)
                copy(ob[:, s, 0:512], ps[:, 5, :]).then_inc(dn_emptied[0], 1)
                for c in range(2):
                    act.wait_ge(dn_emptied[c], e + 1)
                act.dma_start(block_rows(e), ob[:, s, :]).then_inc(eo_out[s], 16)

            keep_xgT(0, 0)
            for e in range(2):
                silu(e, e, True)
                keep_xgT(e + 1, (e + 1) % 2)
                keep_out(e, 0, e, True)
            with act.Fori(1, NE // 2 - 1) as q:
                for s in range(2):
                    silu(q * 2 + s, s, False)
                    keep_xgT(q * 2 + (s + 1), (s + 1) % 2)
                    keep_out(q * 2 + s, q, s, False)
            silu(NE - 2, 0, False)
            keep_xgT(NE - 1, 1)
            keep_out(NE - 2, NE // 2 - 1, 0, False)
            silu(NE - 1, 1, False)
            keep_out(NE - 1, NE // 2 - 1, 1, False)
            for s in range(2):
                act.wait_ge(eo_out[s], 16 * (NE // 2))
            some = act.value_load(ovb[0:1, OVB:OVB + 1], min_val=0, max_val=OVB)
            with act.If(some > 0):
                act.nop().then_inc(ov_out, 16)
                with act.Fori(0, OVB) as j:
                    act.wait_ge(ov_pe, j * 4 + 6)
                    fn(sg[:, 0, :], ps[:, 2, 0:HID], ACT.Silu).then_inc(ov_act, 1)
                    act.wait_ge(ov_dve, j * 4 + 8)
                    act.dma_start(block_rows(j + NE), ob[:, 0, :]).then_inc(ov_out, 16)
                act.wait_ge(ov_out, 16 * OVB + 16)
            with act.Else():
                act.nop()
            act.drain().then_inc(experts_done, 1)
            act.wait_ge(experts_done, 4)
            for i in range(TILES):
                r, s = rows(i), i % 2
                act.wait_ge(ysum_ready, 2 * (i + 1))
                if i:
                    act.wait_ge(std3_ready, i)
                fn(sq[0:r, :], yc[0:r, s, :], ACT.Square, accum_out=ssq3[0:r, i:i + 1]).then_inc(ssq3_ready, 1)
                act.wait_ge(ssq3_ready, i + 1)
                fn(std3[0:r, i:i + 1], ssq3[0:r, i:i + 1], ACT.Sqrt, scale=1.0 / D, bias=const("eps", r)).then_inc(std3_ready, 1)

        @block.vector
        def _(dve):
            v = nc.vector
            steps = [0]

            def link(ins):
                steps[0] += 1
                ins.then_inc(dve_step, 1)
                dve.wait_ge(dve_step, steps[0])

            def inv_rms(n):
                r = rows(ORDER[n])
                x = xb[0:r, n % 3, :]
                dve.wait_ge(x_in[n % 3], 16 * (n // 3 + 1))
                v.tensor_tensor_reduce(out=junk[0:r, 0:D], in0=x, in1=x, scale=1.0, scalar=0.0, op0=ALU.mult, op1=ALU.add,
                                       accum_out=ssq[0:r, n:n + 1]).then_inc(ssq_ready, 1)
                dve.wait_ge(std_ready, n + 1)
                v.reciprocal(rstd[0:r, n:n + 1], std[0:r, n:n + 1]).then_inc(rstd_ready, 1)

            def add_scores(n):
                i = ORDER[n]
                sc = scv(i)
                for m, lo, w, h in score_steps[n]:
                    copied(dve, "1", f"S{m % 2}", ("s", m))
                    dst, src, wt = sc[:, lo:lo + w], rl[:, m % 2, 0:w], W[:, i, h:h + 1]
                    if h == 0:
                        v.tensor_scalar(dst, src, wt, None, ALU.mult).then_inc(score_added, 1)
                    else:
                        dve.wait_ge(score_added, m)
                        v.scalar_tensor_tensor(out=dst, in0=src, scalar=wt, in1=dst, op0=ALU.mult, op1=ALU.add).then_inc(score_added, 1)
                dve.wait_ge(score_added, score_steps[n][-1][0] + 1)

            def select(group):
                n = len(group)
                R = group[0][2]
                lo, hi, mid, cnt, t1, t2, need = (x[0:R, 0:n] for x in (lo_, hi_, mid_, cnt_, t1_, t2_, need_))
                for a, (sc, w, _, lastmask, _, _) in enumerate(group):
                    link(v.tensor_reduce(lo[:, a:a + 1], sc, AX.X, ALU.min))
                    link(v.tensor_reduce(hi[:, a:a + 1], sc, AX.X, ALU.max))
                    k = lastmask.shape[1]
                    link(v.tensor_tensor(sc[:, w - k:w], sc[:, w - k:w], lastmask, ALU.add))
                link(v.tensor_tensor(mid, lo, hi, ALU.add))
                link(v.tensor_scalar(mid, mid, 0.5, None, ALU.mult))
                base, per = steps[0], n + 8
                with dve.Fori(0, ITERS) as it:
                    k = [0]

                    def lnk(ins):
                        k[0] += 1
                        ins.then_inc(dve_step, 1)
                        dve.wait_ge(dve_step, it * per + (base + k[0]))

                    for a, (sc, w, _, _, _, (jk, _, _)) in enumerate(group):
                        lnk(v.tensor_scalar(jk[0:R, 0:w], sc, mid[:, a:a + 1], None, ALU.is_ge, ALU.add, accum_out=cnt[:, a:a + 1]))
                    lnk(v.tensor_scalar(t1, cnt, float(TOPK), -2 * BIG, ALU.is_lt, ALU.mult))
                    lnk(v.tensor_scalar(t2, cnt, float(TOPK), 2 * BIG, ALU.is_ge, ALU.mult))
                    lnk(v.tensor_tensor(t1, t1, mid, ALU.add))
                    lnk(v.tensor_tensor(t2, t2, mid, ALU.add))
                    lnk(v.tensor_tensor(lo, lo, t1, ALU.max))
                    lnk(v.tensor_tensor(hi, hi, t2, ALU.min))
                    lnk(v.tensor_tensor(mid, lo, hi, ALU.add))
                    lnk(v.tensor_scalar(mid, mid, 0.5, None, ALU.mult))
                steps[0] += per * ITERS
                for a, (sc, w, _, _, out, (_, G, T)) in enumerate(group):
                    g, t, nd = G[0:R, 0:w], T[0:R, 0:w], need[:, a:a + 1]
                    link(v.tensor_scalar(g, sc, hi[:, a:a + 1], None, ALU.is_gt, ALU.add, accum_out=nd))
                    link(v.tensor_scalar(nd, nd, -1.0, float(TOPK), ALU.mult, ALU.add))
                    link(v.scalar_tensor_tensor(out=t, in0=sc, scalar=lo[:, a:a + 1], in1=g, op0=ALU.is_ge, op1=ALU.subtract))
                    link(v.tensor_tensor_scan(sc, t, t, 0.0, ALU.add, ALU.max))
                    link(v.scalar_tensor_tensor(out=t, in0=sc, scalar=nd, in1=t, op0=ALU.is_le, op1=ALU.mult))
                    link(v.scalar_tensor_tensor(out=t, in0=t, scalar=-1.0, in1=g, op0=ALU.add, op1=ALU.add))
                    link(v.tensor_scalar(out, t, BIG, None, ALU.mult))

            inv_rms(0)
            inv_rms(1)
            pending = [list(g) for g in SEL_GROUPS]
            for n in range(TILES + 1):
                if n + 2 < TILES:
                    inv_rms(n + 2)
                if n and score_steps[n - 1]:
                    add_scores(n - 1)
                    if n == TILES:
                        dve.drain().then_inc(phase1, 1)
                    if pending[0][-1] == ORDER[n - 1]:
                        select([(scv(i), P * (i + 1), P, const("dmask"), maskv(i), (junk, selG, selT)) for i in pending.pop(0)])
            flat = ps[:, :, :].rearrange("p b n -> p (b n)")
            copied(dve, "2a", "ACC", 0)
            select([(SCs[0:SR, :], LS, SR, const("tailmask", SR), smask[0:SR, :], (sJ, sG, sT))])
            dve.nop().then_inc(smask_ready, 1)
            dve.wait_ge(phase2a, 3)
            link(v.memset(ASUM[:, :], 0.0))
            link(v.memset(G8[:, NG:8], -BIG))
            link(v.memset(A[:, :], 0.0))
            link(v.memset(RK[:, :, :], 0.0))
            link(v.memset(EF[:, :, :], 0.0))
            dve.wait_ge(init_done, 6)

            def route(i):
                r = rows(i)
                v.tensor_tensor(L[0:r, :], ps[0:r, 7, 0:36], bias36[0:r, :], ALU.add).then_inc(emptied["2bM"], 1)
                copied(dve, "2b", "M", ("LG", i))
                link(v.tensor_copy(G8[0:r, 0:NG], L[0:r, 0:NG]))
                link(v.max(gm8[0:r, :], G8[0:r, :]))
                link(v.max_index(gi8[0:r, :], gm8[0:r, :], G8[0:r, :]))
                link(v.tensor_copy(r1[0:r, 4:5], gi8[0:r, 0:1]))
                link(v.tensor_scalar(oh4[0:r, :], const("iota", r)[:, 0:NG], r1[0:r, 4:5], None, ALU.is_equal))
                link(v.tensor_scalar(oh4[0:r, :], oh4[0:r, :], -1.0, BIG, ALU.add, ALU.mult))
                pen = oh4[0:r, :].unsqueeze(2).broadcast_to([r, NG, EPG])
                link(v.tensor_tensor(E32[0:r, :].rearrange("p (g e) -> p g e", g=NG), L[0:r, NG:36].rearrange("p (g e) -> p g e", g=NG),
                                     pen, ALU.add))
                link(v.max(em8[0:r, :], E32[0:r, :]))
                link(v.max_index(ei8[0:r, :], em8[0:r, :], E32[0:r, :]))
                link(v.tensor_scalar(r1[0:r, 0:1], gm8[0:r, 0:1], -1.0, None, ALU.mult))
                v.tensor_tensor(r1[0:r, 1:2], em8[0:r, 1:2], em8[0:r, 0:1], ALU.subtract).then_inc(logits_split, 1)
                link(v.tensor_copy(EF[0:r, i, :], ei8[0:r, 0:2]))
                for k in range(2):
                    link(v.tensor_scalar(OH[0:r, k, :], const("iota", r), EF[0:r, i, k:k + 1], None, ALU.is_equal))
                v.tensor_tensor(A[0:r, :], OH[0:r, 0, :], OH[0:r, 1, :], ALU.add).then_inc(A_ready, 1)
                dve.wait_ge(gexp_ready, i + 1)
                link(v.tensor_scalar(r1[0:r, 5:6], r1[0:r, 3:4], 1.0, None, ALU.add))
                link(v.tensor_tensor(r1[0:r, 5:6], r1[0:r, 5:6], r1[0:r, 2:3], ALU.mult))
                link(v.reciprocal(CW[0:r, i, 0:1], r1[0:r, 5:6]))
                link(v.tensor_tensor(CW[0:r, i, 1:2], CW[0:r, i, 0:1], r1[0:r, 3:4], ALU.mult))

            def rank(i):
                r = rows(i)
                for k in range(2):
                    ins = v.tensor_tensor_reduce(out=rkt[0:r, :], in0=ps[0:r, 7, 0:NE], in1=OH[0:r, k, :], scale=1.0, scalar=0.0,
                                                 op0=ALU.mult, op1=ALU.add, accum_out=RK[0:r, i, k:k + 1])
                    if k == 0:
                        link(ins)
                ins.then_inc(emptied["2bM"], 1)
                copied(dve, "2b", "M", ("RK", i))
                v.tensor_tensor(ASUM[0:r, :], ASUM[0:r, :], A[0:r, :], ALU.add).then_inc(ASUM_ready, 1)
                dve.wait_ge(ASUM_ready, i + 1)

            def tail(t):
                kind, i = t[0], t[1]
                r, s = rows(i), i % 2
                if kind == "OP":
                    take(dve, "2b", "M", t)
                    dve.wait_ge(xr_in[s], 16 * (i // 2 + 1))
                    half = hb[0:r, s, 512 * t[2]:512 * t[2] + 512]
                    v.tensor_tensor(half, ps[0:r, 7, :], half, ALU.add).then_inc(emptied["2bM"], 1)
                    if t[2] == 1:
                        dve.wait_ge(std2_ready, i + 1)
                        if i == 0:
                            dve.wait_ge(gb_in, 16)
                        link(v.reciprocal(rstd2[0:r, i:i + 1], std2[0:r, i:i + 1]))
                        v.scalar_tensor_tensor(out=x2[0:r, s, :], in0=hb[0:r, s, :], scalar=rstd2[0:r, i:i + 1], in1=gb[0:r, :],
                                               op0=ALU.mult, op1=ALU.mult).then_inc(x2_ready, 1)
                elif kind == "LG":
                    take(dve, "2b", "M", t)
                    if i == 0:
                        dve.wait_ge(rw_in, 64)
                    route(i)
                elif kind == "RK":
                    take(dve, "2b", "M", t)
                    rank(i)

            def last_chunk(i, h):
                return ("T", i, h, 4 if i >= 4 else 0)

            for t in tasks:
                kind, i = t[0], t[1]
                if kind == "S":
                    h, w, idx = t[2], P * (i + 1), i * NH + t[2]
                    take(dve, "2b", f"A{h % 2}", t)
                    if idx >= 2:
                        key = last_chunk(*divmod(idx - 2, NH))
                        take(dve, "2b", f"PT{pt_use[key]}", key)
                    sc2 = ps[:, 2 * (h % 2):2 * (h % 2) + 2, :].rearrange("p b n -> p (b n)")[:, 0:w]
                    v.tensor_tensor_reduce(out=Sm[:, h % 2, 0:w], in0=sc2, in1=maskv(i), scale=1.0, scalar=-3e38, op0=ALU.add,
                                           op1=ALU.max, accum_out=mx[:, h:h + 1]).then_inc(emptied[f"2bA{h % 2}"], 1)
                    copied(dve, "2b", f"A{h % 2}", t)
                    v.tensor_scalar(nb[:, h:h + 1], mx[:, h:h + 1], -SCALE, None, ALU.mult).then_inc(s_masked, 1)
                elif kind == "T":
                    h = t[2]
                    if i >= 4:
                        part = pt_use[t + (4,)]
                        n = i + 1 - 4
                        take(dve, "2b", f"PT{part}", t + (4,))
                        if i * NH + h >= 2:
                            dve.wait_ge(av_done, i * NH + h - 1)
                        v.tensor_copy(PT[:, h % 2, 4:4 + n, :], ps[:, 4 + part, 0:n * P].rearrange("p (j q) -> p j q", q=P))\
                            .then_inc(emptied[f"2bPT{part}"], 1)
                elif kind == "V":
                    if t[2] == NH - 1:
                        take(dve, "2b", "O", ("V", i))
                        if i:
                            take(dve, "2b", "M", ("OT", i - 1))
                        dve.wait_ge(s_exp, (i + 1) * NH)
                        e8 = slice(8 * (i % 2), 8 * (i % 2) + 8)
                        link(v.reciprocal(einv[:, e8], esum[:, e8]))
                        inv = einv[:, e8].rearrange("p (g b) -> p g b", g=NKV).unsqueeze(3).broadcast_to([P, NKV, GH, HD])
                        v.tensor_tensor(Osb[:, :].rearrange("p (b g d) -> p g b d", g=NKV, b=GH),
                                        ps[:, 6, :].rearrange("p (g b d) -> p g b d", g=NKV, b=GH), inv, ALU.mult)\
                            .then_inc(emptied["2bO"], 1)
                else:
                    tail(t)
            dve.drain().then_inc(prompts_done, 1)
            dve.wait_ge(prompts_done, 3)
            flat = ps[:, :, :].rearrange("p b n -> p (b n)")
            for b in range(SB):
                take(dve, "2c", "SS", b)
                link(v.tensor_reduce(smx[:, b:b + 1], flat[0:SR, 0:LS], AX.X, ALU.max))
                v.tensor_scalar(snb[:, b:b + 1], smx[:, b:b + 1], -SCALE, None, ALU.mult).then_inc(smax_ready, 1)
                copied(dve, "2c", "SS", b)
                link(v.reciprocal(seinv[:, b:b + 1], sesum[:, b:b + 1]))
                v.tensor_scalar(Ps[0:SR, :], Ps[0:SR, :], seinv[:, b:b + 1], None, ALU.mult).then_inc(snorm_ready, 1)
                part = tk_use["p", b, 1]
                take(dve, "2c", f"TK{part}", ("p", b, 1))
                v.tensor_copy(PTs[:, 8:16, :], ps[:, 5 + part, :].rearrange("p (a t) -> p a t", a=8)).then_inc(emptied[f"2cTK{part}"], 1)
            for t in tail_tasks(NT):
                tail(t)
            take(dve, "2b", "M", "count")
            v.tensor_copy(cntE[:, :], ps[:, 7, 0:NE]).then_inc(emptied["2bM"], 1)
            copied(dve, "2b", "M", "count")
            link(v.tensor_scalar(ovE[:, :], cntE[:, :], float(CAP), None, ALU.is_gt))
            for j in range(2, NTOK // CAP + 1):
                link(v.tensor_scalar(ovX[:, :], cntE[:, :], float(CAP * j), None, ALU.is_gt))
                link(v.tensor_tensor(ovE[:, :], ovE[:, :], ovX[:, :], ALU.add))
            link(v.memset(ovT[:, :], 0.0))
            link(v.tensor_tensor_scan(ovX[:, :], ovE[:, :], ovT[:, :], 0.0, ALU.add, ALU.add))
            link(v.tensor_tensor(ovS[:, :], ovX[:, :], ovE[:, :], ALU.subtract))
            efl, rkf = EF[:, :, :].rearrange("p i k -> p (i k)"), RK[:, :, :].rearrange("p i k -> p (i k)")
            for a in range(2 * TILES):
                link(v.tensor_scalar(ovT[:, :], const("iota"), efl[:, a:a + 1], None, ALU.is_equal))
                link(v.tensor_tensor_reduce(out=rkt[:, :], in0=ovT[:, :], in1=ovS[:, :], scale=1.0, scalar=0.0, op0=ALU.mult,
                                            op1=ALU.add, accum_out=OS[:, a:a + 1]))
            link(v.scalar_tensor_tensor(out=DF[:, :], in0=OS[:, :], scalar=1.0, in1=efl, op0=ALU.mult, op1=ALU.subtract))
            link(v.tensor_scalar(DF[:, :], DF[:, :], float(P), float(NE * P - CAP), ALU.mult, ALU.add))
            link(v.tensor_scalar(DB[:, :], rkf, float(CAP), None, ALU.is_ge))
            link(v.tensor_tensor(DF[:, :], DF[:, :], DB[:, :], ALU.mult))
            link(v.tensor_tensor(DF[:, :], DF[:, :], rkf, ALU.add))
            link(v.scalar_tensor_tensor(out=DF[:, :], in0=efl, scalar=float(P), in1=DF[:, :], op0=ALU.mult, op1=ALU.add))
            link(v.tensor_copy(dest[:, :, :].rearrange("p i k -> p (i k)"), DF[:, :]))
            for j in range(OVB):
                link(v.tensor_scalar(ovT[:, :], ovX[:, :], float(j), None, ALU.is_le, ALU.add, accum_out=ovf[:, j:j + 1]))
            link(v.tensor_copy(ovf[:, OVB:OVB + 1], ovX[:, NE - 1:NE]))
            link(v.tensor_scalar(ovf[:, 0:OVB], ovf[:, 0:OVB], float(NE - 1), None, ALU.min))
            v.tensor_copy(ovb[:, :], ovf[:, :]).then_inc(dest_ready, 1)
            dve.drain().then_inc(phase2, 1)
            dve.wait_ge(phase2, 4)

            def gate(e, s, first):
                dve.wait_ge(silu_ready, e + 1)
                if not first:
                    dve.wait_ge(hT_filled, e)
                v.tensor_tensor(hid[:, :], sg[:, s, :], ps[:, 2 + s, HID:2 * HID], ALU.mult).then_inc(hid_ready, 1)

            def keep_xgT(e, s):
                dve.wait_ge(xT_filled[1], e + 1)
                v.tensor_copy(xgT[:, s, 4:8, :], ps[:, 1, :].rearrange("p (j t) -> p j t", j=4)).then_inc(xT_emptied[1], 1)

            def keep_hT(e, first):
                dve.wait_ge(hT_filled, e + 1)
                if not first:
                    dve.wait_ge(dn_filled[1], e)
                v.tensor_copy(hT[:, :, :].rearrange("p c t -> p (c t)"), ps[:, 4, 0:2 * P]).then_inc(hT_ready, 1)

            def keep_out(e, q, s, first):
                dve.wait_ge(dn_filled[1], e + 1)
                if not first:
                    dve.wait_ge(eo_out[s], q * 16)
                v.tensor_copy(ob[:, s, 512:1024], ps[:, 6, :]).then_inc(dn_emptied[1], 1)

            keep_xgT(0, 0)
            for e in range(2):
                gate(e, e, e == 0)
                keep_xgT(e + 1, (e + 1) % 2)
                keep_hT(e, e == 0)
                keep_out(e, 0, e, True)
            with dve.Fori(1, NE // 2 - 1) as q:
                for s in range(2):
                    gate(q * 2 + s, s, False)
                    keep_xgT(q * 2 + (s + 1), (s + 1) % 2)
                    keep_hT(q * 2 + s, False)
                    keep_out(q * 2 + s, q, s, False)
            gate(NE - 2, 0, False)
            keep_xgT(NE - 1, 1)
            keep_hT(NE - 2, False)
            keep_out(NE - 2, NE // 2 - 1, 0, False)
            gate(NE - 1, 1, False)
            keep_hT(NE - 1, False)
            keep_out(NE - 1, NE // 2 - 1, 1, False)
            for s in range(2):
                dve.wait_ge(eo_out[s], 16 * (NE // 2))
            some = dve.value_load(ovb[0:1, OVB:OVB + 1], min_val=0, max_val=OVB)
            with dve.If(some > 0):
                dve.nop().then_inc(ov_dve, 4)
                with dve.Fori(0, OVB) as j:
                    dve.wait_ge(ov_pe, j * 4 + 5)
                    v.tensor_copy(xgT[:, 0].rearrange("p c t -> p (c t)"), flat[:, 0:1024]).then_inc(ov_dve, 1)
                    dve.wait_ge(ov_act, j + 1)
                    v.tensor_tensor(hid[:, :], sg[:, 0, :], ps[:, 2, HID:2 * HID], ALU.mult).then_inc(ov_dve, 1)
                    dve.wait_ge(ov_pe, j * 4 + 7)
                    v.tensor_copy(hT[:, :, :].rearrange("p c t -> p (c t)"), ps[:, 4, 0:2 * P]).then_inc(ov_dve, 1)
                    dve.wait_ge(ov_pe, j * 4 + 8)
                    dve.wait_ge(ov_out, j * 16 + 16)
                    v.tensor_copy(ob[:, 0, :], flat[:, 5 * 512:7 * 512]).then_inc(ov_dve, 1)
                dve.nop()
            with dve.Else():
                dve.nop()
            dve.drain().then_inc(experts_done, 1)
            dve.wait_ge(experts_done, 4)
            dve.wait_ge(fin_norm_in, 16)

            def finish(i):
                r, s = rows(i), i % 2
                dve.wait_ge(std3_ready, i + 1)
                link(v.reciprocal(rstd3[0:r, i:i + 1], std3[0:r, i:i + 1]))
                v.scalar_tensor_tensor(out=yc[0:r, s, :], in0=yc[0:r, s, :], scalar=rstd3[0:r, i:i + 1], in1=gb[0:r, :],
                                       op0=ALU.mult, op1=ALU.mult).then_inc(y_ready[s], 1)

            for i in range(TILES):
                r, s = rows(i), i % 2
                dve.wait_ge(o_in[s], 32 * (i // 2 + 1))
                dve.wait_ge(hc_in[s], 16 * (i // 2 + 1))
                if i >= 2:
                    dve.wait_ge(y_out[s], 16 * (i // 2))
                v.scalar_tensor_tensor(out=yc[0:r, s, :], in0=o1[0:r, s, :], scalar=CW[0:r, i, 0:1], in1=hc[0:r, s, :],
                                       op0=ALU.mult, op1=ALU.add).then_inc(ysum_ready, 1)
                dve.wait_ge(ysum_ready, 2 * i + 1)
                v.scalar_tensor_tensor(out=yc[0:r, s, :], in0=o2[0:r, s, :], scalar=CW[0:r, i, 1:2], in1=yc[0:r, s, :],
                                       op0=ALU.mult, op1=ALU.add).then_inc(ysum_ready, 1)
                if i:
                    finish(i - 1)
            finish(TILES - 1)


_INS = ['x_prompt', 'x_sample', 'cache_k', 'cache_v', 'cache_idx_k', 'state_pool', 'page_table', 'norm_mix_g', 'w_in',
        'pool_w', 'pool_scale', 'w_out', 'norm_ffn_g', 'router_group_w', 'router_group_b', 'router_expert_w',
        'router_expert_b', 'expert_w_gate', 'expert_w_up', 'expert_w_down', 'final_norm_g']
_OUTS = [(1, SEQ, D), (SB, ST, D), (1, 1, SEQ, NKV, HD), (1, 1, SEQ, NKV, HD), (1, 1, SEQ, HD), (1, 1, HALO, 512),
         (1, SB, ST, NKV, HD), (1, SB, ST, NKV, HD), (1, SB, ST, HD), (1, SB, HALO, 512)]


def kernel(**inputs):
    import concourse.bacc as bacc
    from concourse.bass_utils import run_bass_kernel_spmd

    nc = bacc.Bacc("TRN2", target_bir_lowering=False, num_devices=1)
    arrays, args = {}, []
    table, spread = constants()
    values = [(name, np.ascontiguousarray(inputs[name])) for name in _INS] + [("const_table", table), ("head_select", spread)]
    for name, a in values:
        arrays[f"in_{name}"] = a
        args.append(nc.dram_tensor(f"in_{name}", a.shape, mybir.dt.from_np(a.dtype), kind="ExternalInput").ap())
    for i, shape in enumerate(_OUTS):
        args.append(nc.dram_tensor(f"out_{i}", shape, F32, kind="ExternalOutput").ap())
    program(nc, *args)
    r = run_bass_kernel_spmd(nc, [arrays], core_ids=[0])
    return tuple(r.results[0][f"out_{i}"] for i in range(len(_OUTS)))
```

```python
from contextlib import ExitStack

import numpy as np

import concourse.bass as bass
from concourse import mybir

F32 = mybir.dt.float32
BF16 = mybir.dt.bfloat16
U32 = mybir.dt.uint32
I32 = mybir.dt.int32
ALU = mybir.AluOpType
ACT = mybir.ActivationFunctionType
AX = mybir.AxisListType

P = 128
D = 1024
KC = D // P
SEQ = 1024
NT = SEQ // P
SB, ST = 8, 8
SR = SB * ST
NTOK = SEQ + SR
TILES = NT + 1
PAST, PAGE = 2048, 128
NPG = PAST // PAGE
SLOTS = PAST // P
LS = PAST + ST
HD, NH, NKV = 64, 8, 2
GH = NH // NKV
ROPE = 16
TOPK = 256
NIN = 1864
CU, CQ, CK, CV, CQI, CKI, CWI = 0, 512, 1024, 1152, 1280, 1792, 1856
WINDOWS = (2, 4, 8, 16)
HALO = 15
NG, EPG = 4, 8
NE = NG * EPG
HID = 256
CAP = 96
OVB = 2 * NTOK // CAP
OVB += -OVB % 8
NBLK = NE + OVB
EPS = 1e-6
SCALE = HD ** -0.5
BIG = 1e30
ITERS = 26
EARLY = {7: 10, 8: 12}
ZS = 20
ORDER = [NT] + list(range(NT))

CC = {}
_at = 0
for _n, _w in (("ident", P), ("dmask", P), ("tri", P), ("ones", P), ("cos", TILES * ROPE), ("sin", TILES * ROPE),
               ("pinv", 4 * 16), ("iota", NE), ("tailmask", ST), ("diag", ST), ("tokid", TILES), ("pmod", 1), ("eps", 1), ("z", 1)):
    CC[_n] = (_at, _at + _w)
    _at += _w
NCONST = _at


def constants():
    c = np.zeros((P, NCONST), np.float32)

    def put(name, a):
        lo, hi = CC[name]
        a = np.asarray(a, np.float32)
        c[:a.shape[0], lo:hi] = a.reshape(a.shape[0], -1)

    r = np.arange(P)
    put("ident", np.eye(P))
    put("dmask", np.where(r[None, :] <= r[:, None], 0.0, -BIG))
    put("tri", (r[:, None] < r[None, :]))
    put("ones", np.ones((P, P)))
    half = ROPE // 2
    inv = np.power(np.float32(500000.0), -np.arange(half, dtype=np.float32) / np.float32(half)).astype(np.float32)
    pos = np.zeros((TILES, P), np.float32)
    pos[:NT] = np.arange(SEQ).reshape(NT, P)
    pos[NT, :SR] = PAST + np.arange(SR) % ST
    ang = (pos[:, :, None] * inv).astype(np.float32)
    co, si = np.cos(ang), np.sin(ang)
    put("cos", np.concatenate([co, co], -1).transpose(1, 0, 2))
    put("sin", np.concatenate([-si, si], -1).transpose(1, 0, 2))
    put("pinv", np.tile(np.stack([1.0 / np.minimum(np.arange(16) + 1, w) for w in WINDOWS]).reshape(1, -1), (P, 1)))
    put("iota", np.tile(np.arange(NE)[None], (P, 1)))
    rs = np.arange(SR)
    put("tailmask", np.where(np.arange(ST)[None] <= (rs % ST)[:, None], 0.0, -BIG))
    put("diag", ((rs % ST)[:, None] == np.arange(ST)[None]))
    tok = np.arange(TILES)[None] * P + r[:, None]
    put("tokid", np.minimum(tok, NTOK - 1))
    put("pmod", (r % (P // NPG))[:, None])
    put("eps", np.full((P, 1), EPS))
    s = np.zeros((SR, SB, NH, ST), np.float32)
    for b in range(SB):
        for t in range(ST):
            s[b * ST + t, b, :, t] = 1.0
    return c, s.reshape(SR, SB * SR)


def mask_at(i):
    return P * (i * (i + 1) // 2)


def program(nc, x_prompt, x_sample, cache_k, cache_v, cache_idx_k, state_pool, page_table, norm_mix_g, w_in,
            pool_w, pool_scale, w_out, norm_ffn_g, router_group_w, router_group_b, router_expert_w,
            router_expert_b, expert_w_gate, expert_w_up, expert_w_down, final_norm_g, const_table, head_select,
            y_prompt, y_sample, k_prompt, v_prompt, idx_k_prompt, pool_prompt,
            k_sample, v_sample, idx_k_sample, pool_sample):
    ctx = ExitStack()
    with ctx:
        def sem(name):
            return ctx.enter_context(nc.semaphore(name))

        TOTAL = 53200
        mem = ctx.enter_context(nc.sbuf_tensor("mem", [P, TOTAL], F32))
        ps = ctx.enter_context(nc.psum_tensor("ps", [P, 8, 512], F32))
        at = [0]

        def cut(n, shape=None, dt=F32):
            lo = at[0]
            at[0] += n
            assert at[0] <= TOTAL, at[0]
            v = mem[:, lo:lo + n]
            if dt is not F32:
                v = v.bitcast(dt)
            if shape:
                names = "abcd"[:len(shape)]
                v = v.rearrange(f"p ({' '.join(names)}) -> p {' '.join(names)}", **dict(zip(names, shape)))
            return v

        con = cut(NCONST)
        selb = cut(SB * SR // 2, (SB, SR), BF16)
        stat = cut(256)
        gb = cut(D)
        psc = cut(4)
        early = at[0]
        qT = cut(4 * NTOK, (4, NTOK))
        kiT = cut(NTOK)
        kT = cut(NTOK)
        V = cut(TILES * P, (TILES, P))
        mix_at = at[0]
        mixP = cut(4 * NTOK, (4, NTOK))
        mask_at_word = at[0]
        mask = cut(36 * P // 2, None, BF16)
        kin = mask.bitcast(F32)[:, 3 * P // 2:3 * P // 2 + 2 * SLOTS * HD].rearrange("p (a s d) -> p a s d", a=2, s=SLOTS)
        SC = cut(33 * P)
        junk = cut(512, None, BF16)
        selG = cut(512, None, BF16)
        selT = cut(512, None, BF16)
        rl = cut(2 * 512, (2, 512))
        rl_end = at[0]
        W = cut(TILES * 8, (TILES, 8))
        QS = cut(NH * SR, (SB, NH, ST))
        uC = SC[:, 0:4 * SR].rearrange("p (g t) -> p g t", g=4)
        Ztwice = SC[:, 1024:2048].rearrange("p (h a d) -> p h a d", h=NH, a=2)
        WS = cut(SB * SR, (SB, SR))
        QB = cut(SB * SR, (SB, 2, GH, ST))
        persistent = at[0]

        win = cut(KC * NIN, (KC, NIN))
        qiT = cut(2 * 512, (2, 4, P))
        u2 = cut(2 * 4 * (P + HALO), (2, 4, P + HALO))
        uS = cut(4 * SB * (ST + HALO), (4, SB, ST + HALO))
        xb = cut(3 * D, (3, D))
        xnT = cut(2 * D, (2, KC, P))
        Z = cut(ZS * HD, (ZS, HD))
        sumA = cut(736)
        sumB = cut(736)
        dT = cut(4 * P)
        rt1 = cut(19 * ROPE, (19, ROPE))
        rt2 = cut(19 * ROPE, (19, ROPE))
        pw = cut(4 * P, (4, P))
        stt_in = cut(512)

        at[0] = persistent
        rt = cut(1400)
        rw = cut(KC * 36, (KC, 36))
        wout = cut(8 * D, (8, D))
        SCs = cut(LS)
        sG = cut(LS // 2, None, BF16)
        sT = cut(LS // 2, None, BF16)
        sJ = cut(LS // 2, None, BF16)
        smask = cut(LS // 2, None, BF16)
        region = at[0]
        kiTs = cut(2 * 1024, (2, 8, P))
        rs = cut(2 * LS, (2, LS))
        zslots = cut(NBLK * 16, None, I32)
        at[0] = region
        Sm = cut(3 * 1024, (3, 1024))
        PT = cut(2 * 1024, (2, 8, P))
        hb = cut(2 * D, (2, D))
        x2 = cut(2 * D, (2, D))
        x2T = cut(D, (KC, P))
        Osb = cut(512)
        mixA = cut(512, (4, P))
        at[0] = region
        mixS = cut(4 * SR, (4, SR))
        Os = cut(P)
        KTs = cut(LS)
        Ps = cut(LS)
        PTs = cut((SLOTS + 1) * SR, (SLOTS + 1, SR))
        Kin = [SC[:, 0:2048].rearrange("p (s d) -> p s d", d=P), cut(2048, (SLOTS, P))]
        Vin = [SC[:, 2048:4096].rearrange("p (s d) -> p s d", d=P), cut(2048, (SLOTS, P))]
        Vnew = rl[:, :, :].rearrange("p a n -> p (a n)")[0:ST, :].rearrange("t (b n) -> t b n", b=SB)
        assert at[0] <= TOTAL

        at[0] = early
        wgu, wdn = [], []
        for start, end in ((early, mix_at), (mask_at_word, rl_end)):
            at[0] = start
            wgu.append(cut(2 * KC * HID, (2, KC, HID)))
            wdn.append(cut(2 * D, (2, D)))
            assert at[0] <= end
        at[0] = persistent + 1400
        xg = cut(2 * D, (2, D))
        xgT = cut(2 * KC * CAP, (2, KC, CAP))
        sg = cut(2 * 2 * CAP, (2, 2 * CAP))
        hT = cut(2 * 2 * CAP, (2, 2, CAP))
        assert at[0] <= TOTAL
        at[0] = mix_at
        ob = cut(2 * D, (2, D))
        assert at[0] <= mask_at_word
        at[0] = early
        o1 = cut(2 * D, (2, D))
        o2 = cut(2 * D, (2, D))
        hc = cut(2 * D, (2, D))
        yc = cut(2 * D, (2, D))
        sq = cut(D)
        def const(name, rows=P):
            lo, hi = CC[name]
            return con[0:rows, lo:hi]

        def ident(n):
            return con[0:n, CC["ident"][0]:CC["ident"][0] + n]

        def cs(name, i, rows):
            lo = CC[name][0] + i * ROPE
            return con[0:rows, lo:lo + ROPE]

        def rows(i):
            return SR if i == NT else P

        ssq, std, rstd = stat[:, 0:9], stat[:, 9:18], stat[:, 18:27]
        lo_, hi_, mid_, midh_ = (stat[:, 30 + 7 * j:37 + 7 * j] for j in range(4))
        cnt_, t1_, t2_, need_ = (stat[:, 219 + 7 * j:226 + 7 * j] for j in range(4))
        mx, nb = stat[:, 60:68], stat[:, 68:76]
        esum, einv = stat[:, 76:92], stat[:, 92:108]
        ssq2, std2, rstd2 = stat[:, 108:117], stat[:, 117:126], stat[:, 126:135]
        wsc = stat[0:SR, 135:143]
        pt_i = stat[:, 143:151].bitcast(I32)
        pidx = stat[:, 151:159].bitcast(U32)
        smx, snb, sesum, seinv = (stat[0:SR, 160 + 8 * j:168 + 8 * j] for j in range(4))
        ssq3, std3, rstd3 = stat[:, 192:201], stat[:, 201:210], stat[:, 210:219]

        rt_at = [0]

        def rcut(n, dt=F32):
            rt_at[0] += n
            v = rt[:, rt_at[0] - n:rt_at[0]]
            return v if dt is F32 else v.bitcast(dt)

        bias36 = rcut(36)
        L = rcut(36)
        G8 = rcut(8)
        gm8, gi8 = rcut(8), rcut(8, U32)
        E32 = rcut(NE)
        em8, ei8 = rcut(8), rcut(8, U32)
        r1 = rcut(8)
        gexp = rcut(4)
        oh4 = rcut(4)
        OH = rcut(2 * NE).rearrange("p (k e) -> p k e", k=2)
        A = rcut(NE)
        ASUM = rcut(NE)
        rkt = rcut(NE)
        RK = rcut(2 * TILES).rearrange("p (i k) -> p i k", k=2)
        EF = rcut(2 * TILES).rearrange("p (i k) -> p i k", k=2)
        CW = rcut(2 * TILES).rearrange("p (i k) -> p i k", k=2)
        dest = rcut(2 * TILES, U32).rearrange("p (i k) -> p i k", k=2)
        cntE, ovE, ovS, ovX, ovT = (rcut(NE) for _ in range(5))
        OS, DB, DF = (rcut(2 * TILES) for _ in range(3))
        first = rcut(2 * TILES, U32).rearrange("p (i k) -> p i k", k=2)
        FF = rcut(2)
        toki = rcut(16 * TILES, I32).rearrange("p (i k) -> p i k", k=16)
        ovb = rcut(OVB + 1, I32)
        ovf = rcut(OVB + 1)
        slot_tok = rcut(NBLK, U32)
        assert rt_at[0] <= 1400

        def scv(i):
            lo = mask_at(i) - mask_at(2)
            return SC[:, lo:lo + P * (i + 1)]

        def maskv(i):
            return mask[:, mask_at(i):mask_at(i) + P * (i + 1)]

        def bank(b, r=P, n=512):
            return ps[0:r, b, 0:n]

        def rowsof(ap, i):
            return ap[0][i * P:(i + 1) * P] if i < NT else ap[1]

        x_rows = (x_prompt[0], x_sample.rearrange("b t d -> (b t) d"))
        k_rows = (k_prompt[0, 0].rearrange("t g d -> t (g d)"), k_sample[0].rearrange("b t g d -> (b t) (g d)"))
        v_rows = (v_prompt[0, 0].rearrange("t g d -> t (g d)"), v_sample[0].rearrange("b t g d -> (b t) (g d)"))
        ik_rows = (idx_k_prompt[0, 0], idx_k_sample[0].rearrange("b t d -> (b t) d"))
        y_rows = (y_prompt[0], y_sample.rearrange("b t d -> (b t) d"))
        h_dram = nc.dram_tensor("h_rows", (NTOK, D), F32, kind="Internal").ap()
        xn_dram = nc.dram_tensor("xn_rows", (NTOK, D), F32, kind="Internal").ap()
        w_dram = nc.dram_tensor("index_weights", (SR, NH), F32, kind="Internal").ap()
        slot_dram = nc.dram_tensor("slot_tokens", (NBLK * CAP + 1, 16), I32, kind="Internal").ap()
        eo_dram = nc.dram_tensor("expert_rows", (NBLK * CAP, D), F32, kind="Internal").ap()
        w_in_k = w_in[0].rearrange("(p c) n -> p c n", c=KC)
        gate_k = expert_w_gate[0].rearrange("e (p c) n -> e p c n", c=KC)
        up_k = expert_w_up[0].rearrange("e (p c) n -> e p c n", c=KC)
        down_k = expert_w_down[0].rearrange("e (c p) n -> e p c n", c=2)
        SPP = PAGE // SLOTS
        ci_rows = cache_idx_k[0].rearrange("n (c s) d -> (n c) (s d)", c=SPP)
        ck_rows = cache_k[0].rearrange("n (c s) g d -> (n c) (s g d)", c=SPP)
        cv_rows = cache_v[0].rearrange("n (c s) g d -> (n c) (s g d)", c=SPP)

        PART = {"T0": 0, "T1": 1, "U": 2, "Q": 3, "QI": 4, "KV": 5, "S0": 6, "S1": 7}
        order = [("T0", "state"), ("T0", ("x", 0)), ("T1", ("x", 0))]
        score_steps = {}
        m = 0
        for n in range(TILES + 1):
            if n < TILES:
                order += [(q, n) for q in ("U", "Q", "KV", "QI")]
            if n + 1 < TILES:
                order += [("T0", ("x", n + 1)), ("T1", ("x", n + 1))]
            if n:
                order += [("T0", ("q", n - 1)), ("T1", ("qi", n - 1)), ("T0", ("k", n - 1)), ("T1", ("pool", n - 1))]
                if n - 1 in (0, TILES - 1):
                    order += [("T0", ("u", n - 1))]
                i = ORDER[n - 1]
                score_steps[n - 1] = []
                if 2 <= i < NT:
                    for lo in range(0, P * (i + 1), 512):
                        for h in range(NH):
                            score_steps[n - 1].append((m, lo, min(512, P * (i + 1) - lo), h))
                            order += [(f"S{m % 2}", ("s", m))]
                            m += 1
        n_scores = m
        P2A = {"ACC": 0, "TR": 5, "PS0": 6, "PS1": 7}
        orderA = [("TR", (0, 0)), ("TR", (0, 1))]
        for b in range(SB):
            orderA += [(f"PS{(5 * b + q) % 2}", (b, q)) for q in range(5)]
            if b + 1 < SB:
                orderA += [("TR", (b + 1, 0)), ("TR", (b + 1, 1))]
        orderA += [("ACC", 0)]
        P2B = {"A0": 0, "A1": 2, "PT0": 4, "PT1": 5, "O": 6, "M": 7}

        def tail_tasks(i):
            return ([("OT", i)] if i < NT else []) + [("OP", i, 0), ("OP", i, 1), ("XR", i, 0), ("XR", i, 1), ("LG", i), ("RK", i)]

        def step(kind, idx):
            return [(kind,) + divmod(idx, NH)] if idx < NT * NH else []

        tasks = step("S", 0) + step("S", 1) + step("S", 2) + step("T", 0)
        for i in range(NT):
            rest = tail_tasks(i - 1) if i else []
            for h in range(NH):
                tasks += step("S", i * NH + h + 3)
                if h >= 1 and rest:
                    tasks.append(rest.pop(0))
                tasks += step("T", i * NH + h + 1) + [("V", i, h)]
            assert not rest
        tasks += tail_tasks(NT - 1)
        orderB = []
        npt = 0
        pt_use = {}
        for t in tasks + tail_tasks(NT):
            if t[0] == "S":
                orderB.append((f"A{t[2] % 2}", t))
            elif t[0] == "T":
                for c in range(0, t[1] + 1, 4):
                    pt_use[t + (c,)] = npt % 2
                    orderB.append((f"PT{npt % 2}", t + (c,)))
                    npt += 1
            elif t[0] == "V":
                if t[2] == 0:
                    orderB.append(("O", ("V", t[1])))
            else:
                orderB.append(("M", t))
        orderB.append(("M", "count"))
        P2C = {"SS": 0, "TK0": 5, "TK1": 6, "PV": 7}
        orderC = []
        ntk = 0
        tk_use = {}

        def tk(key):
            nonlocal ntk
            tk_use[key] = ntk % 2
            orderC.append((f"TK{ntk % 2}", key))
            ntk += 1

        def tks(kind, b):
            for c in range({"k": 4, "p": 3, "o": 1}[kind]):
                tk((kind, b, c))

        tks("k", 0)
        orderC.append(("SS", 0))
        tks("k", 1)
        for b in range(SB):
            if b + 1 < SB:
                orderC.append(("SS", b + 1))
            tks("p", b)
            if b:
                tks("o", b - 1)
            if b + 2 < SB:
                tks("k", b + 2)
            orderC.append(("PV", b))
        tks("o", SB - 1)

        filled, emptied, use = {}, {}, {}
        for tag, parts, seq in (("1", PART, order), ("2a", P2A, orderA), ("2b", P2B, orderB), ("2c", P2C, orderC)):
            for q in parts:
                filled[tag + q], emptied[tag + q] = sem(f"filled_{tag}_{q}"), sem(f"emptied_{tag}_{q}")
            seen = {}
            for q, key in seq:
                use[tag, q, key] = seen.get(q, 0)
                seen[q] = seen.get(q, 0) + 1
            use[tag] = seen

        def claim(pe, tag, q, key):
            if use[tag, q, key]:
                pe.wait_ge(emptied[tag + q], use[tag, q, key])

        def settle(pe, tag):
            for q, n in use[tag].items():
                pe.wait_ge(emptied[tag + q], n)

        def take(eng, tag, q, key):
            eng.wait_ge(filled[tag + q], use[tag, q, key] + 1)

        def copied(eng, tag, q, key):
            eng.wait_ge(emptied[tag + q], use[tag, q, key] + 1)

        consts_in = sem("consts_in")
        small_in = sem("small_in")
        w_in_in = [sem(f"w_in_in{c}") for c in range(4)]
        x_in = [sem(f"x_in{s}") for s in range(3)]
        state_in = sem("state_in")
        act_step, dve_step, pool_step = sem("act_step"), sem("dve_step"), sem("pool_step")
        init_done = sem("init_done")
        ssq_ready, std_ready, rstd_ready, xs_ready, xn_ready = sem("ssq_ready"), sem("std_ready"), sem("rstd_ready"), sem("xs_ready"), sem("xn_ready")
        z_ready, kv_out, d_ready, u_out, score_added = sem("z_ready"), sem("kv_out"), sem("d_ready"), sem("u_out"), sem("score_added")
        head_select_in = sem("head_select_in")
        phase1 = sem("phase1_done")
        state_out = sem("state_out")
        wscr_out, wsc_in, pt_in = sem("index_weights_out"), sem("index_weights_in"), sem("page_table_in")
        pidx_ready, WS_ready, QB_ready = sem("page_rows_ready"), sem("WS_ready"), sem("QB_ready")
        ki_in = [sem(f"ki_in{s}") for s in range(2)]
        sec_done, smask_ready = sem("weighted_done"), sem("smask_ready")
        phase2a = sem("phase2a_done")
        wout_in, rw_in, gb_in = sem("wout_in"), sem("router_in"), sem("ffn_norm_in")
        s_masked, s_exp, av_done = sem("scores_masked"), sem("probs_ready"), sem("values_summed")
        xr_in, h_out, x2_out = ([sem(f"{n}{s}") for s in range(2)] for n in ("residual_in", "h_out", "x2_out"))
        ssq2_ready, std2_ready, x2_ready, A_ready, ASUM_ready = (
            sem("ssq2_ready"), sem("std2_ready"), sem("x2_ready"), sem("A_ready"), sem("ASUM_ready"))
        logits_split, gexp_ready = sem("logits_split"), sem("gexp_ready")
        prompts_done = sem("prompt_tiles_done")
        K_in, V_in = [sem(f"K_in{s}") for s in range(2)], [sem(f"V_in{s}") for s in range(2)]
        masks_ready = sem("prompt_masks_ready")
        Vnew_in = sem("Vnew_in")
        smax_ready, sinv_ready = sem("smax_ready"), sem("sinv_ready")
        toki_ready, slots_cleared, dest_ready, slots_out, slots_in = (
            sem("toki_ready"), sem("slots_cleared"), sem("dest_ready"), sem("slots_out"), sem("slots_in"))
        first_ready, ov_slots = sem("first_slots_ready"), sem("overflow_slots")
        phase2 = sem("phase2_done")
        wgu_in, wdn_in, xg_in, eo_out = ([sem(f"{n}{s}") for s in range(2)] for n in ("wgu_in", "wdn_in", "xg_in", "eo_out"))
        xT_filled, xT_emptied = [sem(f"xT_filled{c}") for c in range(2)], [sem(f"xT_emptied{c}") for c in range(2)]
        gu_filled, hid_ready = sem("gate_up_filled"), sem("hidden_ready")
        silu_ready = sem("silu_ready")
        dn_filled, dn_emptied = [sem(f"down_filled{c}") for c in range(2)], [sem(f"down_emptied{c}") for c in range(2)]
        ov_w, ov_x, ov_pe, ov_act, ov_dve, ov_out = (sem(f"overflow_{n}") for n in ("weights_in", "rows_in", "pe", "act", "dve", "out"))
        experts_done = sem("experts_done")
        o_in, hc_in, y_ready, y_out = ([sem(f"{n}{s}") for s in range(2)] for n in ("o_in", "hc_in", "y_ready", "y_out"))
        ysum_ready, ssq3_ready, std3_ready = sem("ysum_ready"), sem("ssq3_ready"), sem("std3_ready")
        fin_norm_in = sem("fin_norm_in")

        block = ctx.enter_context(nc.Block())

        def tiles_out(eng, sems, n):
            for s in range(2):
                eng.wait_ge(sems[s], 16 * ((n + 1 - s) // 2))

        def rowsof_dram(ap, i):
            return ap[i * P:i * P + rows(i)]

        def dyn(ap, e):
            return ap[e] if isinstance(e, int) else ap[bass.ds(e, 1)].rearrange("a p c n -> (a p) c n")

        def block_rows(e):
            v = eo_dram.rearrange("(b p) n -> b p n", p=CAP)
            return v[e] if isinstance(e, int) else v[bass.ds(e, 1)].rearrange("a p n -> (a p) n")

        def store_y(eng, i):
            r, s = rows(i), i % 2
            eng.wait_ge(y_ready[s], i // 2 + 1)
            eng.dma_start(rowsof(y_rows, i), yc[0:r, s, :]).then_inc(y_out[s], 16)

        @block.sync
        def _(sp):
            sp.dma_start(con[:, :], const_table).then_inc(consts_in, 16)
            sp.dma_start(gb[:, :], norm_mix_g[0:1, :].partition_broadcast(P)).then_inc(consts_in, 16)
            sp.dma_start(sumA[0:SR, 0:SB * SR], head_select).then_inc(head_select_in, 16)
            sp.dma_start(stt_in[0:SB * HALO, :], state_pool[0].rearrange("b t c -> (b t) c")).then_inc(state_in, 16)
            for n in range(2):
                r = rows(ORDER[n])
                sp.dma_start(xb[0:r, n % 3, :], rowsof(x_rows, ORDER[n])).then_inc(x_in[n % 3], 16)
            for c in range(4):
                sp.dma_start(win[:, 2 * c:2 * c + 2, :], w_in_k[:, 2 * c:2 * c + 2, :]).then_inc(w_in_in[c], 16)
            sp.dma_start(pw[:, :, :], pool_w[0].rearrange("g c n -> c g n")).then_inc(small_in, 16)
            sp.dma_start(psc[:, :], pool_scale[0].rearrange("(g c) -> c g", g=4),
                         allow_slow_non_contiguous=True).then_inc(small_in, 16)
            for c in range(SPP):
                sp.dma_start(pt_i[c:P:SPP, :], page_table.rearrange("b j -> j b"),
                             allow_slow_non_contiguous=True).then_inc(pt_in, 16)
            sp.dma_start(pool_sample[0, :, 0:HALO - ST, :], state_pool[0, :, ST:HALO, :]).then_inc(state_out, 16)
            for n in range(2, TILES):
                if n >= 3:
                    take(sp, "1", "T1", ("x", n - 3))
                r = rows(ORDER[n])
                sp.dma_start(xb[0:r, n % 3, :], rowsof(x_rows, ORDER[n])).then_inc(x_in[n % 3], 16)
                if n == 2:
                    copied(sp, "1", "KV", 0)
                    sp.dma_start(w_dram, W[0:SR, NT, :]).then_inc(wscr_out, 16)
                    sp.wait_ge(wscr_out, 16)
                    for h in range(NH):
                        sp.dma_start(wsc[h * ST:(h + 1) * ST, :], w_dram.rearrange("(b t) h -> h t b", t=ST)[h],
                                     allow_slow_non_contiguous=True).then_inc(wsc_in, 16)
            sp.wait_ge(phase1, 4)
            sp.dma_start(wout[:, 0:4, :], w_out[0, 0:512, :].rearrange("(g c) n -> c g n", c=P)).then_inc(wout_in, 16)
            for g in range(NKV):
                src = w_out[0, 512 + 256 * g:512 + 256 * g + 256, :].rearrange("(h d) n -> d h n", d=HD)
                sp.dma_start(wout[HD * g:HD * g + HD, 4:8, :], src).then_inc(wout_in, 16)
            sp.dma_start(rw[:, :, 0:NG], router_group_w[0].rearrange("(c p) n -> p c n", p=P)).then_inc(rw_in, 16)
            sp.dma_start(rw[:, :, NG:36], router_expert_w[0].rearrange("(c p) n -> p c n", p=P)).then_inc(rw_in, 16)
            sp.dma_start(bias36[:, 0:NG], router_group_b[0:1, :].partition_broadcast(P)).then_inc(rw_in, 16)
            sp.dma_start(bias36[:, NG:36], router_expert_b[0:1, :].partition_broadcast(P)).then_inc(rw_in, 16)
            sp.dma_start(gb[:, :], norm_ffn_g[0:1, :].partition_broadcast(P)).then_inc(gb_in, 16)
            sp.wait_ge(kv_out, 48 * TILES)
            sp.dma_start(Vnew, v_sample[0].rearrange("b t g d -> t b (g d)")).then_inc(Vnew_in, 16)
            sp.wait_ge(phase2a, 3)

            def tail(i):
                s, r = i % 2, rows(i)
                copied(sp, "2b", "M", ("OP", i, 1))
                sp.dma_start(rowsof_dram(h_dram, i), hb[0:r, s, :]).then_inc(h_out[s], 16)
                sp.wait_ge(x2_ready, i + 1)
                sp.dma_start(rowsof_dram(xn_dram, i), x2[0:r, s, :]).then_inc(x2_out[s], 16)

            def residual(i):
                s, r = i % 2, rows(i)
                if 2 <= i:
                    sp.wait_ge(h_out[s], 16 * (i // 2))
                    sp.wait_ge(x2_ready, i - 1)
                sp.dma_start(hb[0:r, s, :], rowsof(x_rows, i)).then_inc(xr_in[s], 16)

            residual(0)
            residual(1)
            for i in range(NT):
                tail(i)
                if i + 2 < NT:
                    residual(i + 2)
            copied(sp, "2c", "PV", SB - 1)

            def weights(e, q, s):
                sp.dma_start(wgu[s][:, 0], dyn(gate_k, e)).then_inc(wgu_in[s], 16)
                sp.dma_start(wgu[s][:, 1], dyn(up_k, e)).then_inc(wgu_in[s], 16)
                sp.dma_start(wdn[s][:, :, :], dyn(down_k, e)).then_inc(wdn_in[s], 16)

            residual(NT)
            weights(0, 0, 0)
            weights(1, 0, 1)
            tail(NT)
            sp.wait_ge(phase2, 4)
            with sp.Fori(1, NE // 2) as q:
                for s in range(2):
                    sp.wait_ge(dn_filled[1], q * 2 + (s - 1))
                    weights(q * 2 + s, q, s)
            sp.wait_ge(dn_filled[1], NE)
            sp.wait_ge(dest_ready, 1)
            some = sp.value_load(ovb[0:1, OVB:OVB + 1], min_val=0, max_val=OVB)
            with sp.If(some > 0):
                with sp.Fori(0, OVB) as j:
                    sp.wait_ge(ov_pe, j * 3 + 3)
                    e = sp.value_load(ovb[0:1, bass.ds(j, 1)], min_val=0, max_val=NE - 1)
                    sp.dma_start(wgu[0][:, 0], dyn(gate_k, e)).then_inc(ov_w, 16)
                    sp.dma_start(wgu[0][:, 1], dyn(up_k, e)).then_inc(ov_w, 16)
                    sp.dma_start(wdn[0][:, :, :], dyn(down_k, e)).then_inc(ov_w, 16)
                sp.nop()
            with sp.Else():
                sp.nop()
            sp.wait_ge(experts_done, 4)
            tiles_out(sp, h_out, TILES)
            sp.dma_start(gb[:, :], final_norm_g.rearrange("(a n) -> a n", a=1).partition_broadcast(P)).then_inc(fin_norm_in, 16)
            for i in range(TILES):
                s, r = i % 2, rows(i)
                if i >= 2:
                    sp.wait_ge(ysum_ready, 2 * (i - 1))
                sp.dma_start(hc[0:r, s, :], rowsof_dram(h_dram, i)).then_inc(hc_in[s], 16)
                if i >= 1:
                    store_y(sp, i - 1)
            store_y(sp, TILES - 1)
            for s in range(2):
                sp.wait_ge(y_out[s], 16 * ((TILES + 1 - s) // 2))
            sp.wait_ge(state_out, 16)
            sp.wait_ge(u_out, 16 * (SB + 1))

        @block.gpsimd
        def _(pool):
            steps = [0]

            def link(ins):
                steps[0] += 1
                ins.then_inc(pool_step, 1)
                pool.wait_ge(pool_step, steps[0])

            pool.memset(u2[:, 0, :, 0:HALO], 0.0).then_inc(init_done, 1)
            pool.memset(WS[:, :, :], 0.0).then_inc(init_done, 1)
            pool.memset(QB[:, :, :, :, :], 0.0).then_inc(init_done, 1)
            pool.memset(mask[:, 0:3 * P], 0.0).then_inc(init_done, 1)
            pool.wait_ge(consts_in, 32)
            pool.wait_ge(init_done, 4)
            pool.wait_ge(head_select_in, 16)
            link(pool.tensor_copy(selb[0:SR].rearrange("p b r -> p (b r)"), sumA[0:SR, 0:SB * SR]))
            pool.tensor_copy(mask[:, 0:P], const("dmask")).then_inc(init_done, 1)
            pool.tensor_copy(mask[:, 2 * P:3 * P], const("dmask")).then_inc(init_done, 1)

            def norm_weight(n):
                r = rows(ORDER[n])
                pool.wait_ge(xs_ready, n + 1)
                pool.tensor_tensor(xb[0:r, n % 3, :], xb[0:r, n % 3, :], gb[0:r, :], ALU.mult).then_inc(xn_ready, 1)

            def rope(n):
                i = ORDER[n]
                r = rows(i)
                copied(pool, "1", "QI", n)
                z = Z[0:r, 0:19, :]
                c = cs("cos", i, r).unsqueeze(1).broadcast_to([r, 19, ROPE])
                s = cs("sin", i, r).unsqueeze(1).broadcast_to([r, 19, ROPE])
                hf = ROPE // 2
                link(pool.tensor_tensor(rt1[0:r], z[:, :, 0:ROPE], c, ALU.mult))
                link(pool.tensor_tensor(rt2[0:r, :, 0:hf], z[:, :, hf:ROPE], s[:, :, 0:hf], ALU.mult))
                link(pool.tensor_tensor(rt2[0:r, :, hf:ROPE], z[:, :, 0:hf], s[:, :, hf:ROPE], ALU.mult))
                link(pool.tensor_tensor(z[:, :, 0:ROPE], rt1[0:r], rt2[0:r], ALU.add))
                if i == NT:
                    link(pool.tensor_copy(Ztwice[0:r, :, 0, :], Z[0:r, 10:18, :]))
                    link(pool.tensor_copy(Ztwice[0:r, :, 1, :], Z[0:r, 10:18, :]))
                pool.tensor_copy(Z[0:r, 19, :], Z[0:r, 18, :]).then_inc(z_ready, 1)
                pool.dma_start(rowsof(k_rows, i), Z[0:r, 8:10, :].rearrange("p a d -> p (a d)")).then_inc(kv_out, 16)
                pool.dma_start(rowsof(ik_rows, i), Z[0:r, 18, :]).then_inc(kv_out, 16)
                pool.dma_start(rowsof(v_rows, i), V[0:r, i, :]).then_inc(kv_out, 16)

            def pooling(n):
                i = ORDER[n]
                copied(pool, "1", "U", n)
                if i == NT:
                    T = ST + HALO
                    u = uS
                    sa = sumA[:, :].rearrange("p (g b t) -> p g b t", g=4, b=SB)
                    sb_ = sumB[:, :].rearrange("p (g b t) -> p g b t", g=4, b=SB)
                    d = dT[:, 0:4 * SR].rearrange("p (g b t) -> p g b t", g=4, b=SB)
                else:
                    T = P + HALO
                    u = u2[:, i % 2]
                    sa = sumA[:, 0:4 * T].rearrange("p (g t) -> p g t", g=4)
                    sb_ = sumB[:, 0:4 * T].rearrange("p (g t) -> p g t", g=4)
                    d = dT[:, 0:4 * P].rearrange("p (g t) -> p g t", g=4)

                def cutv(v, g, a, b):
                    return v[:, g, :, a:b] if i == NT else v[:, g, a:b]

                g4 = slice(0, 4)
                link(pool.tensor_tensor(cutv(sa, g4, 1, T), cutv(u, g4, 1, T), cutv(u, g4, 0, T - 1), ALU.add))
                g3 = slice(1, 4)
                link(pool.tensor_tensor(cutv(sb_, g3, 3, T), cutv(sa, g3, 3, T), cutv(sa, g3, 1, T - 2), ALU.add))
                g2 = slice(2, 4)
                link(pool.tensor_tensor(cutv(sa, g2, 7, T), cutv(sb_, g2, 7, T), cutv(sb_, g2, 3, T - 4), ALU.add))
                link(pool.tensor_tensor(cutv(sb_, 3, 15, T), cutv(sa, 3, 15, T), cutv(sa, 3, 7, T - 8), ALU.add))
                if n:
                    take(pool, "1", "T1", ("pool", n - 1))
                for g, w in enumerate(WINDOWS):
                    src = (sa, sb_, sa, sb_)[g]
                    if i == NT:
                        link(pool.tensor_scalar(d[:, g], cutv(src, g, HALO, T), 1.0 / w, None, ALU.mult))
                    elif i:
                        link(pool.tensor_scalar(d[:, g, :], src[:, g, HALO:T], 1.0 / w, None, ALU.mult))
                    else:
                        lo = CC["pinv"][0] + 16 * g
                        pool.tensor_tensor(d[:, g, 0:16], src[:, g, HALO:HALO + 16], con[:, lo:lo + 16], ALU.mult)
                        link(pool.tensor_scalar(d[:, g, 16:P], src[:, g, HALO + 16:T], 1.0 / w, None, ALU.mult))
                pool.tensor_tensor(d, d, cutv(u, g4, HALO, T), ALU.subtract).then_inc(d_ready, 1)

            def index_keys(b):
                if b >= 2:
                    take(pool, "2a", "TR", (b - 2, 1))
                pool.indirect_dma_start(kin[:, b % 2].rearrange("p s d -> p (s d)"), None, ci_rows,
                                        bass.IndirectOffsetOnAxis(ap=pidx[:, b:b + 1], axis=0)).then_inc(ki_in[b % 2], 16)

            norm_weight(0)
            norm_weight(1)
            for n in range(TILES):
                rope(n)
                pooling(n)
                if n + 2 < TILES:
                    norm_weight(n + 2)
                if n == 0:
                    pool.wait_ge(pt_in, 16 * SPP)
                    pool.tensor_scalar(pidx, pt_i, float(SPP), const("pmod")[:, 0:1], ALU.mult, ALU.add).then_inc(pidx_ready, 1)
                if n == 4:
                    pool.wait_ge(pidx_ready, 1)
                    index_keys(0)
                    index_keys(1)
            pool.wait_ge(wsc_in, 16 * NH)
            for b in range(SB):
                link(pool.tensor_scalar(WS[0:SR, b, b * ST:(b + 1) * ST], const("diag", SR), wsc[:, b:b + 1], None, ALU.mult))
            for g in range(NKV):
                q0 = qT[HD * g:HD * (g + 1), :, SEQ:NTOK].rearrange("p h (b t) -> p b h t", b=SB)
                link(pool.tensor_copy(QB[HD * g:HD * (g + 1), :, g, :, :], q0))
            pool.wait_ge(kv_out, 48 * TILES)
            pool.drain().then_inc(phase1, 1)

            pool.wait_ge(phase1, 4)
            for b in range(2, SB):
                index_keys(b)
            zero = zslots[:, 0:NBLK * CAP // P * 16]
            link(pool.memset(zslots, 0))
            pool.dma_start(slot_dram[0:NBLK * CAP].rearrange("(p c) k -> p (c k)", p=P), zero).then_inc(slots_cleared, 16)
            per = OVB * CAP * D // (P * 512)
            pool.dma_start(eo_dram[NE * CAP:NBLK * CAP, :].rearrange("(p c) n -> p (c n)", p=P).rearrange("p (c n) -> p c n", c=per),
                           zslots.bitcast(F32)[:, 0:512].unsqueeze(1).broadcast_to([P, per, 512])).then_inc(slots_cleared, 16)
            pool.iota(toki[:, :, :], pattern=[[P, TILES], [0, 16]], base=0, channel_multiplier=1).then_inc(toki_ready, 1)
            pool.wait_ge(slots_cleared, 32)
            for s in range(2):
                pool.wait_ge(ki_in[s], 16 * SB // 2)
            pool.drain().then_inc(phase2a, 1)
            def past(buf, src, b, arrived):
                pool.indirect_dma_start(buf[b % 2].rearrange("p s d -> p (s d)"), None, src,
                                        bass.IndirectOffsetOnAxis(ap=pidx[:, b:b + 1], axis=0)).then_inc(arrived[b % 2], 16)

            def scatter(i):
                r = rows(i)
                pool.wait_ge(first_ready, i + 1)
                for k in range(2):
                    pool.indirect_dma_start(slot_dram, bass.IndirectOffsetOnAxis(ap=first[0:r, i, k:k + 1], axis=0),
                                            toki[0:r, i, :], None).then_inc(slots_out, 16)

            pool.wait_ge(masks_ready, 1)
            past(Kin, ck_rows, 0, K_in)
            past(Vin, cv_rows, 0, V_in)
            for i in range(NT):
                scatter(i)
            pool.wait_ge(prompts_done, 3)
            tiles_out(pool, h_out, NT)
            tiles_out(pool, x2_out, NT)
            past(Kin, ck_rows, 1, K_in)
            past(Vin, cv_rows, 1, V_in)
            for b in range(2, SB):
                take(pool, "2c", f"TK{tk_use['k', b - 2, 3]}", ("k", b - 2, 3))
                past(Kin, ck_rows, b, K_in)
                take(pool, "2c", "PV", b - 2)
                past(Vin, cv_rows, b, V_in)
            scatter(NT)
            pool.wait_ge(slots_out, 16 * 2 * TILES)
            pool.dma_start(slot_tok[0:CAP, 0:NE].bitcast(I32), slot_dram[0:NE * CAP, 0:1].rearrange("(c p) k -> p (c k)", p=CAP),
                           allow_slow_non_contiguous=True).then_inc(slots_in, 16)
            pool.wait_ge(slots_in, 16)
            tiles_out(pool, x2_out, TILES)
            pool.drain().then_inc(phase2, 1)
            pool.wait_ge(phase2, 4)

            for e in range(NE):
                s = e % 2
                if e >= 2:
                    pool.wait_ge(xT_filled[1], e - 1)
                pool.indirect_dma_start(xg[0:CAP, s, :], None, xn_dram,
                                        bass.IndirectOffsetOnAxis(ap=slot_tok[0:CAP, e:e + 1], axis=0)).then_inc(xg_in[s], 16)
            pool.wait_ge(dn_filled[1], NE)
            pool.wait_ge(dest_ready, 1)
            some = pool.value_load(ovb[0:1, OVB:OVB + 1], min_val=0, max_val=OVB)
            with pool.If(some > 0):
                for i in range(TILES):
                    r = rows(i)
                    for k in range(2):
                        pool.indirect_dma_start(slot_dram, bass.IndirectOffsetOnAxis(ap=dest[0:r, i, k:k + 1], axis=0),
                                                toki[0:r, i, :], None).then_inc(ov_slots, 16)
                pool.wait_ge(ov_slots, 16 * 2 * TILES)
                pool.dma_start(slot_tok[0:CAP, NE:NBLK].bitcast(I32),
                               slot_dram[NE * CAP:NBLK * CAP, 0:1].rearrange("(c p) k -> p (c k)", p=CAP),
                               allow_slow_non_contiguous=True).then_inc(ov_slots, 16)
                pool.wait_ge(ov_slots, 16 * 2 * TILES + 16)
                for j in range(OVB):
                    if j:
                        pool.wait_ge(ov_pe, 3 * j + 3)
                    pool.indirect_dma_start(xg[0:CAP, 0, :], None, xn_dram,
                                            bass.IndirectOffsetOnAxis(ap=slot_tok[0:CAP, NE + j:NE + j + 1], axis=0)).then_inc(ov_x, 16)
                pool.nop()
            with pool.Else():
                pool.nop()
            pool.drain().then_inc(experts_done, 1)
            pool.wait_ge(experts_done, 4)
            for i in range(TILES):
                s, r = i % 2, rows(i)
                if i >= 2:
                    pool.wait_ge(ysum_ready, 2 * (i - 1))
                for k, o in ((0, o1), (1, o2)):
                    pool.indirect_dma_start(o[0:r, s, :], None, eo_dram,
                                            bass.IndirectOffsetOnAxis(ap=dest[0:r, i, k:k + 1], axis=0)).then_inc(o_in[s], 16)

        @block.tensor
        def _(pe):
            mm = nc.tensor.matmul
            tr = nc.tensor.transpose

            def x_turn(n):
                r = rows(ORDER[n])
                pe.wait_ge(xn_ready, n + 1)
                for c in range(2):
                    claim(pe, "1", f"T{c}", ("x", n))
                    for j in range(4):
                        ins = tr(ps[:, c, j * P:j * P + r], xb[0:r, n % 3, 4 * c + j:D:KC], ident(r))
                    ins.then_inc(filled[f"1T{c}"], 1)

            def project(n):
                i = ORDER[n]
                r = rows(i)
                s = n % 2
                for c in range(2):
                    copied(pe, "1", f"T{c}", ("x", n))
                claim(pe, "1", "U", n)
                for g in range(4):
                    for k in range(KC):
                        if n == 0 and g == 0 and k % 2 == 0:
                            pe.wait_ge(w_in_in[k // 2], 16)
                        ins = mm(ps[:, PART["U"], g * r:(g + 1) * r], win[:, k, g * P:(g + 1) * P], xnT[:, s, k, 0:r],
                                 start=(k == 0), stop=(k == KC - 1))
                ins.then_inc(filled["1U"], 1)
                for part, spans in (("Q", ((CQ, CK, 0),)), ("KV", ((CK, CQI, 0), (CKI, NIN, CQI - CK))), ("QI", ((CQI, CKI, 0),))):
                    claim(pe, "1", part, n)
                    for a, b, o in spans:
                        for k in range(KC):
                            ins = mm(ps[0:r, PART[part], o:o + b - a], xnT[:, s, k, 0:r], win[:, k, a:b],
                                     start=(k == 0), stop=(k == KC - 1))
                    ins.then_inc(filled["1" + part], 1)

            def z_turn(n):
                i = ORDER[n]
                r = rows(i)
                pe.wait_ge(z_ready, n + 1)
                claim(pe, "1", "T0", ("q", n))
                for c in range(4):
                    ins = tr(ps[:, 0, c * r:(c + 1) * r], Z[0:r, 2 * c:2 * c + 2, :].rearrange("p a d -> p (a d)"), ident(r))
                ins.then_inc(filled["1T0"], 1)
                claim(pe, "1", "T1", ("qi", n))
                if i == NT:
                    for h in range(NH):
                        ins = tr(ps[:, 1, h * r:(h + 1) * r], Ztwice[0:r, h].rearrange("p a d -> p (a d)"), ident(r))
                else:
                    for c in range(4):
                        ins = tr(ps[:, 1, c * r:(c + 1) * r], Z[0:r, 10 + 2 * c:12 + 2 * c, :].rearrange("p a d -> p (a d)"), ident(r))
                ins.then_inc(filled["1T1"], 1)
                claim(pe, "1", "T0", ("k", n))
                for c, z0 in ((0, 8), (1, 18)):
                    ins = tr(ps[:, 0, c * r:(c + 1) * r], Z[0:r, z0:z0 + 2, :].rearrange("p a d -> p (a d)"), ident(r))
                ins.then_inc(filled["1T0"], 1)

            def pool_out(n):
                r = rows(ORDER[n])
                if n == 0:
                    pe.wait_ge(small_in, 32)
                pe.wait_ge(d_ready, n + 1)
                claim(pe, "1", "T1", ("pool", n))
                for g in range(4):
                    ins = mm(ps[:, 1, g * r:(g + 1) * r], pw[:, g, :], dT[:, g * r:(g + 1) * r], start=True, stop=True)
                ins.then_inc(filled["1T1"], 1)

            def u_turn(n):
                claim(pe, "1", "T0", ("u", n))
                for g in range(4):
                    if ORDER[n] == NT:
                        ins = tr(ps[0:SR, 0, g * P:(g + 1) * P], uC[:, g, :], ident(P))
                    else:
                        ins = tr(ps[0:HALO, 0, g * P:(g + 1) * P], u2[:, ORDER[n] % 2, g, P:P + HALO], ident(P))
                ins.then_inc(filled["1T0"], 1)

            def scores(n):
                i = ORDER[n]
                copied(pe, "1", "T1", ("qi", n))
                copied(pe, "1", "T0", ("k", n))
                for m, lo, w, h in score_steps[n]:
                    hf = HD * (h % 2)
                    claim(pe, "1", f"S{m % 2}", ("s", m))
                    mm(ps[:, 6 + m % 2, 0:w], qiT[hf:hf + HD, i % 2, h // 2, :], kiT[hf:hf + HD, lo:lo + w],
                       start=True, stop=True).then_inc(filled[f"1S{m % 2}"], 1)

            pe.wait_ge(consts_in, 32)
            pe.wait_ge(state_in, 16)
            claim(pe, "1", "T0", "state")
            for g in range(4):
                ins = tr(ps[:, 0, g * SB * HALO:(g + 1) * SB * HALO], stt_in[0:SB * HALO, g * P:(g + 1) * P], ident(SB * HALO))
            ins.then_inc(filled["1T0"], 1)
            x_turn(0)
            for n in range(TILES + 1):
                if n < TILES:
                    project(n)
                if n + 1 < TILES:
                    x_turn(n + 1)
                if n:
                    z_turn(n - 1)
                    pool_out(n - 1)
                    if n - 1 in (0, TILES - 1):
                        u_turn(n - 1)
                    if score_steps[n - 1]:
                        scores(n - 1)
            settle(pe, "1")
            pe.drain().then_inc(phase1, 1)
            pe.wait_ge(phase1, 4)


            def ki_turn(b):
                pe.wait_ge(ki_in[b % 2], 16 * (b // 2 + 1))
                for c in range(2):
                    claim(pe, "2a", "TR", (b, c))
                    for j in range(4):
                        a = 2 * (4 * c + j)
                        ins = tr(ps[:, 5, j * P:(j + 1) * P], kin[:, b % 2, a:a + 2, :].rearrange("p s d -> p (s d)"), ident(P))
                    ins.then_inc(filled["2aTR"], 1)

            def s_scores(b):
                copied(pe, "2a", "TR", (b, 1))
                for q in range(5):
                    part = (5 * b + q) % 2
                    claim(pe, "2a", f"PS{part}", (b, q))
                    if q < 4:
                        c, sp_ = q // 2, q % 2
                        hf = HD * sp_
                        mm(ps[0:SR, 6 + part, :], QS[hf:hf + HD, b].rearrange("p h t -> p (h t)"),
                           kiTs[hf:hf + HD, b % 2, 4 * c:4 * c + 4, :].rearrange("p j k -> p (j k)"),
                           start=True, stop=True).then_inc(filled[f"2aPS{part}"], 1)
                    else:
                        mm(ps[0:SR, 6 + part, 0:ST], QS[0:HD, b].rearrange("p h t -> p (h t)"),
                           kiT[0:HD, SEQ + b * ST:SEQ + (b + 1) * ST], start=True, stop=True).then_inc(filled[f"2aPS{part}"], 1)

            def weighted(b):
                for q in range(5):
                    copied(pe, "2a", f"PS{(5 * b + q) % 2}", (b, q))
                for q in range(5):
                    w = 512 if q < 4 else ST
                    ins = mm(ps[0:SR, q, 0:w], WS[0:SR, b, :], rs[0:SR, b % 2, 512 * q:512 * q + w],
                             start=(b == 0), stop=(b == SB - 1))
                ins.then_inc(sec_done, 1)
                if b == SB - 1:
                    pe.wait_ge(sec_done, SB)
                    pe.nop().then_inc(filled["2aACC"], 1)

            ki_turn(0)
            for b in range(SB):
                s_scores(b)
                if b + 1 < SB:
                    ki_turn(b + 1)
                if b:
                    weighted(b - 1)
            weighted(SB - 1)
            settle(pe, "2a")
            pe.drain().then_inc(phase2a, 1)
            pe.wait_ge(phase2a, 3)

            def q_k(i, h):
                part = h % 2
                g, w = h // GH, P * (i + 1)
                claim(pe, "2b", f"A{part}", ("S", i, h))
                for lo in range(0, w, 512):
                    e = min(512, w - lo)
                    ins = mm(ps[:, 2 * part + lo // 512, 0:e], qT[HD * g:HD * (g + 1), h % GH, i * P:(i + 1) * P],
                             kT[HD * g:HD * (g + 1), lo:lo + e], start=True, stop=True)
                ins.then_inc(filled[f"2bA{part}"], 1)

            def p_turn(i, h):
                pe.wait_ge(s_exp, i * NH + h + 1)
                for c in range(0, i + 1, 4):
                    part = pt_use["T", i, h, c]
                    claim(pe, "2b", f"PT{part}", ("T", i, h, c))
                    for j in range(c, min(c + 4, i + 1)):
                        ins = tr(ps[:, 4 + part, (j - c) * P:(j - c + 1) * P], Sm[:, (i * NH + h) % 3, j * P:(j + 1) * P], ident(P))
                    ins.then_inc(filled[f"2bPT{part}"], 1)

            def p_v(i, h):
                if h == 0:
                    claim(pe, "2b", "O", ("V", i))
                g = h // GH
                for c in range(0, i + 1, 4):
                    copied(pe, "2b", f"PT{pt_use['T', i, h, c]}", ("T", i, h, c))
                for j in range(i + 1):
                    ins = mm(ps[:, 6, h * HD:(h + 1) * HD], PT[:, h % 2, j, :], V[:, j, g * HD:(g + 1) * HD],
                             start=(j == 0), stop=(j == i))
                ins.then_inc(av_done, 1)
                if h == NH - 1:
                    pe.wait_ge(av_done, (i + 1) * NH)
                    pe.nop().then_inc(filled["2bO"], 1)

            def tail(t):
                kind, i = t[0], t[1]
                r = rows(i)
                tok = slice(i * P, i * P + r)
                claim(pe, "2b", "M", t)
                if kind == "OT":
                    copied(pe, "2b", "O", ("V", i))
                    for c in range(4):
                        ins = tr(ps[:, 7, c * P:(c + 1) * P], Osb[:, c * P:(c + 1) * P], ident(P))
                elif kind == "OP":
                    if t[2] == 0:
                        if i < NT:
                            copied(pe, "2b", "M", ("OT", i))
                        if i == 0:
                            pe.wait_ge(wout_in, 48)
                    for k in range(8):
                        if k < 4:
                            lhs = mixP[:, k, tok]
                        else:
                            lhs = mixS[:, k - 4, :] if i == NT else mixA[:, k - 4, :]
                        ins = mm(ps[0:r, 7, :], lhs, wout[:, k, 512 * t[2]:512 * t[2] + 512], start=(k == 0), stop=(k == 7))
                elif kind == "XR":
                    pe.wait_ge(x2_ready, i + 1)
                    for j in range(4):
                        c = 4 * t[2] + j
                        ins = tr(ps[:, 7, j * r:(j + 1) * r], x2[0:r, i % 2, c * P:(c + 1) * P], ident(r))
                elif kind == "LG":
                    copied(pe, "2b", "M", ("XR", i, 1))
                    if i == 0:
                        pe.wait_ge(rw_in, 64)
                    for k in range(KC):
                        ins = mm(ps[0:r, 7, 0:36], x2T[:, k, 0:r], rw[:, k, :], start=(k == 0), stop=(k == KC - 1))
                elif kind == "RK":
                    pe.wait_ge(A_ready, i + 1)
                    mm(ps[0:r, 7, 0:NE], const("tri")[0:r, 0:r], A[0:r, :], start=True, stop=False)
                    ins = mm(ps[0:r, 7, 0:NE], const("ones")[:, 0:r], ASUM[:, :], start=False, stop=True)
                ins.then_inc(filled["2bM"], 1)

            for t in tasks:
                if t[0] == "S":
                    q_k(t[1], t[2])
                elif t[0] == "T":
                    p_turn(t[1], t[2])
                elif t[0] == "V":
                    p_v(t[1], t[2])
                else:
                    tail(t)
            for q in ("A0", "A1", "PT0", "PT1", "O"):
                pe.wait_ge(emptied["2b" + q], use["2b"][q])
            pe.wait_ge(emptied["2bM"], use["2b", "M", ("OP", NT, 0)])
            pe.drain().then_inc(prompts_done, 1)
            pe.wait_ge(prompts_done, 3)

            pe.wait_ge(smask_ready, 1)
            pe.wait_ge(Vnew_in, 16)

            def keys(b):
                s = b % 2
                pe.wait_ge(K_in[s], 16 * (b // 2 + 1))
                for c in range(4):
                    part = tk_use["k", b, c]
                    claim(pe, "2c", f"TK{part}", ("k", b, c))
                    for j in range(4):
                        ins = tr(ps[:, 5 + part, j * P:(j + 1) * P], Kin[s][:, 4 * c + j, :], ident(P))
                    ins.then_inc(filled[f"2cTK{part}"], 1)

            def scores_of(b):
                claim(pe, "2c", "SS", b)
                smv = smask[0:SR, 0:PAST].rearrange("r (p s) -> r s p", s=SLOTS)
                lhs = QB[:, b].rearrange("p g h t -> p (g h t)")
                for q in range(5):
                    c = min(q, 3)
                    copied(pe, "2c", f"TK{tk_use['k', b, c]}", ("k", b, c))
                    if q < 4:
                        mm(ps[0:SR, q, :], lhs, KTs[:, 512 * q:512 * (q + 1)], start=True, stop=False)
                        mm(ps[0:SR, q, :], selb[0:SR, b, :], smv[:, 4 * q:4 * q + 4, :], start=False, stop=True)
                    else:
                        mm(ps[0:SR, 4, 0:ST], lhs, kT[:, SEQ + b * ST:SEQ + (b + 1) * ST], start=True, stop=False)
                        ins = mm(ps[0:SR, 4, 0:ST], selb[0:SR, b, :], smask[0:SR, PAST:LS], start=False, stop=True)
                ins.then_inc(filled["2cSS"], 1)

            def probs_turn(b):
                copied(pe, "2c", "SS", b)
                for c in range(3):
                    part = tk_use["p", b, c]
                    claim(pe, "2c", f"TK{part}", ("p", b, c))
                    if c < 2:
                        for j in range(8):
                            a = 8 * c + j
                            ins = tr(ps[:, 5 + part, j * SR:(j + 1) * SR], Ps[0:SR, a * P:(a + 1) * P], ident(SR))
                    else:
                        ins = tr(ps[0:ST, 5 + part, 0:SR], Ps[0:SR, PAST:LS], ident(SR))
                    ins.then_inc(filled[f"2cTK{part}"], 1)

            def values(b):
                claim(pe, "2c", "PV", b)
                pe.wait_ge(V_in[b % 2], 16 * (b // 2 + 1))
                for c in range(3):
                    copied(pe, "2c", f"TK{tk_use['p', b, c]}", ("p", b, c))
                for a in range(SLOTS):
                    mm(ps[0:SR, 7, 0:P], PTs[:, a, :], Vin[b % 2][:, a, :], start=(a == 0), stop=False)
                mm(ps[0:SR, 7, 0:P], PTs[0:ST, SLOTS, :], Vnew[:, b, :], start=False, stop=True).then_inc(filled["2cPV"], 1)

            def out_turn(b):
                part = tk_use["o", b, 0]
                copied(pe, "2c", "PV", b)
                claim(pe, "2c", f"TK{part}", ("o", b, 0))
                tr(ps[:, 5 + part, 0:SR], Os[0:SR, :], ident(SR)).then_inc(filled[f"2cTK{part}"], 1)

            keys(0)
            scores_of(0)
            keys(1)
            for b in range(SB):
                if b + 1 < SB:
                    scores_of(b + 1)
                probs_turn(b)
                if b:
                    out_turn(b - 1)
                if b + 2 < SB:
                    keys(b + 2)
                values(b)
            out_turn(SB - 1)
            settle(pe, "2c")
            for t in tail_tasks(NT):
                tail(t)
            claim(pe, "2b", "M", "count")
            pe.wait_ge(ASUM_ready, TILES)
            mm(ps[:, 7, 0:NE], const("ones"), ASUM[:, :], start=True, stop=True).then_inc(filled["2bM"], 1)
            settle(pe, "2b")
            pe.drain().then_inc(phase2, 1)
            pe.wait_ge(phase2, 4)

            def turn_rows(s, c):
                for j in range(4):
                    ins = tr(ps[:, c, j * CAP:(j + 1) * CAP], xg[0:CAP, s, 4 * c + j:D:KC], ident(CAP))
                return ins

            def products(s):
                for j in range(4):
                    for k in range(KC):
                        ins = mm(ps[:, 2 + s, j * CAP:(j + 1) * CAP], wgu[s][:, j // 2, k, (j % 2) * P:(j % 2 + 1) * P],
                                 xgT[:, s, k, :], start=(k == 0), stop=(k == KC - 1))
                return ins

            def down_half(s, c):
                for k in range(2):
                    ins = mm(ps[0:CAP, 5 + c, :], hT[:, s, k, :], wdn[s][:, k, 512 * c:512 * (c + 1)], start=(k == 0), stop=(k == 1))
                return ins

            def rows_turn(e, q, s, first):
                pe.wait_ge(xg_in[s], q * 16 + 16)
                for c in range(2):
                    if not first:
                        pe.wait_ge(xT_emptied[c], e)
                    turn_rows(s, c).then_inc(xT_filled[c], 1)

            def gate_up(e, q, s, first):
                pe.wait_ge(wgu_in[s], q * 32 + 32)
                for c in range(2):
                    pe.wait_ge(xT_emptied[c], e + 1)
                if not first:
                    pe.wait_ge(hid_ready, e - 1)
                products(s).then_inc(gu_filled, 1)

            def down(e, q, s, first):
                pe.wait_ge(hid_ready, e + 1)
                pe.wait_ge(wdn_in[s], q * 16 + 16)
                for c in range(2):
                    if not first:
                        pe.wait_ge(dn_emptied[c], e)
                    down_half(s, c).then_inc(dn_filled[c], 1)

            rows_turn(0, 0, 0, True)
            gate_up(0, 0, 0, True)
            rows_turn(1, 0, 1, False)
            down(0, 0, 0, True)
            gate_up(1, 0, 1, True)
            rows_turn(2, 1, 0, False)
            down(1, 0, 1, False)
            with pe.Fori(1, NE // 2 - 1) as q:
                gate_up(q * 2, q, 0, False)
                rows_turn(q * 2 + 1, q, 1, False)
                down(q * 2, q, 0, False)
                gate_up(q * 2 + 1, q, 1, False)
                rows_turn(q * 2 + 2, q + 1, 0, False)
                down(q * 2 + 1, q, 1, False)
            gate_up(NE - 2, NE // 2 - 1, 0, False)
            rows_turn(NE - 1, NE // 2 - 1, 1, False)
            down(NE - 2, NE // 2 - 1, 0, False)
            gate_up(NE - 1, NE // 2 - 1, 1, False)
            down(NE - 1, NE // 2 - 1, 1, False)

            pe.wait_ge(dn_emptied[0], NE)
            pe.wait_ge(dn_emptied[1], NE)
            some = pe.value_load(ovb[0:1, OVB:OVB + 1], min_val=0, max_val=OVB)
            with pe.If(some > 0):
                pe.nop().then_inc(ov_pe, 3)
                with pe.Fori(0, OVB) as j:
                    pe.wait_ge(ov_x, j * 16 + 16)
                    pe.wait_ge(ov_dve, j * 3 + 3)
                    turn_rows(0, 0)
                    turn_rows(0, 1).then_inc(ov_pe, 1)
                    pe.wait_ge(ov_w, j * 48 + 48)
                    pe.wait_ge(ov_dve, j * 3 + 4)
                    products(0).then_inc(ov_pe, 1)
                    pe.wait_ge(ov_dve, j * 3 + 5)
                    down_half(0, 0)
                    down_half(0, 1).then_inc(ov_pe, 1)
                pe.nop()
            with pe.Else():
                pe.nop()
            pe.drain().then_inc(experts_done, 1)

        @block.scalar
        def _(act):
            fn = nc.scalar.activation

            def copy(out, in_, scale=1.0):
                return fn(out, in_, ACT.Copy, scale=scale)

            def four(v, r):
                return v[:, 0:4 * r].rearrange("p (g t) -> p g t", g=4)

            def root(n):
                r = rows(ORDER[n])
                act.wait_ge(ssq_ready, n + 1)
                fn(std[0:r, n:n + 1], ssq[0:r, n:n + 1], ACT.Sqrt, scale=1.0 / D, bias=const("eps", r)).then_inc(std_ready, 1)

            def scale_rows(n):
                r = rows(ORDER[n])
                act.wait_ge(rstd_ready, n + 1)
                copy(xb[0:r, n % 3, :], xb[0:r, n % 3, :], scale=rstd[0:r, n:n + 1]).then_inc(xs_ready, 1)

            def keep_xT(n):
                r = rows(ORDER[n])
                for c in range(2):
                    take(act, "1", f"T{c}", ("x", n))
                    copy(xnT[:, n % 2, 4 * c:4 * c + 4, 0:r], ps[:, c, :].rearrange("p (g t) -> p g t", g=4)[:, :, 0:r])\
                        .then_inc(emptied[f"1T{c}"], 1)

            def keep_rows(n):
                i = ORDER[n]
                r = rows(i)
                take(act, "1", "U", n)
                if n >= 2:
                    act.wait_ge(d_ready, n - 1)
                u = four(ps[:, PART["U"], :], r)
                if i == NT:
                    copy(uC, u)
                    copy(uS[:, :, :, HALO:HALO + ST], u.rearrange("p g (b t) -> p g b t", b=SB)).then_inc(emptied["1U"], 1)
                else:
                    if i:
                        act.wait_ge(emptied["1U"], n)
                        copy(u2[:, i % 2, :, 0:HALO], u2[:, (i - 1) % 2, :, P:P + HALO])
                    else:
                        act.wait_ge(init_done, 4)
                    copy(u2[:, i % 2, :, HALO:HALO + P], u).then_inc(emptied["1U"], 1)
                if n:
                    act.wait_ge(kv_out, 48 * n)
                    take(act, "1", "T0", ("k", n - 1))
                take(act, "1", "Q", n)
                copy(Z[0:r, 0:8, :].rearrange("p (b g) d -> p g b d", g=NKV),
                     ps[0:r, PART["Q"], :].rearrange("p (g b d) -> p g b d", g=NKV, b=GH)).then_inc(emptied["1Q"], 1)
                take(act, "1", "KV", n)
                kv = ps[0:r, PART["KV"], :]
                copy(Z[0:r, 8:10, :].rearrange("p a d -> p (a d)"), kv[:, 0:P])
                copy(V[0:r, i, :], kv[:, P:2 * P])
                copy(Z[0:r, 18, :], kv[:, 2 * P:2 * P + HD])
                copy(W[0:r, i, :], kv[:, 2 * P + HD:2 * P + HD + NH], scale=(NH ** -0.5) * (HD ** -0.5)).then_inc(emptied["1KV"], 1)
                take(act, "1", "QI", n)
                copy(Z[0:r, 10:18, :].rearrange("p a d -> p (a d)"), ps[0:r, PART["QI"], :]).then_inc(emptied["1QI"], 1)

            def keep_z(n):
                i = ORDER[n]
                r = rows(i)
                tok = slice(i * P, i * P + r)
                take(act, "1", "T0", ("q", n))
                copy(qT[:, :, tok], four(ps[:, 0, :], r)).then_inc(emptied["1T0"], 1)
                take(act, "1", "T1", ("qi", n))
                if i == NT:
                    copy(QS[:, :, :, :].rearrange("p b h t -> p h b t"), ps[:, 1, :].rearrange("p (h b t) -> p h b t", h=NH, b=SB)).then_inc(emptied["1T1"], 1)
                else:
                    copy(qiT[:, i % 2], four(ps[:, 1, :], r)).then_inc(emptied["1T1"], 1)
                take(act, "1", "T0", ("k", n))
                copy(kT[:, tok], ps[:, 0, 0:r])
                copy(kiT[:, tok], ps[:, 0, r:2 * r]).then_inc(emptied["1T0"], 1)
                take(act, "1", "T1", ("pool", n))
                for g in range(4):
                    ins = copy(mixP[:, g, tok], ps[:, 1, g * r:(g + 1) * r], scale=psc[:, g:g + 1])
                ins.then_inc(emptied["1T1"], 1)
                if n == 0:
                    take(act, "1", "T0", ("u", n))
                    copy(stt_in[0:SR, :], ps[0:SR, 0, :]).then_inc(emptied["1T0"], 1)
                    copied(act, "1", "T0", ("u", n))
                    for b in range(SB):
                        act.dma_start(pool_sample[0, b, HALO - ST:HALO, :], stt_in[b * ST:(b + 1) * ST, :]).then_inc(u_out, 16)
                if n == TILES - 1:
                    take(act, "1", "T0", ("u", n))
                    act.wait_ge(u_out, 16 * SB)
                    copy(stt_in[0:HALO, :], ps[0:HALO, 0, :]).then_inc(emptied["1T0"], 1)
                    copied(act, "1", "T0", ("u", n))
                    act.dma_start(pool_prompt[0, 0], stt_in[0:HALO, :]).then_inc(u_out, 16)
                    act.wait_ge(u_out, 16 * (SB + 1))

            def relus(n):
                for m, lo, w, h in score_steps[n]:
                    take(act, "1", f"S{m % 2}", ("s", m))
                    if m >= 2:
                        act.wait_ge(score_added, m - 1)
                    fn(rl[:, m % 2, 0:w], ps[:, 6 + m % 2, 0:w], ACT.Relu).then_inc(emptied[f"1S{m % 2}"], 1)

            act.wait_ge(consts_in, 32)
            act.wait_ge(small_in, 32)
            take(act, "1", "T0", "state")
            copy(uS[:, :, :, 0:HALO], ps[:, 0, 0:4 * SB * HALO].rearrange("p (g b t) -> p g b t", g=4, b=SB))\
                .then_inc(emptied["1T0"], 1)
            for n in range(2):
                root(n)
                scale_rows(n)
            keep_xT(0)
            for n in range(TILES + 1):
                if n + 2 < TILES:
                    root(n + 2)
                if n + 1 < TILES:
                    keep_xT(n + 1)
                if n + 2 < TILES:
                    scale_rows(n + 2)
                if n:
                    keep_z(n - 1)
                if n < TILES:
                    keep_rows(n)
                if n:
                    relus(n - 1)
            act.drain().then_inc(phase1, 1)
            act.wait_ge(phase1, 4)

            def keep_ki(b):
                for c in range(2):
                    take(act, "2a", "TR", (b, c))
                    copy(kiTs[:, b % 2, 4 * c:4 * c + 4, :], four(ps[:, 5, :], P)).then_inc(emptied["2aTR"], 1)

            keep_ki(0)
            for b in range(SB):
                for q in range(5):
                    part, w = (5 * b + q) % 2, 512 if q < 4 else ST
                    take(act, "2a", f"PS{part}", (b, q))
                    if b >= 2 and q == 0:
                        act.wait_ge(sec_done, b - 1)
                    fn(rs[0:SR, b % 2, 512 * q:512 * q + w], ps[0:SR, 6 + part, 0:w], ACT.Relu).then_inc(emptied[f"2aPS{part}"], 1)
                if b + 1 < SB:
                    keep_ki(b + 1)
            take(act, "2a", "ACC", 0)
            inorder = SCs[0:SR, 0:PAST].rearrange("r (p s) -> r s p", s=SLOTS)
            for q in range(4):
                a = 8 * (q // 2) + q % 2
                copy(inorder[:, a:a + 7:2, :], ps[0:SR, q, :].rearrange("r (s p) -> r s p", s=4))
            copy(SCs[0:SR, PAST:LS], ps[0:SR, 4, 0:ST]).then_inc(emptied["2aACC"], 1)
            act.drain().then_inc(phase2a, 1)
            act.wait_ge(phase2a, 3)

            def tail(t):
                kind, i = t[0], t[1]
                r, s = rows(i), i % 2
                if kind == "OT":
                    take(act, "2b", "M", t)
                    copy(mixA[:, :, :], four(ps[:, 7, :], P)).then_inc(emptied["2bM"], 1)
                elif kind == "OP" and t[2] == 1:
                    copied(act, "2b", "M", t)
                    if i >= 2:
                        act.wait_ge(x2_out[s], 16 * (i // 2))
                        take(act, "2b", "M", ("XR", i - 2, 1))
                    fn(x2[0:r, s, :], hb[0:r, s, :], ACT.Square, accum_out=ssq2[0:r, i:i + 1]).then_inc(ssq2_ready, 1)
                    act.wait_ge(ssq2_ready, i + 1)
                    fn(std2[0:r, i:i + 1], ssq2[0:r, i:i + 1], ACT.Sqrt, scale=1.0 / D, bias=const("eps", r)).then_inc(std2_ready, 1)
                elif kind == "XR":
                    take(act, "2b", "M", t)
                    copy(x2T[:, 4 * t[2]:4 * t[2] + 4, 0:r], four(ps[:, 7, :], r)).then_inc(emptied["2bM"], 1)
                elif kind == "LG":
                    act.wait_ge(logits_split, i + 1)
                    fn(gexp[0:r, :], G8[0:r, 0:NG], ACT.Exp, bias=r1[0:r, 0:1], accum_out=r1[0:r, 2:3])
                    fn(r1[0:r, 3:4], r1[0:r, 1:2], ACT.Exp).then_inc(gexp_ready, 1)

            for t in tasks:
                kind, i = t[0], t[1]
                if kind == "S":
                    h, w = t[2], P * (i + 1)
                    probs = Sm[:, (i * NH + h) % 3, 0:w]
                    act.wait_ge(s_masked, i * NH + h + 1)
                    fn(probs, probs, ACT.Exp, bias=nb[:, h:h + 1], scale=SCALE,
                       accum_out=esum[:, 8 * (i % 2) + h:8 * (i % 2) + h + 1]).then_inc(s_exp, 1)
                elif kind == "T":
                    h = t[2]
                    part = pt_use[t + (0,)]
                    n = min(4, i + 1)
                    take(act, "2b", f"PT{part}", t + (0,))
                    if i * NH + h >= 2:
                        act.wait_ge(av_done, i * NH + h - 1)
                    copy(PT[:, h % 2, 0:n, :], ps[:, 4 + part, 0:n * P].rearrange("p (j q) -> p j q", q=P))\
                        .then_inc(emptied[f"2bPT{part}"], 1)
                elif kind != "V":
                    tail(t)
            act.drain().then_inc(prompts_done, 1)
            act.wait_ge(prompts_done, 3)
            tiles_out(act, h_out, NT)
            tiles_out(act, x2_out, NT)

            flat = ps[:, :, :].rearrange("p b n -> p (b n)")

            def keep_keys(b):
                for c in (2, 3):
                    part = tk_use["k", b, c]
                    take(act, "2c", f"TK{part}", ("k", b, c))
                    copy(KTs[:, 512 * c:512 * (c + 1)], ps[:, 5 + part, :]).then_inc(emptied[f"2cTK{part}"], 1)

            def exps(b):
                act.wait_ge(smax_ready, b + 1)
                fn(Ps[0:SR, :], flat[0:SR, 0:LS], ACT.Exp, bias=snb[:, b:b + 1], scale=SCALE,
                   accum_out=sesum[:, b:b + 1]).then_inc(emptied["2cSS"], 1)

            def keep_probs(b):
                for c in range(3):
                    part = tk_use["p", b, c]
                    take(act, "2c", f"TK{part}", ("p", b, c))
                    if c == 0 and b:
                        take(act, "2c", "PV", b - 1)
                    if c < 2:
                        copy(PTs[:, 8 * c:8 * c + 8, :], ps[:, 5 + part, :].rearrange("p (a t) -> p a t", a=8)).then_inc(emptied[f"2cTK{part}"], 1)
                    else:
                        copy(PTs[0:ST, SLOTS, :], ps[0:ST, 5 + part, 0:SR]).then_inc(emptied[f"2cTK{part}"], 1)

            def keep_values(b):
                take(act, "2c", "PV", b)
                act.wait_ge(sinv_ready, b + 1)
                if b:
                    take(act, "2c", f"TK{tk_use['o', b - 1, 0]}", ("o", b - 1, 0))
                copy(Os[0:SR, :], ps[0:SR, 7, 0:P], scale=seinv[:, b:b + 1]).then_inc(emptied["2cPV"], 1)

            def keep_turned(b):
                part = tk_use["o", b, 0]
                take(act, "2c", f"TK{part}", ("o", b, 0))
                for g in range(NKV):
                    pv = ps[HD * g:HD * (g + 1), 5 + part, 32 * g:32 * g + 32].rearrange("p (h t) -> p h t", h=GH)
                    ins = copy(mixS[HD * g:HD * (g + 1), :, b * ST:(b + 1) * ST], pv)
                ins.then_inc(emptied[f"2cTK{part}"], 1)

            keep_keys(0)
            exps(0)
            keep_keys(1)
            for b in range(SB):
                keep_probs(b)
                if b:
                    keep_turned(b - 1)
                if b + 1 < SB:
                    exps(b + 1)
                if b + 2 < SB:
                    keep_keys(b + 2)
                keep_values(b)
            keep_turned(SB - 1)
            for t in tail_tasks(NT):
                tail(t)
            act.drain().then_inc(phase2, 1)
            act.wait_ge(phase2, 4)

            def silu(e, s, first):
                act.wait_ge(gu_filled, e + 1)
                if not first:
                    act.wait_ge(hid_ready, e - 1)
                fn(sg[:, s, :], ps[:, 2 + s, 0:2 * CAP], ACT.Silu).then_inc(silu_ready, 1)

            def keep_xgT(e, s):
                act.wait_ge(xT_filled[0], e + 1)
                copy(xgT[:, s, 0:4, :], four(ps[:, 0, :], CAP)).then_inc(xT_emptied[0], 1)

            def keep_out(e, q, s, first):
                act.wait_ge(dn_filled[0], e + 1)
                if not first:
                    act.wait_ge(eo_out[s], q * 16)
                copy(ob[0:CAP, s, 0:512], ps[0:CAP, 5, :]).then_inc(dn_emptied[0], 1)
                for c in range(2):
                    act.wait_ge(dn_emptied[c], e + 1)
                act.dma_start(block_rows(e), ob[0:CAP, s, :]).then_inc(eo_out[s], 16)

            keep_xgT(0, 0)
            for e in range(2):
                silu(e, e, True)
                keep_xgT(e + 1, (e + 1) % 2)
                keep_out(e, 0, e, True)
            with act.Fori(1, NE // 2 - 1) as q:
                for s in range(2):
                    silu(q * 2 + s, s, False)
                    keep_xgT(q * 2 + (s + 1), (s + 1) % 2)
                    keep_out(q * 2 + s, q, s, False)
            silu(NE - 2, 0, False)
            keep_xgT(NE - 1, 1)
            keep_out(NE - 2, NE // 2 - 1, 0, False)
            silu(NE - 1, 1, False)
            keep_out(NE - 1, NE // 2 - 1, 1, False)
            for s in range(2):
                act.wait_ge(eo_out[s], 16 * (NE // 2))
            some = act.value_load(ovb[0:1, OVB:OVB + 1], min_val=0, max_val=OVB)
            with act.If(some > 0):
                act.nop().then_inc(ov_out, 16)
                with act.Fori(0, OVB) as j:
                    act.wait_ge(ov_pe, j * 3 + 5)
                    fn(sg[:, 0, :], ps[:, 2, 0:2 * CAP], ACT.Silu).then_inc(ov_act, 1)
                    act.wait_ge(ov_dve, j * 3 + 6)
                    act.dma_start(block_rows(j + NE), ob[0:CAP, 0, :]).then_inc(ov_out, 16)
                act.wait_ge(ov_out, 16 * OVB + 16)
            with act.Else():
                act.nop()
            act.drain().then_inc(experts_done, 1)
            act.wait_ge(experts_done, 4)
            for i in range(TILES):
                r, s = rows(i), i % 2
                act.wait_ge(ysum_ready, 2 * (i + 1))
                if i:
                    act.wait_ge(std3_ready, i)
                fn(sq[0:r, :], yc[0:r, s, :], ACT.Square, accum_out=ssq3[0:r, i:i + 1]).then_inc(ssq3_ready, 1)
                act.wait_ge(ssq3_ready, i + 1)
                fn(std3[0:r, i:i + 1], ssq3[0:r, i:i + 1], ACT.Sqrt, scale=1.0 / D, bias=const("eps", r)).then_inc(std3_ready, 1)

        @block.vector
        def _(dve):
            v = nc.vector
            steps = [0]

            def link(ins):
                steps[0] += 1
                ins.then_inc(dve_step, 1)
                dve.wait_ge(dve_step, steps[0])

            def inv_rms(n):
                r = rows(ORDER[n])
                x = xb[0:r, n % 3, :]
                dve.wait_ge(x_in[n % 3], 16 * (n // 3 + 1))
                v.tensor_tensor_reduce(out=junk[0:r, 0:D], in0=x, in1=x, scale=1.0, scalar=0.0, op0=ALU.mult, op1=ALU.add,
                                       accum_out=ssq[0:r, n:n + 1]).then_inc(ssq_ready, 1)
                dve.wait_ge(std_ready, n + 1)
                v.reciprocal(rstd[0:r, n:n + 1], std[0:r, n:n + 1]).then_inc(rstd_ready, 1)

            def add_scores(n):
                i = ORDER[n]
                sc = scv(i)
                for m, lo, w, h in score_steps[n]:
                    copied(dve, "1", f"S{m % 2}", ("s", m))
                    dst, src, wt = sc[:, lo:lo + w], rl[:, m % 2, 0:w], W[:, i, h:h + 1]
                    if h == 0:
                        v.tensor_scalar(dst, src, wt, None, ALU.mult).then_inc(score_added, 1)
                    else:
                        dve.wait_ge(score_added, m)
                        v.scalar_tensor_tensor(out=dst, in0=src, scalar=wt, in1=dst, op0=ALU.mult, op1=ALU.add).then_inc(score_added, 1)
                dve.wait_ge(score_added, score_steps[n][-1][0] + 1)

            def bound(group, c0):
                R, cols = group[0][2], slice(c0, c0 + len(group))
                lo, hi, mid, midh = (x[0:R, cols] for x in (lo_, hi_, mid_, midh_))
                for a, (sc, w, _, lastmask, _, _) in enumerate(group):
                    v.tensor_reduce(lo[:, a:a + 1], sc, AX.X, ALU.min)
                    link(v.tensor_reduce(hi[:, a:a + 1], sc, AX.X, ALU.max))
                    k = lastmask.shape[1]
                    ins = v.tensor_tensor(sc[:, w - k:w], sc[:, w - k:w], lastmask, ALU.add)
                link(ins)
                v.tensor_scalar(lo, lo, 0.5, None, ALU.mult)
                link(v.tensor_scalar(hi, hi, 0.5, None, ALU.mult))
                link(v.tensor_tensor(mid, lo, hi, ALU.add))
                link(v.tensor_scalar(midh, mid, 0.5, None, ALU.mult))

            def halve(group, c0, base):
                n = len(group)
                R, cols = group[0][2], slice(c0, c0 + n)
                lo, hi, mid, midh, cnt, t1, t2 = (x[0:R, cols] for x in (lo_, hi_, mid_, midh_, cnt_, t1_, t2_))
                k = [0]

                def lnk(ins):
                    k[0] += 1
                    ins.then_inc(dve_step, 1)
                    dve.wait_ge(dve_step, base + k[0])

                for a, (sc, w, _, _, _, bufs) in enumerate(group):
                    if a >= 3:
                        dve.wait_ge(dve_step, base + (a - 2))
                    v.tensor_scalar(bufs[a % 3][0:R, 0:w], sc, mid[:, a:a + 1], None, ALU.is_ge, ALU.add,
                                    accum_out=cnt[:, a:a + 1]).then_inc(dve_step, 1)
                k[0] = n
                dve.wait_ge(dve_step, base + n)
                v.tensor_scalar(t1, cnt, float(TOPK), -2 * BIG, ALU.is_lt, ALU.mult)
                lnk(v.tensor_scalar(t2, cnt, float(TOPK), 2 * BIG, ALU.is_ge, ALU.mult))
                v.tensor_tensor(t1, t1, midh, ALU.add)
                lnk(v.tensor_tensor(t2, t2, midh, ALU.add))
                v.tensor_tensor(lo, lo, t1, ALU.max)
                lnk(v.tensor_tensor(hi, hi, t2, ALU.min))
                lnk(v.tensor_tensor(mid, lo, hi, ALU.add))
                v.tensor_scalar(midh, mid, 0.5, None, ALU.mult)
                return k[0]

            def unhalve(group, c0):
                R, cols = group[0][2], slice(c0, c0 + len(group))
                v.tensor_scalar(lo_[0:R, cols], lo_[0:R, cols], 2.0, None, ALU.mult)
                link(v.tensor_scalar(hi_[0:R, cols], hi_[0:R, cols], 2.0, None, ALU.mult))

            def admit(entry, c):
                sc, w, R, _, out, (_, G, T) = entry
                g, t, nd = G[0:R, 0:w], T[0:R, 0:w], need_[0:R, c:c + 1]
                link(v.tensor_scalar(g, sc, hi_[0:R, c:c + 1], None, ALU.is_gt, ALU.add, accum_out=nd))
                v.tensor_scalar(nd, nd, -1.0, float(TOPK), ALU.mult, ALU.add)
                link(v.scalar_tensor_tensor(out=t, in0=sc, scalar=lo_[0:R, c:c + 1], in1=g, op0=ALU.is_ge, op1=ALU.subtract))
                yield
                link(v.tensor_tensor_scan(sc, t, t, 0.0, ALU.add, ALU.max))
                yield
                link(v.scalar_tensor_tensor(out=t, in0=sc, scalar=nd, in1=t, op0=ALU.is_le, op1=ALU.mult))
                yield
                link(v.scalar_tensor_tensor(out=t, in0=t, scalar=-1.0, in1=g, op0=ALU.add, op1=ALU.add))
                yield
                link(v.tensor_scalar(out, t, BIG, None, ALU.mult))

            def prompt_group(tiles):
                return [(scv(i), P * (i + 1), P, const("dmask"), maskv(i), (junk, selG, selT)) for i in tiles]

            def halvings(group, c0, times):
                base, per = steps[0], len(group) + 4
                with dve.Fori(0, times // 2) as it:
                    halve(group, c0, it * (2 * per) + base)
                    assert halve(group, c0, it * (2 * per) + (base + per)) == per
                steps[0] += per * times

            def admit_group(group, c0):
                unhalve(group, c0)
                for a, entry in enumerate(group):
                    for _ in admit(entry, c0 + a):
                        pass

            def select_samples():
                group = [(SCs[0:SR, :], LS, SR, const("tailmask", SR), smask[0:SR, :], (sJ, sG, sT))]
                bound(group, 6)
                yield
                for _ in range(ITERS):
                    steps[0] += halve(group, 6, steps[0])
                    yield
                unhalve(group, 6)
                yield from admit(group[0], 6)
                dve.nop().then_inc(smask_ready, 1)

            inv_rms(0)
            inv_rms(1)
            near, far = prompt_group((2, 3, 4)), prompt_group((5, 6, 7))
            for n in range(TILES + 1):
                if n + 2 < TILES:
                    inv_rms(n + 2)
                if n == TILES - 2:
                    bound(near, 0)
                if n in EARLY:
                    halvings(near, 0, EARLY[n])
                if n and score_steps[n - 1]:
                    add_scores(n - 1)
            dve.drain().then_inc(phase1, 1)
            halvings(near, 0, ITERS - sum(EARLY.values()))
            bound(far, 3)
            halvings(far, 3, ITERS)
            take(dve, "2a", "TR", (SB - 1, 1))
            admit_group(near, 0)
            admit_group(far, 3)
            dve.nop().then_inc(masks_ready, 1)
            dve.wait_ge(phase1, 4)
            dve.wait_ge(phase2a, 3)
            link(v.memset(ASUM[:, :], 0.0))
            link(v.memset(G8[:, NG:8], -BIG))
            link(v.memset(A[:, :], 0.0))
            link(v.memset(RK[:, :, :], 0.0))
            link(v.memset(EF[:, :, :], 0.0))
            dve.wait_ge(init_done, 6)

            def route(i):
                r = rows(i)
                v.tensor_tensor(L[0:r, :], ps[0:r, 7, 0:36], bias36[0:r, :], ALU.add).then_inc(emptied["2bM"], 1)
                copied(dve, "2b", "M", ("LG", i))
                link(v.tensor_copy(G8[0:r, 0:NG], L[0:r, 0:NG]))
                link(v.max(gm8[0:r, :], G8[0:r, :]))
                link(v.max_index(gi8[0:r, :], gm8[0:r, :], G8[0:r, :]))
                link(v.tensor_copy(r1[0:r, 4:5], gi8[0:r, 0:1]))
                link(v.tensor_scalar(oh4[0:r, :], const("iota", r)[:, 0:NG], r1[0:r, 4:5], None, ALU.is_equal))
                link(v.tensor_scalar(oh4[0:r, :], oh4[0:r, :], -1.0, BIG, ALU.add, ALU.mult))
                pen = oh4[0:r, :].unsqueeze(2).broadcast_to([r, NG, EPG])
                link(v.tensor_tensor(E32[0:r, :].rearrange("p (g e) -> p g e", g=NG), L[0:r, NG:36].rearrange("p (g e) -> p g e", g=NG),
                                     pen, ALU.add))
                link(v.max(em8[0:r, :], E32[0:r, :]))
                link(v.max_index(ei8[0:r, :], em8[0:r, :], E32[0:r, :]))
                link(v.tensor_scalar(r1[0:r, 0:1], gm8[0:r, 0:1], -1.0, None, ALU.mult))
                v.tensor_tensor(r1[0:r, 1:2], em8[0:r, 1:2], em8[0:r, 0:1], ALU.subtract).then_inc(logits_split, 1)
                link(v.tensor_copy(EF[0:r, i, :], ei8[0:r, 0:2]))
                for k in range(2):
                    link(v.tensor_scalar(OH[0:r, k, :], const("iota", r), EF[0:r, i, k:k + 1], None, ALU.is_equal))
                v.tensor_tensor(A[0:r, :], OH[0:r, 0, :], OH[0:r, 1, :], ALU.add).then_inc(A_ready, 1)
                dve.wait_ge(gexp_ready, i + 1)
                link(v.tensor_scalar(r1[0:r, 5:6], r1[0:r, 3:4], 1.0, None, ALU.add))
                link(v.tensor_tensor(r1[0:r, 5:6], r1[0:r, 5:6], r1[0:r, 2:3], ALU.mult))
                link(v.reciprocal(CW[0:r, i, 0:1], r1[0:r, 5:6]))
                link(v.tensor_tensor(CW[0:r, i, 1:2], CW[0:r, i, 0:1], r1[0:r, 3:4], ALU.mult))

            def rank(i):
                r = rows(i)
                for k in range(2):
                    ins = v.tensor_tensor_reduce(out=rkt[0:r, :], in0=ps[0:r, 7, 0:NE], in1=OH[0:r, k, :], scale=1.0, scalar=0.0,
                                                 op0=ALU.mult, op1=ALU.add, accum_out=RK[0:r, i, k:k + 1])
                    if k == 0:
                        link(ins)
                ins.then_inc(emptied["2bM"], 1)
                copied(dve, "2b", "M", ("RK", i))
                v.tensor_tensor(ASUM[0:r, :], ASUM[0:r, :], A[0:r, :], ALU.add).then_inc(ASUM_ready, 1)
                dve.wait_ge(ASUM_ready, i + 1)
                link(v.tensor_scalar(FF[0:r, :], RK[0:r, i, :], float(CAP), float(NBLK * CAP), ALU.is_ge, ALU.mult))
                link(v.tensor_tensor(FF[0:r, :], FF[0:r, :], RK[0:r, i, :], ALU.add))
                link(v.scalar_tensor_tensor(out=FF[0:r, :], in0=EF[0:r, i, :], scalar=float(CAP), in1=FF[0:r, :],
                                            op0=ALU.mult, op1=ALU.add))
                link(v.tensor_scalar(FF[0:r, :], FF[0:r, :], float(NBLK * CAP), None, ALU.min))
                v.tensor_copy(first[0:r, i, :], FF[0:r, :]).then_inc(first_ready, 1)

            def tail(t):
                kind, i = t[0], t[1]
                r, s = rows(i), i % 2
                if kind == "OP":
                    take(dve, "2b", "M", t)
                    dve.wait_ge(xr_in[s], 16 * (i // 2 + 1))
                    half = hb[0:r, s, 512 * t[2]:512 * t[2] + 512]
                    v.tensor_tensor(half, ps[0:r, 7, :], half, ALU.add).then_inc(emptied["2bM"], 1)
                    if t[2] == 1:
                        dve.wait_ge(std2_ready, i + 1)
                        if i == 0:
                            dve.wait_ge(gb_in, 16)
                        link(v.reciprocal(rstd2[0:r, i:i + 1], std2[0:r, i:i + 1]))
                        v.scalar_tensor_tensor(out=x2[0:r, s, :], in0=hb[0:r, s, :], scalar=rstd2[0:r, i:i + 1], in1=gb[0:r, :],
                                               op0=ALU.mult, op1=ALU.mult).then_inc(x2_ready, 1)
                elif kind == "LG":
                    take(dve, "2b", "M", t)
                    if i == 0:
                        dve.wait_ge(rw_in, 64)
                    route(i)
                elif kind == "RK":
                    take(dve, "2b", "M", t)
                    rank(i)

            def last_chunk(i, h):
                return ("T", i, h, 4 if i >= 4 else 0)

            samples = select_samples()
            for t in tasks:
                kind, i = t[0], t[1]
                if kind == "V" and i >= 2:
                    next(samples, None)
                if kind == "S":
                    h, w, idx = t[2], P * (i + 1), i * NH + t[2]
                    take(dve, "2b", f"A{h % 2}", t)
                    if idx >= 3:
                        key = last_chunk(*divmod(idx - 3, NH))
                        take(dve, "2b", f"PT{pt_use[key]}", key)
                    sc2 = ps[:, 2 * (h % 2):2 * (h % 2) + 2, :].rearrange("p b n -> p (b n)")[:, 0:w]
                    v.tensor_tensor_reduce(out=Sm[:, idx % 3, 0:w], in0=sc2, in1=maskv(i), scale=1.0, scalar=-3e38, op0=ALU.add,
                                           op1=ALU.max, accum_out=mx[:, h:h + 1]).then_inc(emptied[f"2bA{h % 2}"], 1)
                    copied(dve, "2b", f"A{h % 2}", t)
                    v.tensor_scalar(nb[:, h:h + 1], mx[:, h:h + 1], -SCALE, None, ALU.mult).then_inc(s_masked, 1)
                elif kind == "T":
                    h = t[2]
                    if i >= 4:
                        part = pt_use[t + (4,)]
                        n = i + 1 - 4
                        take(dve, "2b", f"PT{part}", t + (4,))
                        if i * NH + h >= 2:
                            dve.wait_ge(av_done, i * NH + h - 1)
                        v.tensor_copy(PT[:, h % 2, 4:4 + n, :], ps[:, 4 + part, 0:n * P].rearrange("p (j q) -> p j q", q=P))\
                            .then_inc(emptied[f"2bPT{part}"], 1)
                elif kind == "V":
                    if t[2] == NH - 1:
                        take(dve, "2b", "O", ("V", i))
                        if i:
                            take(dve, "2b", "M", ("OT", i - 1))
                        dve.wait_ge(s_exp, (i + 1) * NH)
                        e8 = slice(8 * (i % 2), 8 * (i % 2) + 8)
                        link(v.reciprocal(einv[:, e8], esum[:, e8]))
                        inv = einv[:, e8].rearrange("p (g b) -> p g b", g=NKV).unsqueeze(3).broadcast_to([P, NKV, GH, HD])
                        v.tensor_tensor(Osb[:, :].rearrange("p (b g d) -> p g b d", g=NKV, b=GH),
                                        ps[:, 6, :].rearrange("p (g b d) -> p g b d", g=NKV, b=GH), inv, ALU.mult)\
                            .then_inc(emptied["2bO"], 1)
                else:
                    tail(t)
            assert next(samples, "through") == "through"
            dve.drain().then_inc(prompts_done, 1)
            dve.wait_ge(prompts_done, 3)
            flat = ps[:, :, :].rearrange("p b n -> p (b n)")
            def keep_keys(b):
                for c in (0, 1):
                    part = tk_use["k", b, c]
                    take(dve, "2c", f"TK{part}", ("k", b, c))
                    v.tensor_copy(KTs[:, 512 * c:512 * (c + 1)], ps[:, 5 + part, :]).then_inc(emptied[f"2cTK{part}"], 1)

            keep_keys(0)
            for b in range(SB):
                take(dve, "2c", "SS", b)
                link(v.tensor_reduce(smx[:, b:b + 1], flat[0:SR, 0:LS], AX.X, ALU.max))
                v.tensor_scalar(snb[:, b:b + 1], smx[:, b:b + 1], -SCALE, None, ALU.mult).then_inc(smax_ready, 1)
                if b + 1 < SB:
                    keep_keys(b + 1)
                copied(dve, "2c", "SS", b)
                v.reciprocal(seinv[:, b:b + 1], sesum[:, b:b + 1]).then_inc(sinv_ready, 1)
            for t in tail_tasks(NT):
                tail(t)
            take(dve, "2b", "M", "count")
            v.tensor_copy(cntE[:, :], ps[:, 7, 0:NE]).then_inc(emptied["2bM"], 1)
            copied(dve, "2b", "M", "count")
            link(v.tensor_scalar(ovT[:, :], const("iota"), float(CAP), float(CAP), ALU.mult, ALU.add))
            many = NTOK // CAP
            wide = sJ.bitcast(F32)[:, 0:NE * many].rearrange("p (e j) -> p e j", e=NE)
            link(v.tensor_tensor(wide, cntE[:, :].unsqueeze(2).broadcast_to([P, NE, many]),
                                 ovT[:, 0:many].unsqueeze(1).broadcast_to([P, NE, many]), ALU.is_gt))
            link(v.tensor_reduce(ovE[:, :], wide, AX.X, ALU.add))
            link(v.memset(ovT[:, :], 0.0))
            link(v.tensor_tensor_scan(ovX[:, :], ovE[:, :], ovT[:, :], 0.0, ALU.add, ALU.add))
            link(v.tensor_tensor(ovS[:, :], ovX[:, :], ovE[:, :], ALU.subtract))
            efl, rkf = EF[:, :, :].rearrange("p i k -> p (i k)"), RK[:, :, :].rearrange("p i k -> p (i k)")
            n = 2 * TILES
            wide = sJ.bitcast(F32)[:, 0:n * NE].rearrange("p (a e) -> p a e", e=NE)
            link(v.tensor_tensor(wide, const("iota").unsqueeze(1).broadcast_to([P, n, NE]),
                                 efl.unsqueeze(2).broadcast_to([P, n, NE]), ALU.is_equal))
            link(v.tensor_tensor(wide, wide, ovS[:, :].unsqueeze(1).broadcast_to([P, n, NE]), ALU.mult))
            link(v.tensor_reduce(OS[:, :], wide, AX.X, ALU.add))
            link(v.scalar_tensor_tensor(out=DF[:, :], in0=OS[:, :], scalar=1.0, in1=efl, op0=ALU.mult, op1=ALU.subtract))
            link(v.tensor_scalar(DF[:, :], DF[:, :], float(CAP), float((NE - 1) * CAP), ALU.mult, ALU.add))
            link(v.tensor_scalar(DB[:, :], rkf, float(CAP), None, ALU.is_ge))
            link(v.tensor_tensor(DF[:, :], DF[:, :], DB[:, :], ALU.mult))
            link(v.tensor_tensor(DF[:, :], DF[:, :], rkf, ALU.add))
            link(v.scalar_tensor_tensor(out=DF[:, :], in0=efl, scalar=float(CAP), in1=DF[:, :], op0=ALU.mult, op1=ALU.add))
            link(v.tensor_copy(dest[:, :, :].rearrange("p i k -> p (i k)"), DF[:, :]))
            wide = sJ.bitcast(F32)[:, 0:OVB * NE].rearrange("p (j e) -> p j e", e=NE)
            link(v.tensor_tensor(wide, ovX[:, :].unsqueeze(1).broadcast_to([P, OVB, NE]),
                                 const("iota")[:, 0:OVB].unsqueeze(2).broadcast_to([P, OVB, NE]), ALU.is_le))
            link(v.tensor_reduce(ovf[:, 0:OVB], wide, AX.X, ALU.add))
            link(v.tensor_copy(ovf[:, OVB:OVB + 1], ovX[:, NE - 1:NE]))
            link(v.tensor_scalar(ovf[:, 0:OVB], ovf[:, 0:OVB], float(NE - 1), None, ALU.min))
            v.tensor_copy(ovb[:, :], ovf[:, :]).then_inc(dest_ready, 1)
            dve.drain().then_inc(phase2, 1)
            dve.wait_ge(phase2, 4)

            def gated(s):
                return v.tensor_tensor(hT[:, s].rearrange("p c t -> p (c t)"), sg[:, s, :], ps[:, 2 + s, 2 * CAP:4 * CAP], ALU.mult)

            def gate(e, s):
                dve.wait_ge(silu_ready, e + 1)
                gated(s).then_inc(hid_ready, 1)

            def keep_xgT(e, s):
                dve.wait_ge(xT_filled[1], e + 1)
                v.tensor_copy(xgT[:, s, 4:8, :], ps[:, 1, 0:4 * CAP].rearrange("p (j t) -> p j t", j=4)).then_inc(xT_emptied[1], 1)

            def keep_out(e, q, s, first):
                dve.wait_ge(dn_filled[1], e + 1)
                if not first:
                    dve.wait_ge(eo_out[s], q * 16)
                v.tensor_copy(ob[0:CAP, s, 512:1024], ps[0:CAP, 6, :]).then_inc(dn_emptied[1], 1)

            keep_xgT(0, 0)
            for e in range(2):
                gate(e, e)
                keep_xgT(e + 1, (e + 1) % 2)
                keep_out(e, 0, e, True)
            with dve.Fori(1, NE // 2 - 1) as q:
                for s in range(2):
                    gate(q * 2 + s, s)
                    keep_xgT(q * 2 + (s + 1), (s + 1) % 2)
                    keep_out(q * 2 + s, q, s, False)
            gate(NE - 2, 0)
            keep_xgT(NE - 1, 1)
            keep_out(NE - 2, NE // 2 - 1, 0, False)
            gate(NE - 1, 1)
            keep_out(NE - 1, NE // 2 - 1, 1, False)
            for s in range(2):
                dve.wait_ge(eo_out[s], 16 * (NE // 2))
            some = dve.value_load(ovb[0:1, OVB:OVB + 1], min_val=0, max_val=OVB)
            with dve.If(some > 0):
                dve.nop().then_inc(ov_dve, 3)
                with dve.Fori(0, OVB) as j:
                    dve.wait_ge(ov_pe, j * 3 + 4)
                    v.tensor_copy(xgT[:, 0].rearrange("p (a j) t -> p a (j t)", a=2), ps[:, 0:2, 0:4 * CAP]).then_inc(ov_dve, 1)
                    dve.wait_ge(ov_act, j + 1)
                    gated(0).then_inc(ov_dve, 1)
                    dve.wait_ge(ov_pe, j * 3 + 6)
                    dve.wait_ge(ov_out, j * 16 + 16)
                    v.tensor_copy(ob[0:CAP, 0, :], flat[0:CAP, 5 * 512:7 * 512]).then_inc(ov_dve, 1)
                dve.nop()
            with dve.Else():
                dve.nop()
            dve.drain().then_inc(experts_done, 1)
            dve.wait_ge(experts_done, 4)
            dve.wait_ge(fin_norm_in, 16)

            def finish(i):
                r, s = rows(i), i % 2
                dve.wait_ge(std3_ready, i + 1)
                link(v.reciprocal(rstd3[0:r, i:i + 1], std3[0:r, i:i + 1]))
                v.scalar_tensor_tensor(out=yc[0:r, s, :], in0=yc[0:r, s, :], scalar=rstd3[0:r, i:i + 1], in1=gb[0:r, :],
                                       op0=ALU.mult, op1=ALU.mult).then_inc(y_ready[s], 1)

            for i in range(TILES):
                r, s = rows(i), i % 2
                dve.wait_ge(o_in[s], 32 * (i // 2 + 1))
                dve.wait_ge(hc_in[s], 16 * (i // 2 + 1))
                if i >= 2:
                    dve.wait_ge(y_out[s], 16 * (i // 2))
                v.scalar_tensor_tensor(out=yc[0:r, s, :], in0=o1[0:r, s, :], scalar=CW[0:r, i, 0:1], in1=hc[0:r, s, :],
                                       op0=ALU.mult, op1=ALU.add).then_inc(ysum_ready, 1)
                dve.wait_ge(ysum_ready, 2 * i + 1)
                v.scalar_tensor_tensor(out=yc[0:r, s, :], in0=o2[0:r, s, :], scalar=CW[0:r, i, 1:2], in1=yc[0:r, s, :],
                                       op0=ALU.mult, op1=ALU.add).then_inc(ysum_ready, 1)
                if i:
                    finish(i - 1)
            finish(TILES - 1)


_INS = ['x_prompt', 'x_sample', 'cache_k', 'cache_v', 'cache_idx_k', 'state_pool', 'page_table', 'norm_mix_g', 'w_in',
        'pool_w', 'pool_scale', 'w_out', 'norm_ffn_g', 'router_group_w', 'router_group_b', 'router_expert_w',
        'router_expert_b', 'expert_w_gate', 'expert_w_up', 'expert_w_down', 'final_norm_g']
_OUTS = [(1, SEQ, D), (SB, ST, D), (1, 1, SEQ, NKV, HD), (1, 1, SEQ, NKV, HD), (1, 1, SEQ, HD), (1, 1, HALO, 512),
         (1, SB, ST, NKV, HD), (1, SB, ST, NKV, HD), (1, SB, ST, HD), (1, SB, HALO, 512)]


def kernel(**inputs):
    import concourse.bacc as bacc
    from concourse.bass_utils import run_bass_kernel_spmd

    nc = bacc.Bacc("TRN2", target_bir_lowering=False, num_devices=1)
    arrays, args = {}, []
    table, spread = constants()
    values = [(name, np.ascontiguousarray(inputs[name])) for name in _INS] + [("const_table", table), ("head_select", spread)]
    for name, a in values:
        arrays[f"in_{name}"] = a
        args.append(nc.dram_tensor(f"in_{name}", a.shape, mybir.dt.from_np(a.dtype), kind="ExternalInput").ap())
    for i, shape in enumerate(_OUTS):
        args.append(nc.dram_tensor(f"out_{i}", shape, F32, kind="ExternalOutput").ap())
    program(nc, *args)
    r = run_bass_kernel_spmd(nc, [arrays], core_ids=[0])
    return tuple(r.results[0][f"out_{i}"] for i in range(len(_OUTS)))
```

```python
from contextlib import ExitStack

import numpy as np

import concourse.bass as bass
from concourse import mybir

F32 = mybir.dt.float32
BF16 = mybir.dt.bfloat16
U32 = mybir.dt.uint32
I32 = mybir.dt.int32
ALU = mybir.AluOpType
ACT = mybir.ActivationFunctionType
AX = mybir.AxisListType

P = 128
D = 1024
KC = D // P
SEQ = 1024
NT = SEQ // P
SB, ST = 8, 8
SR = SB * ST
NTOK = SEQ + SR
TILES = NT + 1
PAST, PAGE = 2048, 128
NPG = PAST // PAGE
SLOTS = PAST // P
LS = PAST + ST
HD, NH, NKV = 64, 8, 2
GH = NH // NKV
ROPE = 16
TOPK = 256
NIN = 1864
CU, CQ, CK, CV, CQI, CKI, CWI = 0, 512, 1024, 1152, 1280, 1792, 1856
WINDOWS = (2, 4, 8, 16)
HALO = 15
NG, EPG = 4, 8
NE = NG * EPG
HID = 256
CAP = 96
OVB = 2 * NTOK // CAP
OVB += -OVB % 8
NBLK = NE + OVB
EPS = 1e-6
SCALE = HD ** -0.5
BIG = 1e30
ITERS = 26
PIECES = {"S": (2, False), "T": (2, False), "V": (1, True)}
WSLOTS = 4
OSLOTS = 6
OQ = 4
SAMPLES_FROM = (3, 0)
EARLY = {7: 6, 8: 6}
ZS = 20
ORDER = [NT] + list(range(NT))

CC = {}
_at = 0
for _n, _w in (("ident", P), ("dmask", P), ("tri", P), ("ones", P), ("cos", TILES * ROPE), ("sin", TILES * ROPE),
               ("pinv", 4 * 16), ("iota", NE), ("tailmask", ST), ("diag", ST), ("tokid", TILES), ("pmod", 1), ("eps", 1), ("z", 1)):
    CC[_n] = (_at, _at + _w)
    _at += _w
NCONST = _at


def constants():
    c = np.zeros((P, NCONST), np.float32)

    def put(name, a):
        lo, hi = CC[name]
        a = np.asarray(a, np.float32)
        c[:a.shape[0], lo:hi] = a.reshape(a.shape[0], -1)

    r = np.arange(P)
    put("ident", np.eye(P))
    put("dmask", np.where(r[None, :] <= r[:, None], 0.0, -BIG))
    put("tri", (r[:, None] < r[None, :]))
    put("ones", np.ones((P, P)))
    half = ROPE // 2
    inv = np.power(np.float32(500000.0), -np.arange(half, dtype=np.float32) / np.float32(half)).astype(np.float32)
    pos = np.zeros((TILES, P), np.float32)
    pos[:NT] = np.arange(SEQ).reshape(NT, P)
    pos[NT, :SR] = PAST + np.arange(SR) % ST
    ang = (pos[:, :, None] * inv).astype(np.float32)
    co, si = np.cos(ang), np.sin(ang)
    put("cos", np.concatenate([co, co], -1).transpose(1, 0, 2))
    put("sin", np.concatenate([-si, si], -1).transpose(1, 0, 2))
    put("pinv", np.tile(np.stack([1.0 / np.minimum(np.arange(16) + 1, w) for w in WINDOWS]).reshape(1, -1), (P, 1)))
    put("iota", np.tile(np.arange(NE)[None], (P, 1)))
    rs = np.arange(SR)
    put("tailmask", np.where(np.arange(ST)[None] <= (rs % ST)[:, None], 0.0, -BIG))
    put("diag", ((rs % ST)[:, None] == np.arange(ST)[None]))
    tok = np.arange(TILES)[None] * P + r[:, None]
    put("tokid", np.minimum(tok, NTOK - 1))
    put("pmod", (r % (P // NPG))[:, None])
    put("eps", np.full((P, 1), EPS))
    s = np.zeros((SR, SB, NH, ST), np.float32)
    for b in range(SB):
        for t in range(ST):
            s[b * ST + t, b, :, t] = 1.0
    return c, s.reshape(SR, SB * SR)


def mask_at(i):
    return P * (i * (i + 1) // 2)


def program(nc, x_prompt, x_sample, cache_k, cache_v, cache_idx_k, state_pool, page_table, norm_mix_g, w_in,
            pool_w, pool_scale, w_out, norm_ffn_g, router_group_w, router_group_b, router_expert_w,
            router_expert_b, expert_w_gate, expert_w_up, expert_w_down, final_norm_g, const_table, head_select,
            y_prompt, y_sample, k_prompt, v_prompt, idx_k_prompt, pool_prompt,
            k_sample, v_sample, idx_k_sample, pool_sample):
    ctx = ExitStack()
    with ctx:
        def sem(name):
            return ctx.enter_context(nc.semaphore(name))

        TOTAL = 53200
        mem = ctx.enter_context(nc.sbuf_tensor("mem", [P, TOTAL], F32))
        ps = ctx.enter_context(nc.psum_tensor("ps", [P, 8, 512], F32))
        at = [0]

        def cut(n, shape=None, dt=F32):
            lo = at[0]
            at[0] += n
            assert at[0] <= TOTAL, at[0]
            v = mem[:, lo:lo + n]
            if dt is not F32:
                v = v.bitcast(dt)
            if shape:
                names = "abcd"[:len(shape)]
                v = v.rearrange(f"p ({' '.join(names)}) -> p {' '.join(names)}", **dict(zip(names, shape)))
            return v

        con = cut(NCONST)
        selb = cut(SB * SR // 2, (SB, SR), BF16)
        stat = cut(256)
        gb = cut(D)
        psc = cut(4)
        early = at[0]
        kT = cut(NTOK)
        q_at = at[0]
        qT = cut(4 * NTOK, (4, NTOK))
        kiT = cut(NTOK)
        V = cut(TILES * P, (TILES, P))
        mix_at = at[0]
        mixP = cut(4 * NTOK, (4, NTOK))
        mask_at_word = at[0]
        mask = cut(36 * P // 2, None, BF16)
        kin = mask.bitcast(F32)[:, 3 * P // 2:3 * P // 2 + 2 * SLOTS * HD].rearrange("p (a s d) -> p a s d", a=2, s=SLOTS)
        SC = cut(33 * P)
        junk = cut(512, None, BF16)
        selG = cut(512, None, BF16)
        selT = cut(512, None, BF16)
        rl = cut(2 * 512, (2, 512))
        rl_end = at[0]
        W = cut(TILES * 8, (TILES, 8))
        QS = cut(NH * SR, (SB, NH, ST))
        uC = SC[:, 0:4 * SR].rearrange("p (g t) -> p g t", g=4)
        Ztwice = SC[:, 1024:2048].rearrange("p (h a d) -> p h a d", h=NH, a=2)
        WS = cut(SB * SR, (SB, SR))
        QB = cut(SB * SR, (SB, 2, GH, ST))
        persistent = at[0]

        win = cut(KC * NIN, (KC, NIN))
        qiT = cut(2 * 512, (2, 4, P))
        u2 = cut(2 * 4 * (P + HALO), (2, 4, P + HALO))
        uS = cut(4 * SB * (ST + HALO), (4, SB, ST + HALO))
        xb = cut(3 * D, (3, D))
        xnT = cut(2 * D, (2, KC, P))
        Z = cut(ZS * HD, (ZS, HD))
        sumA = cut(736)
        sumB = cut(736)
        dT = cut(4 * P)
        rt1 = cut(19 * ROPE, (19, ROPE))
        rt2 = cut(19 * ROPE, (19, ROPE))
        pw = cut(4 * P, (4, P))
        stt_in = cut(512)

        at[0] = persistent
        rt = cut(1400)
        rw = cut(KC * 36, (KC, 36))
        wout = cut(8 * D, (8, D))
        SCs = cut(LS)
        sG = cut(LS // 2, None, BF16)
        sT = cut(LS // 2, None, BF16)
        sJ = cut(LS // 2, None, BF16)
        smask = cut(LS // 2, None, BF16)
        region = at[0]
        kiTs = cut(2 * 1024, (2, 8, P))
        rs = cut(2 * LS, (2, LS))
        zslots = cut(NBLK * 16, None, I32)
        at[0] = region
        Sm = cut(3 * 1024, (3, 1024))
        PT = cut(2 * 1024, (2, 8, P))
        hb = cut(2 * D, (2, D))
        x2 = cut(2 * D, (2, D))
        x2T = cut(D, (KC, P))
        Osb = cut(512)
        mixA = cut(512, (4, P))
        at[0] = region
        mixS = cut(4 * SR, (4, SR))
        Os = cut(P)
        KTs = cut(LS)
        Ps = cut(LS)
        PTs = cut((SLOTS + 1) * SR, (SLOTS + 1, SR))
        Kin = [SC[:, 0:2048].rearrange("p (s d) -> p s d", d=P), cut(2048, (SLOTS, P))]
        Vin = [SC[:, 2048:4096].rearrange("p (s d) -> p s d", d=P), cut(2048, (SLOTS, P))]
        Vnew = rl[:, :, :].rearrange("p a n -> p (a n)")[0:ST, :].rearrange("t (b n) -> t b n", b=SB)
        assert at[0] <= TOTAL

        at[0] = early
        rows_at = TOTAL - 2 * OSLOTS * D
        wgu, wdn = [], []
        for start, end in ((q_at, mix_at), (mask_at_word, rl_end), (rows_at, rows_at + OSLOTS * D),
                           (rows_at + OSLOTS * D, rows_at + 2 * OSLOTS * D)):
            at[0] = start
            wgu.append(cut(2 * KC * HID, (2, KC, HID)))
            wdn.append(cut(2 * D, (2, D)))
            assert at[0] <= end
        at[0] = persistent + 1400
        xg = cut(2 * D, (2, D))
        xgT = cut(2 * KC * CAP, (2, KC, CAP))
        sg = cut(2 * 2 * CAP, (2, 2 * CAP))
        hT = cut(2 * 2 * CAP, (2, 2, CAP))
        assert at[0] <= TOTAL
        hc = cut(TILES * D, (TILES, D))
        sq = cut(D // 2, None, BF16)
        assert at[0] <= rows_at
        at[0] = rows_at
        o1 = cut(OSLOTS * D, (OSLOTS, D))
        o2 = cut(OSLOTS * D, (OSLOTS, D))
        at[0] = mix_at
        ob = cut(2 * D, (2, D))
        assert at[0] <= mask_at_word
        def const(name, rows=P):
            lo, hi = CC[name]
            return con[0:rows, lo:hi]

        def ident(n):
            return con[0:n, CC["ident"][0]:CC["ident"][0] + n]

        def cs(name, i, rows):
            lo = CC[name][0] + i * ROPE
            return con[0:rows, lo:lo + ROPE]

        def rows(i):
            return SR if i == NT else P

        ssq, std, rstd = stat[:, 0:9], stat[:, 9:18], stat[:, 18:27]
        lo_, hi_, mid_, midh_ = (stat[:, 30 + 7 * j:37 + 7 * j] for j in range(4))
        cnt_, t1_, t2_, need_ = (stat[:, 219 + 7 * j:226 + 7 * j] for j in range(4))
        mx, nb = stat[:, 60:68], stat[:, 68:76]
        esum, einv = stat[:, 76:92], stat[:, 92:108]
        ssq2, std2, rstd2 = stat[:, 108:117], stat[:, 117:126], stat[:, 126:135]
        wsc = stat[0:SR, 135:143]
        pt_i = stat[:, 143:151].bitcast(I32)
        pidx = stat[:, 151:159].bitcast(U32)
        smx, snb, sesum, seinv = (stat[0:SR, 160 + 8 * j:168 + 8 * j] for j in range(4))
        ssq3, std3, rstd3 = stat[:, 192:201], stat[:, 201:210], stat[:, 210:219]

        rt_at = [0]

        def rcut(n, dt=F32):
            rt_at[0] += n
            v = rt[:, rt_at[0] - n:rt_at[0]]
            return v if dt is F32 else v.bitcast(dt)

        bias36 = rcut(36)
        L = rcut(36)
        G8 = rcut(8)
        gm8, gi8 = rcut(8), rcut(8, U32)
        E32 = rcut(NE)
        em8, ei8 = rcut(8), rcut(8, U32)
        r1 = rcut(8)
        gexp = rcut(4)
        oh4 = rcut(4)
        OH = rcut(2 * NE).rearrange("p (k e) -> p k e", k=2)
        A = rcut(NE)
        ASUM = rcut(NE)
        rkt = rcut(NE)
        RK = rcut(2 * TILES).rearrange("p (i k) -> p i k", k=2)
        EF = rcut(2 * TILES).rearrange("p (i k) -> p i k", k=2)
        CW = rcut(2 * TILES).rearrange("p (i k) -> p i k", k=2)
        dest = rcut(2 * TILES, U32).rearrange("p (i k) -> p i k", k=2)
        cntE, ovE, ovS, ovX, ovT = (rcut(NE) for _ in range(5))
        OS, DB, DF = (rcut(2 * TILES) for _ in range(3))
        first = rcut(2 * TILES, U32).rearrange("p (i k) -> p i k", k=2)
        FF = rcut(2)
        behind = rcut(2 * TILES).rearrange("p (i k) -> p i k", k=2)
        toki = rcut(16 * TILES, I32).rearrange("p (i k) -> p i k", k=16)
        ovb = rcut(OVB + 1, I32)
        ovf = rcut(OVB + 1)
        slot_tok = rcut(NBLK, U32)
        assert rt_at[0] <= 1400

        def scv(i):
            lo = mask_at(i) - mask_at(2)
            return SC[:, lo:lo + P * (i + 1)]

        def maskv(i):
            return mask[:, mask_at(i):mask_at(i) + P * (i + 1)]

        def bank(b, r=P, n=512):
            return ps[0:r, b, 0:n]

        def rowsof(ap, i):
            return ap[0][i * P:(i + 1) * P] if i < NT else ap[1]

        x_rows = (x_prompt[0], x_sample.rearrange("b t d -> (b t) d"))
        k_rows = (k_prompt[0, 0].rearrange("t g d -> t (g d)"), k_sample[0].rearrange("b t g d -> (b t) (g d)"))
        v_rows = (v_prompt[0, 0].rearrange("t g d -> t (g d)"), v_sample[0].rearrange("b t g d -> (b t) (g d)"))
        ik_rows = (idx_k_prompt[0, 0], idx_k_sample[0].rearrange("b t d -> (b t) d"))
        y_rows = (y_prompt[0], y_sample.rearrange("b t d -> (b t) d"))
        h_dram = nc.dram_tensor("h_rows", (NTOK, D), F32, kind="Internal").ap()
        xn_dram = nc.dram_tensor("xn_rows", (NTOK, D), F32, kind="Internal").ap()
        w_dram = nc.dram_tensor("index_weights", (SR, NH), F32, kind="Internal").ap()
        slot_dram = nc.dram_tensor("slot_tokens", (NBLK * CAP + 2 * NTOK, 16), I32, kind="Internal").ap()
        eo_dram = nc.dram_tensor("expert_rows", (NBLK * CAP, D), F32, kind="Internal").ap()
        w_in_k = w_in[0].rearrange("(p c) n -> p c n", c=KC)
        gate_k = expert_w_gate[0].rearrange("e (p c) n -> e p c n", c=KC)
        up_k = expert_w_up[0].rearrange("e (p c) n -> e p c n", c=KC)
        down_k = expert_w_down[0].rearrange("e (c p) n -> e p c n", c=2)
        SPP = PAGE // SLOTS
        ci_rows = cache_idx_k[0].rearrange("n (c s) d -> (n c) (s d)", c=SPP)
        ck_rows = cache_k[0].rearrange("n (c s) g d -> (n c) (s g d)", c=SPP)
        cv_rows = cache_v[0].rearrange("n (c s) g d -> (n c) (s g d)", c=SPP)

        PART = {"T0": 0, "T1": 1, "U": 2, "Q": 3, "QI": 4, "KV": 5, "S0": 6, "S1": 7}
        order = [("T0", "state"), ("T0", ("x", 0)), ("T1", ("x", 0))]
        score_steps = {}
        m = 0
        for n in range(TILES + 1):
            if n < TILES:
                order += [(q, n) for q in ("U", "Q", "KV", "QI")]
            if n + 1 < TILES:
                order += [("T0", ("x", n + 1)), ("T1", ("x", n + 1))]
            if n:
                order += [("T0", ("q", n - 1)), ("T1", ("qi", n - 1)), ("T0", ("k", n - 1)), ("T1", ("pool", n - 1))]
                if n - 1 in (0, TILES - 1):
                    order += [("T0", ("u", n - 1))]
                i = ORDER[n - 1]
                score_steps[n - 1] = []
                if 2 <= i < NT:
                    for lo in range(0, P * (i + 1), 512):
                        for h in range(NH):
                            score_steps[n - 1].append((m, lo, min(512, P * (i + 1) - lo), h))
                            order += [(f"S{m % 2}", ("s", m))]
                            m += 1
        n_scores = m
        P2A = {"ACC": 0, "TR": 5, "PS0": 6, "PS1": 7}
        orderA = [("TR", (0, 0)), ("TR", (0, 1))]
        for b in range(SB):
            orderA += [(f"PS{(5 * b + q) % 2}", (b, q)) for q in range(5)]
            if b + 1 < SB:
                orderA += [("TR", (b + 1, 0)), ("TR", (b + 1, 1))]
        orderA += [("ACC", 0)]
        P2B = {"A0": 0, "A1": 2, "PT0": 4, "PT1": 5, "O": 6, "M": 7}

        def tail_tasks(i):
            return ([("OT", i)] if i < NT else []) + [
                ("OP", i, 0), ("OP", i, 1), ("SQ", i), ("NM", i), ("XR", i, 0), ("XR", i, 1), ("LG", i), ("RK", i)]

        def step(kind, idx):
            return [(kind,) + divmod(idx, NH)] if idx < NT * NH else []

        tasks = step("S", 0) + step("S", 1) + step("S", 2) + step("T", 0)
        for i in range(NT):
            for h in range(NH):
                tasks += step("S", i * NH + h + 3) + step("T", i * NH + h + 1)
                if i >= 2:
                    tasks += {0: tail_tasks(i - 2)[7:8], 2: tail_tasks(i - 2)[8:9]}.get(h, [])
                if i:
                    near = tail_tasks(i - 1)
                    tasks += {1: near[0:1], 3: near[1:2], 4: near[2:4], 5: near[4:5], 6: near[5:6], 7: near[6:7]}.get(h, [])
                tasks += [("V", i, h)]
        last = tail_tasks(NT - 1)
        tasks += tail_tasks(NT - 2)[7:8] + last[0:2] + tail_tasks(NT - 2)[8:9] + last[2:]
        orderB = []
        npt = 0
        pt_use = {}
        for t in tasks + tail_tasks(NT):
            if t[0] == "S":
                orderB.append((f"A{t[2] % 2}", t))
            elif t[0] == "T":
                for c in range(0, t[1] + 1, 4):
                    pt_use[t + (c,)] = npt % 2
                    orderB.append((f"PT{npt % 2}", t + (c,)))
                    npt += 1
            elif t[0] == "V":
                if t[2] == 0:
                    orderB.append(("O", ("V", t[1])))
            elif t[0] not in ("SQ", "NM"):
                orderB.append(("M", t))
        orderB.append(("M", "count"))
        P2C = {"SS": 0, "TK0": 5, "TK1": 6, "PV": 7}
        orderC = []
        ntk = 0
        tk_use = {}

        def tk(key):
            nonlocal ntk
            tk_use[key] = ntk % 2
            orderC.append((f"TK{ntk % 2}", key))
            ntk += 1

        def tks(kind, b):
            for c in range({"k": 4, "p": 3, "o": 1}[kind]):
                tk((kind, b, c))

        tks("k", 0)
        orderC.append(("SS", 0))
        tks("k", 1)
        for b in range(SB):
            if b + 1 < SB:
                orderC.append(("SS", b + 1))
            tks("p", b)
            if b:
                tks("o", b - 1)
            if b + 2 < SB:
                tks("k", b + 2)
            orderC.append(("PV", b))
        tks("o", SB - 1)

        filled, emptied, use = {}, {}, {}
        for tag, parts, seq in (("1", PART, order), ("2a", P2A, orderA), ("2b", P2B, orderB), ("2c", P2C, orderC)):
            for q in parts:
                filled[tag + q], emptied[tag + q] = sem(f"filled_{tag}_{q}"), sem(f"emptied_{tag}_{q}")
            seen = {}
            for q, key in seq:
                use[tag, q, key] = seen.get(q, 0)
                seen[q] = seen.get(q, 0) + 1
            use[tag] = seen

        def claim(pe, tag, q, key):
            if use[tag, q, key]:
                pe.wait_ge(emptied[tag + q], use[tag, q, key])

        def settle(pe, tag):
            for q, n in use[tag].items():
                pe.wait_ge(emptied[tag + q], n)

        def take(eng, tag, q, key):
            eng.wait_ge(filled[tag + q], use[tag, q, key] + 1)

        def copied(eng, tag, q, key):
            eng.wait_ge(emptied[tag + q], use[tag, q, key] + 1)

        consts_in = sem("consts_in")
        small_in = sem("small_in")
        w_in_in = [sem(f"w_in_in{c}") for c in range(4)]
        x_in = [sem(f"x_in{s}") for s in range(3)]
        state_in = sem("state_in")
        dve_step, pool_step = sem("dve_step"), sem("pool_step")
        init_done = sem("init_done")
        ssq_ready, std_ready, rstd_ready, xs_ready, xn_ready = sem("ssq_ready"), sem("std_ready"), sem("rstd_ready"), sem("xs_ready"), sem("xn_ready")
        z_ready, kv_out, d_ready, u_out, score_added = sem("z_ready"), sem("kv_out"), sem("d_ready"), sem("u_out"), sem("score_added")
        head_select_in = sem("head_select_in")
        phase1 = sem("phase1_done")
        state_out = sem("state_out")
        wscr_out, wsc_in, pt_in = sem("index_weights_out"), sem("index_weights_in"), sem("page_table_in")
        pidx_ready = sem("page_rows_ready")
        ki_in = [sem(f"ki_in{s}") for s in range(2)]
        far_step, sample_step = sem("far_step"), sem("sample_step")
        sec_done, smask_ready = sem("weighted_done"), sem("smask_ready")
        phase2a = sem("phase2a_done")
        wout_in, rw_in, gb_in = sem("wout_in"), sem("router_in"), sem("ffn_norm_in")
        s_masked, s_exp, av_done = sem("scores_masked"), sem("probs_ready"), sem("values_summed")
        xr_in, h_out, x2_out = ([sem(f"{n}{s}") for s in range(2)] for n in ("residual_in", "h_out", "x2_out"))
        ssq2_ready, std2_ready, x2_ready, A_ready, ASUM_ready = (
            sem("ssq2_ready"), sem("std2_ready"), sem("x2_ready"), sem("A_ready"), sem("ASUM_ready"))
        logits_split, gexp_ready = sem("logits_split"), sem("gexp_ready")
        prompts_done = sem("prompt_tiles_done")
        K_in, V_in = [sem(f"K_in{s}") for s in range(2)], [sem(f"V_in{s}") for s in range(2)]
        masks_ready = sem("prompt_masks_ready")
        Vnew_in = sem("Vnew_in")
        smax_ready, sinv_ready = sem("smax_ready"), sem("sinv_ready")
        toki_ready, slots_cleared, dest_ready, slots_out, slots_in = (
            sem("toki_ready"), sem("slots_cleared"), sem("dest_ready"), sem("slots_out"), sem("slots_in"))
        first_ready, ov_slots = sem("first_slots_ready"), sem("overflow_slots")
        phase2 = sem("phase2_done")
        we_in = [sem(f"expert_weights_in{w}") for w in range(WSLOTS)]
        xg_in, eo_out = ([sem(f"{n}{s}") for s in range(2)] for n in ("xg_in", "eo_out"))
        xT_filled, xT_emptied = [sem(f"xT_filled{c}") for c in range(2)], [sem(f"xT_emptied{c}") for c in range(2)]
        gu_filled, hid_ready = sem("gate_up_filled"), sem("hidden_ready")
        silu_ready = sem("silu_ready")
        dn_filled, dn_emptied = [sem(f"down_filled{c}") for c in range(2)], [sem(f"down_emptied{c}") for c in range(2)]
        ov_w, ov_x, ov_pe, ov_act, ov_dve, ov_out = (sem(f"overflow_{n}") for n in ("weights_in", "rows_in", "pe", "act", "dve", "out"))
        experts_done = sem("experts_done")
        o_in = [sem(f"o_in{s}") for s in range(OQ)]
        hc_in, y_ready, y_out = sem("h_and_norm_in"), sem("y_ready"), sem("y_out")
        ysum_ready, ssq3_ready, std3_ready = sem("ysum_ready"), sem("ssq3_ready"), sem("std3_ready")

        block = ctx.enter_context(nc.Block())

        def tiles_out(eng, sems, n):
            for s in range(2):
                eng.wait_ge(sems[s], 16 * ((n + 1 - s) // 2))

        def rowsof_dram(ap, i):
            return ap[i * P:i * P + rows(i)]

        def dyn(ap, e):
            return ap[e] if isinstance(e, int) else ap[bass.ds(e, 1)].rearrange("a p c n -> (a p) c n")

        def block_rows(e):
            v = eo_dram.rearrange("(b p) n -> b p n", p=CAP)
            return v[e] if isinstance(e, int) else v[bass.ds(e, 1)].rearrange("a p n -> (a p) n")

        def above(e, n):
            return not isinstance(e, int) or e > n

        def pair(q, u):
            return q * (WSLOTS // 2) + u // 2

        def store_y(eng, i):
            eng.wait_ge(y_ready, i + 1)
            eng.dma_start(rowsof(y_rows, i), hc[0:rows(i), i, :]).then_inc(y_out, 16)

        @block.sync
        def _(sp):
            sp.dma_start(con[:, :], const_table).then_inc(consts_in, 16)
            sp.dma_start(gb[:, :], norm_mix_g[0:1, :].partition_broadcast(P)).then_inc(consts_in, 16)
            sp.dma_start(sumA[0:SR, 0:SB * SR], head_select).then_inc(head_select_in, 16)
            sp.dma_start(stt_in[0:SB * HALO, :], state_pool[0].rearrange("b t c -> (b t) c")).then_inc(state_in, 16)

            def rows_in(n):
                sp.dma_start(xb[0:rows(ORDER[n]), n % 3, :], rowsof(x_rows, ORDER[n])).then_inc(x_in[n % 3], 16)

            rows_in(0)
            for c in range(4):
                sp.dma_start(win[:, 2 * c:2 * c + 2, :], w_in_k[:, 2 * c:2 * c + 2, :]).then_inc(w_in_in[c], 16)
                if c == 0:
                    rows_in(1)
            sp.dma_start(pw[:, :, :], pool_w[0].rearrange("g c n -> c g n")).then_inc(small_in, 16)
            sp.dma_start(psc[:, :], pool_scale[0].rearrange("(g c) -> c g", g=4),
                         allow_slow_non_contiguous=True).then_inc(small_in, 16)
            for c in range(SPP):
                sp.dma_start(pt_i[c:P:SPP, :], page_table.rearrange("b j -> j b"),
                             allow_slow_non_contiguous=True).then_inc(pt_in, 16)
            sp.dma_start(pool_sample[0, :, 0:HALO - ST, :], state_pool[0, :, ST:HALO, :]).then_inc(state_out, 16)
            for n in range(2, TILES):
                if n >= 3:
                    take(sp, "1", "T1", ("x", n - 3))
                rows_in(n)
                if n == 2:
                    copied(sp, "1", "KV", 0)
                    sp.dma_start(w_dram, W[0:SR, NT, :]).then_inc(wscr_out, 16)
                    sp.wait_ge(wscr_out, 16)
                    for h in range(NH):
                        sp.dma_start(wsc[h * ST:(h + 1) * ST, :], w_dram.rearrange("(b t) h -> h t b", t=ST)[h],
                                     allow_slow_non_contiguous=True).then_inc(wsc_in, 16)
            sp.wait_ge(phase1, 4)
            sp.dma_start(wout[:, 0:4, :], w_out[0, 0:512, :].rearrange("(g c) n -> c g n", c=P)).then_inc(wout_in, 16)
            for g in range(NKV):
                src = w_out[0, 512 + 256 * g:512 + 256 * g + 256, :].rearrange("(h d) n -> d h n", d=HD)
                sp.dma_start(wout[HD * g:HD * g + HD, 4:8, :], src).then_inc(wout_in, 16)
            sp.dma_start(rw[:, :, 0:NG], router_group_w[0].rearrange("(c p) n -> p c n", p=P)).then_inc(rw_in, 16)
            sp.dma_start(rw[:, :, NG:36], router_expert_w[0].rearrange("(c p) n -> p c n", p=P)).then_inc(rw_in, 16)
            sp.dma_start(bias36[:, 0:NG], router_group_b[0:1, :].partition_broadcast(P)).then_inc(rw_in, 16)
            sp.dma_start(bias36[:, NG:36], router_expert_b[0:1, :].partition_broadcast(P)).then_inc(rw_in, 16)
            sp.dma_start(gb[:, :], norm_ffn_g[0:1, :].partition_broadcast(P)).then_inc(gb_in, 16)
            sp.wait_ge(kv_out, 48 * TILES)
            sp.dma_start(Vnew, v_sample[0].rearrange("b t g d -> t b (g d)")).then_inc(Vnew_in, 16)
            sp.wait_ge(phase2a, 3)

            def tail(i):
                s, r = i % 2, rows(i)
                copied(sp, "2b", "M", ("OP", i, 1))
                sp.dma_start(rowsof_dram(h_dram, i), hb[0:r, s, :]).then_inc(h_out[s], 16)
                sp.wait_ge(x2_ready, i + 1)
                sp.dma_start(rowsof_dram(xn_dram, i), x2[0:r, s, :]).then_inc(x2_out[s], 16)

            def residual(i):
                s, r = i % 2, rows(i)
                if 2 <= i:
                    sp.wait_ge(h_out[s], 16 * (i // 2))
                    sp.wait_ge(x2_ready, i - 1)
                sp.dma_start(hb[0:r, s, :], rowsof(x_rows, i)).then_inc(xr_in[s], 16)

            residual(0)
            residual(1)
            for i in range(NT):
                tail(i)
                if i + 2 < NT:
                    residual(i + 2)

            def weights(e, w):
                for half, src in ((0, gate_k), (1, up_k)):
                    sp.dma_start(wgu[w][:, half], dyn(src, e)).then_inc(we_in[w], 16)
                sp.dma_start(wdn[w][:, :, :], dyn(down_k, e)).then_inc(we_in[w], 16)

            sp.wait_ge(prompts_done, 3)
            weights(0, 0)
            copied(sp, "2c", "PV", SB - 1)

            residual(NT)
            weights(1, 1)
            tail(NT)
            sp.wait_ge(phase2, 4)
            for s in range(2):
                sp.wait_ge(xg_in[s], 16)
            weights(2, 2)
            weights(3, 3)
            with sp.Fori(1, NE // WSLOTS) as q:
                for u in range(WSLOTS):
                    sp.wait_ge(dn_filled[1], q * WSLOTS + (u - WSLOTS + 1))
                    weights(q * WSLOTS + u, u)
            tiles_out(sp, h_out, TILES)
            sp.wait_ge(dest_ready, 1)
            for i in range(TILES):
                sp.dma_start(hc[0:rows(i), i, :], rowsof_dram(h_dram, i)).then_inc(hc_in, 16)
            sp.dma_start(gb[:, :], final_norm_g.rearrange("(a n) -> a n", a=1).partition_broadcast(P)).then_inc(hc_in, 16)
            sp.wait_ge(dn_filled[1], NE)
            sp.wait_ge(dest_ready, 1)
            some = sp.value_load(ovb[0:1, OVB:OVB + 1], min_val=0, max_val=OVB)
            with sp.If(some > 0):
                with sp.Fori(0, OVB) as j:
                    sp.wait_ge(ov_pe, j * 3 + 3)
                    e = sp.value_load(ovb[0:1, bass.ds(j, 1)], min_val=0, max_val=NE - 1)
                    sp.dma_start(wgu[0][:, 0], dyn(gate_k, e)).then_inc(ov_w, 16)
                    sp.dma_start(wgu[0][:, 1], dyn(up_k, e)).then_inc(ov_w, 16)
                    sp.dma_start(wdn[0][:, :, :], dyn(down_k, e)).then_inc(ov_w, 16)
                sp.nop()
            with sp.Else():
                sp.nop()
            for i in range(TILES):
                store_y(sp, i)
            sp.wait_ge(y_out, 16 * TILES)
            sp.wait_ge(state_out, 16)
            sp.wait_ge(u_out, 16 * (SB + 1))

        @block.gpsimd
        def _(pool):
            steps = [0]

            def link(ins):
                steps[0] += 1
                ins.then_inc(pool_step, 1)
                pool.wait_ge(pool_step, steps[0])

            pool.memset(u2[:, 0, :, 0:HALO], 0.0).then_inc(init_done, 1)
            pool.memset(WS[:, :, :], 0.0).then_inc(init_done, 1)
            pool.memset(QB[:, :, :, :, :], 0.0).then_inc(init_done, 1)
            pool.memset(mask[:, 0:3 * P], 0.0).then_inc(init_done, 1)
            pool.wait_ge(consts_in, 32)
            pool.wait_ge(init_done, 4)
            pool.wait_ge(head_select_in, 16)
            link(pool.tensor_copy(selb[0:SR].rearrange("p b r -> p (b r)"), sumA[0:SR, 0:SB * SR]))
            pool.tensor_copy(mask[:, 0:P], const("dmask")).then_inc(init_done, 1)
            pool.tensor_copy(mask[:, 2 * P:3 * P], const("dmask")).then_inc(init_done, 1)

            def norm_weight(n):
                r = rows(ORDER[n])
                pool.wait_ge(xs_ready, n + 1)
                pool.tensor_tensor(xb[0:r, n % 3, :], xb[0:r, n % 3, :], gb[0:r, :], ALU.mult).then_inc(xn_ready, 1)

            def rope(n):
                i = ORDER[n]
                r = rows(i)
                copied(pool, "1", "QI", n)
                z = Z[0:r, 0:19, :]
                c = cs("cos", i, r).unsqueeze(1).broadcast_to([r, 19, ROPE])
                s = cs("sin", i, r).unsqueeze(1).broadcast_to([r, 19, ROPE])
                hf = ROPE // 2
                link(pool.tensor_tensor(rt1[0:r], z[:, :, 0:ROPE], c, ALU.mult))
                link(pool.tensor_tensor(rt2[0:r, :, 0:hf], z[:, :, hf:ROPE], s[:, :, 0:hf], ALU.mult))
                link(pool.tensor_tensor(rt2[0:r, :, hf:ROPE], z[:, :, 0:hf], s[:, :, hf:ROPE], ALU.mult))
                link(pool.tensor_tensor(z[:, :, 0:ROPE], rt1[0:r], rt2[0:r], ALU.add))
                if i == NT:
                    link(pool.tensor_copy(Ztwice[0:r, :, 0, :], Z[0:r, 10:18, :]))
                    link(pool.tensor_copy(Ztwice[0:r, :, 1, :], Z[0:r, 10:18, :]))
                pool.tensor_copy(Z[0:r, 19, :], Z[0:r, 18, :]).then_inc(z_ready, 1)
                pool.dma_start(rowsof(k_rows, i), Z[0:r, 8:10, :].rearrange("p a d -> p (a d)")).then_inc(kv_out, 16)
                pool.dma_start(rowsof(ik_rows, i), Z[0:r, 18, :]).then_inc(kv_out, 16)
                pool.dma_start(rowsof(v_rows, i), V[0:r, i, :]).then_inc(kv_out, 16)

            def pooling(n):
                i = ORDER[n]
                copied(pool, "1", "U", n)
                if i == NT:
                    T = ST + HALO
                    u = uS
                    sa = sumA[:, :].rearrange("p (g b t) -> p g b t", g=4, b=SB)
                    sb_ = sumB[:, :].rearrange("p (g b t) -> p g b t", g=4, b=SB)
                    d = dT[:, 0:4 * SR].rearrange("p (g b t) -> p g b t", g=4, b=SB)
                else:
                    T = P + HALO
                    u = u2[:, i % 2]
                    sa = sumA[:, 0:4 * T].rearrange("p (g t) -> p g t", g=4)
                    sb_ = sumB[:, 0:4 * T].rearrange("p (g t) -> p g t", g=4)
                    d = dT[:, 0:4 * P].rearrange("p (g t) -> p g t", g=4)

                def cutv(v, g, a, b):
                    return v[:, g, :, a:b] if i == NT else v[:, g, a:b]

                g4 = slice(0, 4)
                link(pool.tensor_tensor(cutv(sa, g4, 1, T), cutv(u, g4, 1, T), cutv(u, g4, 0, T - 1), ALU.add))
                g3 = slice(1, 4)
                link(pool.tensor_tensor(cutv(sb_, g3, 3, T), cutv(sa, g3, 3, T), cutv(sa, g3, 1, T - 2), ALU.add))
                g2 = slice(2, 4)
                link(pool.tensor_tensor(cutv(sa, g2, 7, T), cutv(sb_, g2, 7, T), cutv(sb_, g2, 3, T - 4), ALU.add))
                link(pool.tensor_tensor(cutv(sb_, 3, 15, T), cutv(sa, 3, 15, T), cutv(sa, 3, 7, T - 8), ALU.add))
                if n:
                    take(pool, "1", "T1", ("pool", n - 1))
                for g, w in enumerate(WINDOWS):
                    src = (sa, sb_, sa, sb_)[g]
                    if i == NT:
                        link(pool.tensor_scalar(d[:, g], cutv(src, g, HALO, T), 1.0 / w, None, ALU.mult))
                    elif i:
                        link(pool.tensor_scalar(d[:, g, :], src[:, g, HALO:T], 1.0 / w, None, ALU.mult))
                    else:
                        lo = CC["pinv"][0] + 16 * g
                        pool.tensor_tensor(d[:, g, 0:16], src[:, g, HALO:HALO + 16], con[:, lo:lo + 16], ALU.mult)
                        link(pool.tensor_scalar(d[:, g, 16:P], src[:, g, HALO + 16:T], 1.0 / w, None, ALU.mult))
                pool.tensor_tensor(d, d, cutv(u, g4, HALO, T), ALU.subtract).then_inc(d_ready, 1)

            def index_keys(b):
                if b >= 2:
                    take(pool, "2a", "TR", (b - 2, 1))
                pool.indirect_dma_start(kin[:, b % 2].rearrange("p s d -> p (s d)"), None, ci_rows,
                                        bass.IndirectOffsetOnAxis(ap=pidx[:, b:b + 1], axis=0)).then_inc(ki_in[b % 2], 16)

            norm_weight(0)
            norm_weight(1)
            for n in range(TILES):
                rope(n)
                pooling(n)
                if n + 2 < TILES:
                    norm_weight(n + 2)
                if n == 0:
                    pool.wait_ge(pt_in, 16 * SPP)
                    pool.tensor_scalar(pidx, pt_i, float(SPP), const("pmod")[:, 0:1], ALU.mult, ALU.add).then_inc(pidx_ready, 1)
                if n == 4:
                    pool.wait_ge(pidx_ready, 1)
                    index_keys(0)
                    index_keys(1)
            pool.wait_ge(wsc_in, 16 * NH)
            for b in range(SB):
                link(pool.tensor_scalar(WS[0:SR, b, b * ST:(b + 1) * ST], const("diag", SR), wsc[:, b:b + 1], None, ALU.mult))
            for g in range(NKV):
                q0 = qT[HD * g:HD * (g + 1), :, SEQ:NTOK].rearrange("p h (b t) -> p b h t", b=SB)
                link(pool.tensor_copy(QB[HD * g:HD * (g + 1), :, g, :, :], q0))
            pool.wait_ge(kv_out, 48 * TILES)
            pool.drain().then_inc(phase1, 1)

            pool.wait_ge(phase1, 4)
            for b in range(2, SB):
                index_keys(b)
            zero = zslots[:, 0:NBLK * CAP // P * 16]
            link(pool.memset(zslots, 0))
            pool.dma_start(slot_dram[0:NBLK * CAP].rearrange("(p c) k -> p (c k)", p=P), zero).then_inc(slots_cleared, 16)
            per = OVB * CAP * D // (P * 512)
            pool.dma_start(eo_dram[NE * CAP:NBLK * CAP, :].rearrange("(p c) n -> p (c n)", p=P).rearrange("p (c n) -> p c n", c=per),
                           zslots.bitcast(F32)[:, 0:512].unsqueeze(1).broadcast_to([P, per, 512])).then_inc(slots_cleared, 16)
            pool.iota(toki[:, :, :], pattern=[[P, TILES], [0, 16]], base=0, channel_multiplier=1).then_inc(toki_ready, 1)
            pool.wait_ge(slots_cleared, 32)
            for s in range(2):
                pool.wait_ge(ki_in[s], 16 * SB // 2)
            pool.drain().then_inc(phase2a, 1)
            def past(buf, src, b, arrived):
                pool.indirect_dma_start(buf[b % 2].rearrange("p s d -> p (s d)"), None, src,
                                        bass.IndirectOffsetOnAxis(ap=pidx[:, b:b + 1], axis=0)).then_inc(arrived[b % 2], 16)

            def scatter(i):
                r = rows(i)
                pool.wait_ge(first_ready, i + 1)
                for k in range(2):
                    pool.indirect_dma_start(slot_dram, bass.IndirectOffsetOnAxis(ap=first[0:r, i, k:k + 1], axis=0),
                                            toki[0:r, i, :], None).then_inc(slots_out, 16)

            pool.wait_ge(masks_ready, 1)
            past(Kin, ck_rows, 0, K_in)
            past(Vin, cv_rows, 0, V_in)
            for i in range(NT):
                scatter(i)
            pool.wait_ge(prompts_done, 3)
            tiles_out(pool, h_out, NT)
            tiles_out(pool, x2_out, NT)
            past(Kin, ck_rows, 1, K_in)
            past(Vin, cv_rows, 1, V_in)
            for b in range(2, SB):
                take(pool, "2c", f"TK{tk_use['k', b - 2, 3]}", ("k", b - 2, 3))
                past(Kin, ck_rows, b, K_in)
                take(pool, "2c", "PV", b - 2)
                past(Vin, cv_rows, b, V_in)
            scatter(NT)
            pool.wait_ge(slots_out, 16 * 2 * TILES)
            pool.dma_start(slot_tok[0:CAP, 0:NE].bitcast(I32), slot_dram[0:NE * CAP, 0:1].rearrange("(c p) k -> p (c k)", p=CAP),
                           allow_slow_non_contiguous=True).then_inc(slots_in, 16)
            pool.wait_ge(slots_in, 16)
            tiles_out(pool, x2_out, TILES)
            pool.drain().then_inc(phase2, 1)
            pool.wait_ge(phase2, 4)

            for e in range(NE):
                s = e % 2
                if e >= 2:
                    pool.wait_ge(xT_filled[1], e - 1)
                pool.indirect_dma_start(xg[0:CAP, s, :], None, xn_dram,
                                        bass.IndirectOffsetOnAxis(ap=slot_tok[0:CAP, e:e + 1], axis=0)).then_inc(xg_in[s], 16)
            pool.wait_ge(dn_filled[1], NE)
            pool.wait_ge(dest_ready, 1)
            some = pool.value_load(ovb[0:1, OVB:OVB + 1], min_val=0, max_val=OVB)
            with pool.If(some > 0):
                for i in range(TILES):
                    r = rows(i)
                    for k in range(2):
                        pool.indirect_dma_start(slot_dram, bass.IndirectOffsetOnAxis(ap=dest[0:r, i, k:k + 1], axis=0),
                                                toki[0:r, i, :], None).then_inc(ov_slots, 16)
                pool.wait_ge(ov_slots, 16 * 2 * TILES)
                pool.dma_start(slot_tok[0:CAP, NE:NBLK].bitcast(I32),
                               slot_dram[NE * CAP:NBLK * CAP, 0:1].rearrange("(c p) k -> p (c k)", p=CAP),
                               allow_slow_non_contiguous=True).then_inc(ov_slots, 16)
                pool.wait_ge(ov_slots, 16 * 2 * TILES + 16)
                for j in range(OVB):
                    if j:
                        pool.wait_ge(ov_pe, 3 * j + 3)
                    pool.indirect_dma_start(xg[0:CAP, 0, :], None, xn_dram,
                                            bass.IndirectOffsetOnAxis(ap=slot_tok[0:CAP, NE + j:NE + j + 1], axis=0)).then_inc(ov_x, 16)
                pool.nop()
            with pool.Else():
                pool.nop()
            pool.wait_ge(experts_done, 1)
            for i in range(TILES):
                s, r = i % OSLOTS, rows(i)
                if i >= OQ:
                    pool.wait_ge(o_in[i % OQ], 32 * (i // OQ))
                if i >= OSLOTS:
                    pool.wait_ge(ysum_ready, 2 * (i - OSLOTS + 1))
                for k, o in ((0, o1), (1, o2)):
                    pool.indirect_dma_start(o[0:r, s, :], None, eo_dram,
                                            bass.IndirectOffsetOnAxis(ap=dest[0:r, i, k:k + 1], axis=0)).then_inc(o_in[i % OQ], 16)

        @block.tensor
        def _(pe):
            mm = nc.tensor.matmul
            tr = nc.tensor.transpose

            def x_turn(n):
                r = rows(ORDER[n])
                pe.wait_ge(xn_ready, n + 1)
                for c in range(2):
                    claim(pe, "1", f"T{c}", ("x", n))
                    for j in range(4):
                        ins = tr(ps[:, c, j * P:j * P + r], xb[0:r, n % 3, 4 * c + j:D:KC], ident(r))
                    ins.then_inc(filled[f"1T{c}"], 1)

            def project(n):
                i = ORDER[n]
                r = rows(i)
                s = n % 2
                for c in range(2):
                    copied(pe, "1", f"T{c}", ("x", n))
                claim(pe, "1", "U", n)
                for g in range(4):
                    for k in range(KC):
                        if n == 0 and g == 0 and k % 2 == 0:
                            pe.wait_ge(w_in_in[k // 2], 16)
                        ins = mm(ps[:, PART["U"], g * r:(g + 1) * r], win[:, k, g * P:(g + 1) * P], xnT[:, s, k, 0:r],
                                 start=(k == 0), stop=(k == KC - 1))
                ins.then_inc(filled["1U"], 1)
                for part, spans in (("Q", ((CQ, CK, 0),)), ("KV", ((CK, CQI, 0), (CKI, NIN, CQI - CK))), ("QI", ((CQI, CKI, 0),))):
                    claim(pe, "1", part, n)
                    for a, b, o in spans:
                        for k in range(KC):
                            ins = mm(ps[0:r, PART[part], o:o + b - a], xnT[:, s, k, 0:r], win[:, k, a:b],
                                     start=(k == 0), stop=(k == KC - 1))
                    ins.then_inc(filled["1" + part], 1)

            def z_turn(n):
                i = ORDER[n]
                r = rows(i)
                pe.wait_ge(z_ready, n + 1)
                claim(pe, "1", "T0", ("q", n))
                for c in range(4):
                    ins = tr(ps[:, 0, c * r:(c + 1) * r], Z[0:r, 2 * c:2 * c + 2, :].rearrange("p a d -> p (a d)"), ident(r))
                ins.then_inc(filled["1T0"], 1)
                claim(pe, "1", "T1", ("qi", n))
                if i == NT:
                    for h in range(NH):
                        ins = tr(ps[:, 1, h * r:(h + 1) * r], Ztwice[0:r, h].rearrange("p a d -> p (a d)"), ident(r))
                else:
                    for c in range(4):
                        ins = tr(ps[:, 1, c * r:(c + 1) * r], Z[0:r, 10 + 2 * c:12 + 2 * c, :].rearrange("p a d -> p (a d)"), ident(r))
                ins.then_inc(filled["1T1"], 1)
                claim(pe, "1", "T0", ("k", n))
                for c, z0 in ((0, 8), (1, 18)):
                    ins = tr(ps[:, 0, c * r:(c + 1) * r], Z[0:r, z0:z0 + 2, :].rearrange("p a d -> p (a d)"), ident(r))
                ins.then_inc(filled["1T0"], 1)

            def pool_out(n):
                r = rows(ORDER[n])
                if n == 0:
                    pe.wait_ge(small_in, 32)
                pe.wait_ge(d_ready, n + 1)
                claim(pe, "1", "T1", ("pool", n))
                for g in range(4):
                    ins = mm(ps[:, 1, g * r:(g + 1) * r], pw[:, g, :], dT[:, g * r:(g + 1) * r], start=True, stop=True)
                ins.then_inc(filled["1T1"], 1)

            def u_turn(n):
                claim(pe, "1", "T0", ("u", n))
                for g in range(4):
                    if ORDER[n] == NT:
                        ins = tr(ps[0:SR, 0, g * P:(g + 1) * P], uC[:, g, :], ident(P))
                    else:
                        ins = tr(ps[0:HALO, 0, g * P:(g + 1) * P], u2[:, ORDER[n] % 2, g, P:P + HALO], ident(P))
                ins.then_inc(filled["1T0"], 1)

            def scores(n):
                i = ORDER[n]
                copied(pe, "1", "T1", ("qi", n))
                copied(pe, "1", "T0", ("k", n))
                for m, lo, w, h in score_steps[n]:
                    hf = HD * (h % 2)
                    claim(pe, "1", f"S{m % 2}", ("s", m))
                    mm(ps[:, 6 + m % 2, 0:w], qiT[hf:hf + HD, i % 2, h // 2, :], kiT[hf:hf + HD, lo:lo + w],
                       start=True, stop=True).then_inc(filled[f"1S{m % 2}"], 1)

            pe.wait_ge(consts_in, 32)
            pe.wait_ge(state_in, 16)
            claim(pe, "1", "T0", "state")
            for g in range(4):
                ins = tr(ps[:, 0, g * SB * HALO:(g + 1) * SB * HALO], stt_in[0:SB * HALO, g * P:(g + 1) * P], ident(SB * HALO))
            ins.then_inc(filled["1T0"], 1)
            x_turn(0)
            for n in range(TILES + 1):
                if n < TILES:
                    project(n)
                if n + 1 < TILES:
                    x_turn(n + 1)
                if n:
                    z_turn(n - 1)
                    pool_out(n - 1)
                    if n - 1 in (0, TILES - 1):
                        u_turn(n - 1)
                    if score_steps[n - 1]:
                        scores(n - 1)
            settle(pe, "1")
            pe.drain().then_inc(phase1, 1)
            pe.wait_ge(phase1, 4)


            def ki_turn(b):
                pe.wait_ge(ki_in[b % 2], 16 * (b // 2 + 1))
                for c in range(2):
                    claim(pe, "2a", "TR", (b, c))
                    for j in range(4):
                        a = 2 * (4 * c + j)
                        ins = tr(ps[:, 5, j * P:(j + 1) * P], kin[:, b % 2, a:a + 2, :].rearrange("p s d -> p (s d)"), ident(P))
                    ins.then_inc(filled["2aTR"], 1)

            def s_scores(b):
                copied(pe, "2a", "TR", (b, 1))
                for q in range(5):
                    part = (5 * b + q) % 2
                    claim(pe, "2a", f"PS{part}", (b, q))
                    if q < 4:
                        c, sp_ = q // 2, q % 2
                        hf = HD * sp_
                        mm(ps[0:SR, 6 + part, :], QS[hf:hf + HD, b].rearrange("p h t -> p (h t)"),
                           kiTs[hf:hf + HD, b % 2, 4 * c:4 * c + 4, :].rearrange("p j k -> p (j k)"),
                           start=True, stop=True).then_inc(filled[f"2aPS{part}"], 1)
                    else:
                        mm(ps[0:SR, 6 + part, 0:ST], QS[0:HD, b].rearrange("p h t -> p (h t)"),
                           kiT[0:HD, SEQ + b * ST:SEQ + (b + 1) * ST], start=True, stop=True).then_inc(filled[f"2aPS{part}"], 1)

            def weighted(b):
                for q in range(5):
                    copied(pe, "2a", f"PS{(5 * b + q) % 2}", (b, q))
                for q in range(5):
                    w = 512 if q < 4 else ST
                    ins = mm(ps[0:SR, q, 0:w], WS[0:SR, b, :], rs[0:SR, b % 2, 512 * q:512 * q + w],
                             start=(b == 0), stop=(b == SB - 1))
                ins.then_inc(sec_done, 1)
                if b == SB - 1:
                    pe.wait_ge(sec_done, SB)
                    pe.nop().then_inc(filled["2aACC"], 1)

            ki_turn(0)
            for b in range(SB):
                s_scores(b)
                if b + 1 < SB:
                    ki_turn(b + 1)
                if b:
                    weighted(b - 1)
            weighted(SB - 1)
            settle(pe, "2a")
            pe.drain().then_inc(phase2a, 1)
            pe.wait_ge(phase2a, 3)

            def q_k(i, h):
                part = h % 2
                g, w = h // GH, P * (i + 1)
                claim(pe, "2b", f"A{part}", ("S", i, h))
                for lo in range(0, w, 512):
                    e = min(512, w - lo)
                    ins = mm(ps[:, 2 * part + lo // 512, 0:e], qT[HD * g:HD * (g + 1), h % GH, i * P:(i + 1) * P],
                             kT[HD * g:HD * (g + 1), lo:lo + e], start=True, stop=True)
                ins.then_inc(filled[f"2bA{part}"], 1)

            def p_turn(i, h):
                pe.wait_ge(s_exp, i * NH + h + 1)
                for c in range(0, i + 1, 4):
                    part = pt_use["T", i, h, c]
                    claim(pe, "2b", f"PT{part}", ("T", i, h, c))
                    for j in range(c, min(c + 4, i + 1)):
                        ins = tr(ps[:, 4 + part, (j - c) * P:(j - c + 1) * P], Sm[:, (i * NH + h) % 3, j * P:(j + 1) * P], ident(P))
                    ins.then_inc(filled[f"2bPT{part}"], 1)

            def p_v(i, h):
                if h == 0:
                    claim(pe, "2b", "O", ("V", i))
                g = h // GH
                for c in range(0, i + 1, 4):
                    copied(pe, "2b", f"PT{pt_use['T', i, h, c]}", ("T", i, h, c))
                for j in range(i + 1):
                    ins = mm(ps[:, 6, h * HD:(h + 1) * HD], PT[:, h % 2, j, :], V[:, j, g * HD:(g + 1) * HD],
                             start=(j == 0), stop=(j == i))
                ins.then_inc(av_done, 1)
                if h == NH - 1:
                    pe.wait_ge(av_done, (i + 1) * NH)
                    pe.nop().then_inc(filled["2bO"], 1)

            def tail(t):
                kind, i = t[0], t[1]
                r = rows(i)
                tok = slice(i * P, i * P + r)
                if kind in ("SQ", "NM"):
                    return
                claim(pe, "2b", "M", t)
                if kind == "OT":
                    copied(pe, "2b", "O", ("V", i))
                    for c in range(4):
                        ins = tr(ps[:, 7, c * P:(c + 1) * P], Osb[:, c * P:(c + 1) * P], ident(P))
                elif kind == "OP":
                    if t[2] == 0:
                        if i < NT:
                            copied(pe, "2b", "M", ("OT", i))
                        if i == 0:
                            pe.wait_ge(wout_in, 48)
                    for k in range(8):
                        if k < 4:
                            lhs = mixP[:, k, tok]
                        else:
                            lhs = mixS[:, k - 4, :] if i == NT else mixA[:, k - 4, :]
                        ins = mm(ps[0:r, 7, :], lhs, wout[:, k, 512 * t[2]:512 * t[2] + 512], start=(k == 0), stop=(k == 7))
                elif kind == "XR":
                    pe.wait_ge(x2_ready, i + 1)
                    for j in range(4):
                        c = 4 * t[2] + j
                        ins = tr(ps[:, 7, j * r:(j + 1) * r], x2[0:r, i % 2, c * P:(c + 1) * P], ident(r))
                elif kind == "LG":
                    copied(pe, "2b", "M", ("XR", i, 1))
                    if i == 0:
                        pe.wait_ge(rw_in, 64)
                    for k in range(KC):
                        ins = mm(ps[0:r, 7, 0:36], x2T[:, k, 0:r], rw[:, k, :], start=(k == 0), stop=(k == KC - 1))
                elif kind == "RK":
                    pe.wait_ge(A_ready, i + 1)
                    mm(ps[0:r, 7, 0:NE], const("tri")[0:r, 0:r], A[0:r, :], start=True, stop=False)
                    ins = mm(ps[0:r, 7, 0:NE], const("ones")[:, 0:r], ASUM[:, :], start=False, stop=True)
                ins.then_inc(filled["2bM"], 1)

            for t in tasks:
                if t[0] == "S":
                    q_k(t[1], t[2])
                elif t[0] == "T":
                    p_turn(t[1], t[2])
                elif t[0] == "V":
                    p_v(t[1], t[2])
                else:
                    tail(t)
            for q in ("A0", "A1", "PT0", "PT1", "O"):
                pe.wait_ge(emptied["2b" + q], use["2b"][q])
            pe.wait_ge(emptied["2bM"], use["2b", "M", ("OP", NT, 0)])
            pe.drain().then_inc(prompts_done, 1)
            pe.wait_ge(prompts_done, 3)

            pe.wait_ge(smask_ready, 1)
            pe.wait_ge(Vnew_in, 16)

            def keys(b):
                s = b % 2
                pe.wait_ge(K_in[s], 16 * (b // 2 + 1))
                for c in range(4):
                    part = tk_use["k", b, c]
                    claim(pe, "2c", f"TK{part}", ("k", b, c))
                    for j in range(4):
                        ins = tr(ps[:, 5 + part, j * P:(j + 1) * P], Kin[s][:, 4 * c + j, :], ident(P))
                    ins.then_inc(filled[f"2cTK{part}"], 1)

            def scores_of(b):
                claim(pe, "2c", "SS", b)
                smv = smask[0:SR, 0:PAST].rearrange("r (p s) -> r s p", s=SLOTS)
                lhs = QB[:, b].rearrange("p g h t -> p (g h t)")
                for q in range(5):
                    c = min(q, 3)
                    copied(pe, "2c", f"TK{tk_use['k', b, c]}", ("k", b, c))
                    if q < 4:
                        mm(ps[0:SR, q, :], lhs, KTs[:, 512 * q:512 * (q + 1)], start=True, stop=False)
                        mm(ps[0:SR, q, :], selb[0:SR, b, :], smv[:, 4 * q:4 * q + 4, :], start=False, stop=True)
                    else:
                        mm(ps[0:SR, 4, 0:ST], lhs, kT[:, SEQ + b * ST:SEQ + (b + 1) * ST], start=True, stop=False)
                        ins = mm(ps[0:SR, 4, 0:ST], selb[0:SR, b, :], smask[0:SR, PAST:LS], start=False, stop=True)
                ins.then_inc(filled["2cSS"], 1)

            def probs_turn(b):
                copied(pe, "2c", "SS", b)
                for c in range(3):
                    part = tk_use["p", b, c]
                    claim(pe, "2c", f"TK{part}", ("p", b, c))
                    if c < 2:
                        for j in range(8):
                            a = 8 * c + j
                            ins = tr(ps[:, 5 + part, j * SR:(j + 1) * SR], Ps[0:SR, a * P:(a + 1) * P], ident(SR))
                    else:
                        ins = tr(ps[0:ST, 5 + part, 0:SR], Ps[0:SR, PAST:LS], ident(SR))
                    ins.then_inc(filled[f"2cTK{part}"], 1)

            def values(b):
                claim(pe, "2c", "PV", b)
                pe.wait_ge(V_in[b % 2], 16 * (b // 2 + 1))
                for c in range(3):
                    copied(pe, "2c", f"TK{tk_use['p', b, c]}", ("p", b, c))
                for a in range(SLOTS):
                    mm(ps[0:SR, 7, 0:P], PTs[:, a, :], Vin[b % 2][:, a, :], start=(a == 0), stop=False)
                mm(ps[0:SR, 7, 0:P], PTs[0:ST, SLOTS, :], Vnew[:, b, :], start=False, stop=True).then_inc(filled["2cPV"], 1)

            def out_turn(b):
                part = tk_use["o", b, 0]
                copied(pe, "2c", "PV", b)
                claim(pe, "2c", f"TK{part}", ("o", b, 0))
                tr(ps[:, 5 + part, 0:SR], Os[0:SR, :], ident(SR)).then_inc(filled[f"2cTK{part}"], 1)

            keys(0)
            scores_of(0)
            keys(1)
            for b in range(SB):
                if b + 1 < SB:
                    scores_of(b + 1)
                probs_turn(b)
                if b:
                    out_turn(b - 1)
                if b + 2 < SB:
                    keys(b + 2)
                values(b)
            out_turn(SB - 1)
            settle(pe, "2c")
            for t in tail_tasks(NT):
                tail(t)
            claim(pe, "2b", "M", "count")
            pe.wait_ge(ASUM_ready, TILES)
            mm(ps[:, 7, 0:NE], const("ones"), ASUM[:, :], start=True, stop=True).then_inc(filled["2bM"], 1)
            settle(pe, "2b")
            pe.drain().then_inc(phase2, 1)
            pe.wait_ge(phase2, 4)

            def turn_rows(s, c):
                for j in range(4):
                    ins = tr(ps[:, c, j * CAP:(j + 1) * CAP], xg[0:CAP, s, 4 * c + j:D:KC], ident(CAP))
                return ins

            def products(s, w):
                for j in range(4):
                    for k in range(KC):
                        ins = mm(ps[:, 2 + s, j * CAP:(j + 1) * CAP], wgu[w][:, j // 2, k, (j % 2) * P:(j % 2 + 1) * P],
                                 xgT[:, s, k, :], start=(k == 0), stop=(k == KC - 1))
                return ins

            def down_half(s, w, c):
                for k in range(2):
                    ins = mm(ps[0:CAP, 5 + c, :], hT[:, s, k, :], wdn[w][:, k, 512 * c:512 * (c + 1)], start=(k == 0), stop=(k == 1))
                return ins

            def rows_turn(q, u):
                e, s = q * WSLOTS + u, u % 2
                pe.wait_ge(xg_in[s], pair(q, u) * 16 + 16)
                for c in range(2):
                    if above(e, 0):
                        pe.wait_ge(xT_emptied[c], e)
                    turn_rows(s, c).then_inc(xT_filled[c], 1)

            def gate_up(q, u):
                e, s = q * WSLOTS + u, u % 2
                pe.wait_ge(we_in[u], q * 48 + 48)
                for c in range(2):
                    pe.wait_ge(xT_emptied[c], e + 1)
                if above(e, 1):
                    pe.wait_ge(hid_ready, q * WSLOTS + (u - 1))
                products(s, u).then_inc(gu_filled, 1)

            def down(q, u):
                e, s = q * WSLOTS + u, u % 2
                pe.wait_ge(hid_ready, e + 1)
                for c in range(2):
                    if above(e, 0):
                        pe.wait_ge(dn_emptied[c], e)
                    down_half(s, u, c).then_inc(dn_filled[c], 1)

            def experts(q, last=False):
                for u in range(WSLOTS):
                    gate_up(q, u)
                    if u < WSLOTS - 1:
                        rows_turn(q, u + 1)
                    elif not last:
                        rows_turn(q + 1, 0)
                    down(q, u)

            rows_turn(0, 0)
            experts(0)
            with pe.Fori(1, NE // WSLOTS - 1) as q:
                experts(q)
            experts(NE // WSLOTS - 1, last=True)

            pe.wait_ge(dn_emptied[0], NE)
            pe.wait_ge(dn_emptied[1], NE)
            pe.wait_ge(dest_ready, 1)
            some = pe.value_load(ovb[0:1, OVB:OVB + 1], min_val=0, max_val=OVB)
            with pe.If(some > 0):
                pe.nop().then_inc(ov_pe, 3)
                with pe.Fori(0, OVB) as j:
                    pe.wait_ge(ov_x, j * 16 + 16)
                    pe.wait_ge(ov_dve, j * 3 + 3)
                    turn_rows(0, 0)
                    turn_rows(0, 1).then_inc(ov_pe, 1)
                    pe.wait_ge(ov_w, j * 48 + 48)
                    pe.wait_ge(ov_dve, j * 3 + 4)
                    products(0, 0).then_inc(ov_pe, 1)
                    pe.wait_ge(ov_dve, j * 3 + 5)
                    down_half(0, 0, 0)
                    down_half(0, 0, 1).then_inc(ov_pe, 1)
                pe.nop()
            with pe.Else():
                pe.nop()

        @block.scalar
        def _(act):
            fn = nc.scalar.activation

            def copy(out, in_, scale=1.0):
                return fn(out, in_, ACT.Copy, scale=scale)

            def four(v, r):
                return v[:, 0:4 * r].rearrange("p (g t) -> p g t", g=4)

            def root(n):
                r = rows(ORDER[n])
                act.wait_ge(ssq_ready, n + 1)
                fn(std[0:r, n:n + 1], ssq[0:r, n:n + 1], ACT.Sqrt, scale=1.0 / D, bias=const("eps", r)).then_inc(std_ready, 1)

            def scale_rows(n):
                r = rows(ORDER[n])
                act.wait_ge(rstd_ready, n + 1)
                copy(xb[0:r, n % 3, :], xb[0:r, n % 3, :], scale=rstd[0:r, n:n + 1]).then_inc(xs_ready, 1)

            def keep_xT(n):
                r = rows(ORDER[n])
                for c in range(2):
                    take(act, "1", f"T{c}", ("x", n))
                    copy(xnT[:, n % 2, 4 * c:4 * c + 4, 0:r], ps[:, c, :].rearrange("p (g t) -> p g t", g=4)[:, :, 0:r])\
                        .then_inc(emptied[f"1T{c}"], 1)

            def keep_u(n):
                i = ORDER[n]
                r = rows(i)
                take(act, "1", "U", n)
                if n >= 2:
                    act.wait_ge(d_ready, n - 1)
                u = four(ps[:, PART["U"], :], r)
                if i == NT:
                    copy(uC, u)
                    copy(uS[:, :, :, HALO:HALO + ST], u.rearrange("p g (b t) -> p g b t", b=SB)).then_inc(emptied["1U"], 1)
                else:
                    if i:
                        act.wait_ge(emptied["1U"], n)
                        copy(u2[:, i % 2, :, 0:HALO], u2[:, (i - 1) % 2, :, P:P + HALO])
                    else:
                        act.wait_ge(init_done, 4)
                    copy(u2[:, i % 2, :, HALO:HALO + P], u).then_inc(emptied["1U"], 1)

            def keep_rows(n):
                i = ORDER[n]
                r = rows(i)
                if n:
                    act.wait_ge(kv_out, 48 * n)
                    take(act, "1", "T0", ("k", n - 1))
                take(act, "1", "Q", n)
                copy(Z[0:r, 0:8, :].rearrange("p (b g) d -> p g b d", g=NKV),
                     ps[0:r, PART["Q"], :].rearrange("p (g b d) -> p g b d", g=NKV, b=GH)).then_inc(emptied["1Q"], 1)
                take(act, "1", "KV", n)
                kv = ps[0:r, PART["KV"], :]
                copy(Z[0:r, 8:10, :].rearrange("p a d -> p (a d)"), kv[:, 0:P])
                copy(V[0:r, i, :], kv[:, P:2 * P])
                copy(Z[0:r, 18, :], kv[:, 2 * P:2 * P + HD])
                copy(W[0:r, i, :], kv[:, 2 * P + HD:2 * P + HD + NH], scale=(NH ** -0.5) * (HD ** -0.5)).then_inc(emptied["1KV"], 1)
                take(act, "1", "QI", n)
                copy(Z[0:r, 10:18, :].rearrange("p a d -> p (a d)"), ps[0:r, PART["QI"], :]).then_inc(emptied["1QI"], 1)

            def keep_z(n):
                i = ORDER[n]
                r = rows(i)
                tok = slice(i * P, i * P + r)
                take(act, "1", "T0", ("q", n))
                copy(qT[:, :, tok], four(ps[:, 0, :], r)).then_inc(emptied["1T0"], 1)
                take(act, "1", "T1", ("qi", n))
                if i == NT:
                    copy(QS[:, :, :, :].rearrange("p b h t -> p h b t"), ps[:, 1, :].rearrange("p (h b t) -> p h b t", h=NH, b=SB)).then_inc(emptied["1T1"], 1)
                else:
                    copy(qiT[:, i % 2], four(ps[:, 1, :], r)).then_inc(emptied["1T1"], 1)
                take(act, "1", "T0", ("k", n))
                copy(kT[:, tok], ps[:, 0, 0:r])
                copy(kiT[:, tok], ps[:, 0, r:2 * r]).then_inc(emptied["1T0"], 1)
                take(act, "1", "T1", ("pool", n))
                if n == 0:
                    act.wait_ge(small_in, 32)
                for g in range(4):
                    ins = copy(mixP[:, g, tok], ps[:, 1, g * r:(g + 1) * r], scale=psc[:, g:g + 1])
                ins.then_inc(emptied["1T1"], 1)
                if n == 0:
                    take(act, "1", "T0", ("u", n))
                    copy(stt_in[0:SR, :], ps[0:SR, 0, :]).then_inc(emptied["1T0"], 1)
                    copied(act, "1", "T0", ("u", n))
                    for b in range(SB):
                        act.dma_start(pool_sample[0, b, HALO - ST:HALO, :], stt_in[b * ST:(b + 1) * ST, :]).then_inc(u_out, 16)
                if n == TILES - 1:
                    take(act, "1", "T0", ("u", n))
                    act.wait_ge(u_out, 16 * SB)
                    copy(stt_in[0:HALO, :], ps[0:HALO, 0, :]).then_inc(emptied["1T0"], 1)
                    copied(act, "1", "T0", ("u", n))
                    act.dma_start(pool_prompt[0, 0], stt_in[0:HALO, :]).then_inc(u_out, 16)
                    act.wait_ge(u_out, 16 * (SB + 1))

            def relus(n):
                for m, lo, w, h in score_steps[n]:
                    take(act, "1", f"S{m % 2}", ("s", m))
                    if m >= 2:
                        act.wait_ge(score_added, m - 1)
                    fn(rl[:, m % 2, 0:w], ps[:, 6 + m % 2, 0:w], ACT.Relu).then_inc(emptied[f"1S{m % 2}"], 1)

            act.wait_ge(consts_in, 32)
            take(act, "1", "T0", "state")
            copy(uS[:, :, :, 0:HALO], ps[:, 0, 0:4 * SB * HALO].rearrange("p (g b t) -> p g b t", g=4, b=SB))\
                .then_inc(emptied["1T0"], 1)
            for n in range(2):
                root(n)
                scale_rows(n)
            keep_xT(0)
            for n in range(TILES + 1):
                if n + 2 < TILES:
                    root(n + 2)
                if n + 1 < TILES:
                    keep_xT(n + 1)
                if n + 2 < TILES:
                    scale_rows(n + 2)
                if n < TILES:
                    keep_u(n)
                if n:
                    keep_z(n - 1)
                if n < TILES:
                    keep_rows(n)
                if n:
                    relus(n - 1)
            act.drain().then_inc(phase1, 1)
            act.wait_ge(phase1, 4)

            def keep_ki(b):
                for c in range(2):
                    take(act, "2a", "TR", (b, c))
                    copy(kiTs[:, b % 2, 4 * c:4 * c + 4, :], four(ps[:, 5, :], P)).then_inc(emptied["2aTR"], 1)

            keep_ki(0)
            for b in range(SB):
                for q in range(5):
                    part, w = (5 * b + q) % 2, 512 if q < 4 else ST
                    take(act, "2a", f"PS{part}", (b, q))
                    if b >= 2 and q == 0:
                        act.wait_ge(sec_done, b - 1)
                    fn(rs[0:SR, b % 2, 512 * q:512 * q + w], ps[0:SR, 6 + part, 0:w], ACT.Relu).then_inc(emptied[f"2aPS{part}"], 1)
                if b + 1 < SB:
                    keep_ki(b + 1)
            take(act, "2a", "ACC", 0)
            inorder = SCs[0:SR, 0:PAST].rearrange("r (p s) -> r s p", s=SLOTS)
            for q in range(4):
                a = 8 * (q // 2) + q % 2
                copy(inorder[:, a:a + 7:2, :], ps[0:SR, q, :].rearrange("r (s p) -> r s p", s=4))
            copy(SCs[0:SR, PAST:LS], ps[0:SR, 4, 0:ST]).then_inc(emptied["2aACC"], 1)
            act.drain().then_inc(phase2a, 1)
            act.wait_ge(phase2a, 3)

            def tail(t):
                kind, i = t[0], t[1]
                r, s = rows(i), i % 2
                if kind == "OT":
                    take(act, "2b", "M", t)
                    copy(mixA[:, :, :], four(ps[:, 7, :], P)).then_inc(emptied["2bM"], 1)
                elif kind == "SQ":
                    copied(act, "2b", "M", ("OP", i, 1))
                    if i >= 2:
                        act.wait_ge(x2_out[s], 16 * (i // 2))
                        take(act, "2b", "M", ("XR", i - 2, 1))
                    fn(x2[0:r, s, :], hb[0:r, s, :], ACT.Square, accum_out=ssq2[0:r, i:i + 1]).then_inc(ssq2_ready, 1)
                    act.wait_ge(ssq2_ready, i + 1)
                    fn(std2[0:r, i:i + 1], ssq2[0:r, i:i + 1], ACT.Sqrt, scale=1.0 / D, bias=const("eps", r)).then_inc(std2_ready, 1)
                elif kind == "XR":
                    take(act, "2b", "M", t)
                    copy(x2T[:, 4 * t[2]:4 * t[2] + 4, 0:r], four(ps[:, 7, :], r)).then_inc(emptied["2bM"], 1)
                elif kind == "LG":
                    act.wait_ge(logits_split, i + 1)
                    fn(gexp[0:r, :], G8[0:r, 0:NG], ACT.Exp, bias=r1[0:r, 0:1], accum_out=r1[0:r, 2:3])
                    fn(r1[0:r, 3:4], r1[0:r, 1:2], ACT.Exp).then_inc(gexp_ready, 1)

            for t in tasks:
                kind, i = t[0], t[1]
                if kind == "S":
                    h, w = t[2], P * (i + 1)
                    probs = Sm[:, (i * NH + h) % 3, 0:w]
                    act.wait_ge(s_masked, i * NH + h + 1)
                    fn(probs, probs, ACT.Exp, bias=nb[:, h:h + 1], scale=SCALE,
                       accum_out=esum[:, 8 * (i % 2) + h:8 * (i % 2) + h + 1]).then_inc(s_exp, 1)
                elif kind == "T":
                    h = t[2]
                    part = pt_use[t + (0,)]
                    n = min(4, i + 1)
                    take(act, "2b", f"PT{part}", t + (0,))
                    if i * NH + h >= 2:
                        act.wait_ge(av_done, i * NH + h - 1)
                    copy(PT[:, h % 2, 0:n, :], ps[:, 4 + part, 0:n * P].rearrange("p (j q) -> p j q", q=P))\
                        .then_inc(emptied[f"2bPT{part}"], 1)
                elif kind != "V":
                    tail(t)
            act.drain().then_inc(prompts_done, 1)
            act.wait_ge(prompts_done, 3)
            tiles_out(act, h_out, NT)
            tiles_out(act, x2_out, NT)

            flat = ps[:, :, :].rearrange("p b n -> p (b n)")

            def keep_keys(b):
                for c in (2, 3):
                    part = tk_use["k", b, c]
                    take(act, "2c", f"TK{part}", ("k", b, c))
                    copy(KTs[:, 512 * c:512 * (c + 1)], ps[:, 5 + part, :]).then_inc(emptied[f"2cTK{part}"], 1)

            def exps(b):
                act.wait_ge(smax_ready, b + 1)
                fn(Ps[0:SR, :], flat[0:SR, 0:LS], ACT.Exp, bias=snb[:, b:b + 1], scale=SCALE,
                   accum_out=sesum[:, b:b + 1]).then_inc(emptied["2cSS"], 1)

            def keep_probs(b):
                for c in range(3):
                    part = tk_use["p", b, c]
                    take(act, "2c", f"TK{part}", ("p", b, c))
                    if c == 0 and b:
                        take(act, "2c", "PV", b - 1)
                    if c < 2:
                        copy(PTs[:, 8 * c:8 * c + 8, :], ps[:, 5 + part, :].rearrange("p (a t) -> p a t", a=8)).then_inc(emptied[f"2cTK{part}"], 1)
                    else:
                        copy(PTs[0:ST, SLOTS, :], ps[0:ST, 5 + part, 0:SR]).then_inc(emptied[f"2cTK{part}"], 1)

            def keep_values(b):
                take(act, "2c", "PV", b)
                act.wait_ge(sinv_ready, b + 1)
                if b:
                    take(act, "2c", f"TK{tk_use['o', b - 1, 0]}", ("o", b - 1, 0))
                copy(Os[0:SR, :], ps[0:SR, 7, 0:P], scale=seinv[:, b:b + 1]).then_inc(emptied["2cPV"], 1)

            def keep_turned(b):
                part = tk_use["o", b, 0]
                take(act, "2c", f"TK{part}", ("o", b, 0))
                for g in range(NKV):
                    pv = ps[HD * g:HD * (g + 1), 5 + part, 32 * g:32 * g + 32].rearrange("p (h t) -> p h t", h=GH)
                    ins = copy(mixS[HD * g:HD * (g + 1), :, b * ST:(b + 1) * ST], pv)
                ins.then_inc(emptied[f"2cTK{part}"], 1)

            keep_keys(0)
            exps(0)
            keep_keys(1)
            for b in range(SB):
                keep_probs(b)
                if b:
                    keep_turned(b - 1)
                if b + 1 < SB:
                    exps(b + 1)
                if b + 2 < SB:
                    keep_keys(b + 2)
                keep_values(b)
            keep_turned(SB - 1)
            for t in tail_tasks(NT):
                tail(t)
            act.drain().then_inc(phase2, 1)
            act.wait_ge(phase2, 4)

            def silu(q, u):
                e, s = q * WSLOTS + u, u % 2
                act.wait_ge(gu_filled, e + 1)
                if above(e, 1):
                    act.wait_ge(hid_ready, q * WSLOTS + (u - 1))
                fn(sg[:, s, :], ps[:, 2 + s, 0:2 * CAP], ACT.Silu).then_inc(silu_ready, 1)

            def keep_xgT(q, u):
                act.wait_ge(xT_filled[0], q * WSLOTS + (u + 1))
                copy(xgT[:, u % 2, 0:4, :], four(ps[:, 0, :], CAP)).then_inc(xT_emptied[0], 1)

            def keep_out(q, u):
                e, s = q * WSLOTS + u, u % 2
                act.wait_ge(dn_filled[0], e + 1)
                if above(e, 1):
                    act.wait_ge(eo_out[s], pair(q, u) * 16)
                copy(ob[0:CAP, s, 0:512], ps[0:CAP, 5, :]).then_inc(dn_emptied[0], 1)
                for c in range(2):
                    act.wait_ge(dn_emptied[c], e + 1)
                act.dma_start(block_rows(e), ob[0:CAP, s, :]).then_inc(eo_out[s], 16)

            def experts(q, last=False):
                for u in range(WSLOTS):
                    silu(q, u)
                    if u < WSLOTS - 1 or not last:
                        keep_xgT(q, u + 1) if u < WSLOTS - 1 else keep_xgT(q + 1, 0)
                    keep_out(q, u)

            keep_xgT(0, 0)
            experts(0)
            with act.Fori(1, NE // WSLOTS - 1) as q:
                experts(q)
            experts(NE // WSLOTS - 1, last=True)
            for s in range(2):
                act.wait_ge(eo_out[s], 16 * (NE // 2))
            act.wait_ge(dest_ready, 1)
            some = act.value_load(ovb[0:1, OVB:OVB + 1], min_val=0, max_val=OVB)
            with act.If(some > 0):
                act.nop().then_inc(ov_out, 16)
                with act.Fori(0, OVB) as j:
                    act.wait_ge(ov_pe, j * 3 + 5)
                    fn(sg[:, 0, :], ps[:, 2, 0:2 * CAP], ACT.Silu).then_inc(ov_act, 1)
                    act.wait_ge(ov_dve, j * 3 + 6)
                    act.dma_start(block_rows(j + NE), ob[0:CAP, 0, :]).then_inc(ov_out, 16)
                act.wait_ge(ov_out, 16 * OVB + 16)
            with act.Else():
                act.nop()
            act.drain().then_inc(experts_done, 1)
            for i in range(TILES):
                r, s = rows(i), i % 2
                act.wait_ge(ysum_ready, 2 * (i + 1))
                if i:
                    act.wait_ge(std3_ready, i)
                fn(sq[0:r, :], hc[0:r, i, :], ACT.Square, accum_out=ssq3[0:r, i:i + 1]).then_inc(ssq3_ready, 1)
                act.wait_ge(ssq3_ready, i + 1)
                fn(std3[0:r, i:i + 1], ssq3[0:r, i:i + 1], ACT.Sqrt, scale=1.0 / D, bias=const("eps", r)).then_inc(std3_ready, 1)

        @block.vector
        def _(dve):
            v = nc.vector
            steps = [0]

            def link(ins):
                steps[0] += 1
                ins.then_inc(dve_step, 1)
                dve.wait_ge(dve_step, steps[0])

            def inv_rms(n):
                r = rows(ORDER[n])
                x = xb[0:r, n % 3, :]
                dve.wait_ge(x_in[n % 3], 16 * (n // 3 + 1))
                v.tensor_tensor_reduce(out=junk[0:r, 0:D], in0=x, in1=x, scale=1.0, scalar=0.0, op0=ALU.mult, op1=ALU.add,
                                       accum_out=ssq[0:r, n:n + 1]).then_inc(ssq_ready, 1)
                dve.wait_ge(std_ready, n + 1)
                v.reciprocal(rstd[0:r, n:n + 1], std[0:r, n:n + 1]).then_inc(rstd_ready, 1)

            def add_scores(n):
                i = ORDER[n]
                sc = scv(i)
                for m, lo, w, h in score_steps[n]:
                    copied(dve, "1", f"S{m % 2}", ("s", m))
                    dst, src, wt = sc[:, lo:lo + w], rl[:, m % 2, 0:w], W[:, i, h:h + 1]
                    if h == 0:
                        v.tensor_scalar(dst, src, wt, None, ALU.mult).then_inc(score_added, 1)
                    else:
                        dve.wait_ge(score_added, m)
                        v.scalar_tensor_tensor(out=dst, in0=src, scalar=wt, in1=dst, op0=ALU.mult, op1=ALU.add).then_inc(score_added, 1)
                dve.wait_ge(score_added, score_steps[n][-1][0] + 1)

            def bound(group, c0):
                R, cols = group[0][2], slice(c0, c0 + len(group))
                lo, hi, mid = (x[0:R, cols] for x in (lo_, hi_, mid_))
                for a, (sc, w, _, lastmask, _, _) in enumerate(group):
                    v.tensor_reduce(lo[:, a:a + 1], sc, AX.X, ALU.min)
                    yield "long"
                    link(v.tensor_reduce(hi[:, a:a + 1], sc, AX.X, ALU.max))
                    k = lastmask.shape[1]
                    ins = v.tensor_tensor(sc[:, w - k:w], sc[:, w - k:w], lastmask, ALU.add)
                link(ins)
                v.tensor_scalar(lo, lo, 0.5, None, ALU.mult)
                link(v.tensor_scalar(hi, hi, 0.5, None, ALU.mult))
                link(v.tensor_tensor(mid, lo, hi, ALU.add))

            def halve(group, c0, step, base):
                n = len(group)
                R, cols = group[0][2], slice(c0, c0 + n)
                lo, hi, mid, midh, cnt, t1, t2 = (x[0:R, cols] for x in (lo_, hi_, mid_, midh_, cnt_, t1_, t2_))
                yield "long"
                if not isinstance(base, int) or base:
                    dve.wait_ge(step, base)
                v.tensor_scalar(midh, mid, 0.5, None, ALU.mult)
                for a, (sc, w, _, _, _, bufs) in enumerate(group):
                    if a >= 3:
                        dve.wait_ge(step, base + (a - 2))
                    v.tensor_scalar(bufs[a % 3][0:R, 0:w], sc, mid[:, a:a + 1], None, ALU.is_ge, ALU.add,
                                    accum_out=cnt[:, a:a + 1]).then_inc(step, 1)
                yield "short"
                dve.wait_ge(step, base + n)
                v.tensor_scalar(t1, cnt, float(TOPK), -2 * BIG, ALU.is_lt, ALU.mult)
                v.tensor_scalar(t2, cnt, float(TOPK), 2 * BIG, ALU.is_ge, ALU.mult).then_inc(step, 1)
                yield "short"
                dve.wait_ge(step, base + (n + 1))
                v.tensor_tensor(t1, t1, midh, ALU.add)
                v.tensor_tensor(t2, t2, midh, ALU.add).then_inc(step, 1)
                yield "short"
                dve.wait_ge(step, base + (n + 2))
                v.tensor_tensor(lo, lo, t1, ALU.max)
                v.tensor_tensor(hi, hi, t2, ALU.min).then_inc(step, 1)
                yield "short"
                dve.wait_ge(step, base + (n + 3))
                v.tensor_tensor(mid, lo, hi, ALU.add).then_inc(step, 1)

            def unhalve(group, c0):
                R, cols = group[0][2], slice(c0, c0 + len(group))
                v.tensor_scalar(lo_[0:R, cols], lo_[0:R, cols], 2.0, None, ALU.mult)
                link(v.tensor_scalar(hi_[0:R, cols], hi_[0:R, cols], 2.0, None, ALU.mult))

            def admit(entry, c):
                sc, w, R, _, out, (_, G, T) = entry
                g, t, nd = G[0:R, 0:w], T[0:R, 0:w], need_[0:R, c:c + 1]
                yield "long"
                link(v.tensor_scalar(g, sc, hi_[0:R, c:c + 1], None, ALU.is_gt, ALU.add, accum_out=nd))
                yield "long"
                v.tensor_scalar(nd, nd, -1.0, float(TOPK), ALU.mult, ALU.add)
                link(v.scalar_tensor_tensor(out=t, in0=sc, scalar=lo_[0:R, c:c + 1], in1=g, op0=ALU.is_ge, op1=ALU.subtract))
                yield "long"
                link(v.tensor_tensor_scan(sc, t, t, 0.0, ALU.add, ALU.max))
                yield "long"
                link(v.scalar_tensor_tensor(out=t, in0=sc, scalar=nd, in1=t, op0=ALU.is_le, op1=ALU.mult))
                yield "long"
                link(v.scalar_tensor_tensor(out=t, in0=t, scalar=-1.0, in1=g, op0=ALU.add, op1=ALU.add))
                yield "long"
                link(v.tensor_scalar(out, t, BIG, None, ALU.mult))

            def run(pieces):
                for _ in pieces:
                    pass

            def prompt_group(tiles):
                return [(scv(i), P * (i + 1), P, const("dmask"), maskv(i), (junk, selG, selT)) for i in tiles]

            def halvings(group, c0, times):
                base, per = steps[0], len(group) + 4
                with dve.Fori(0, times // 2) as it:
                    for half in range(2):
                        run(halve(group, c0, dve_step, it * (2 * per) + (base + half * per)))
                steps[0] += per * times
                dve.wait_ge(dve_step, steps[0])

            def admit_group(group, c0):
                unhalve(group, c0)
                for a, entry in enumerate(group):
                    run(admit(entry, c0 + a))

            def select(group, c0, step, ready):
                per = len(group) + 4
                yield "long"
                yield from bound(group, c0)
                for k in range(ITERS):
                    yield from halve(group, c0, step, k * per)
                yield "short"
                dve.wait_ge(step, ITERS * per)
                unhalve(group, c0)
                for a, entry in enumerate(group):
                    yield from admit(entry, c0 + a)
                dve.nop().then_inc(ready, 1)

            def advance(work, pieces, long):
                for _ in range(pieces):
                    if work and (long or work[1] == "short"):
                        work[1] = next(work[0], None)
                        if work[1] is None:
                            work.clear()
                            return

            def begin(*selection):
                work = select(*selection)
                return [work, next(work)]

            inv_rms(0)
            inv_rms(1)
            near, far = prompt_group((2, 3, 4)), prompt_group((6, 7))
            for n in range(TILES + 1):
                if n + 2 < TILES:
                    inv_rms(n + 2)
                if n == TILES - 2:
                    run(bound(near, 0))
                if n in EARLY:
                    halvings(near, 0, EARLY[n])
                if n and score_steps[n - 1]:
                    add_scores(n - 1)
            dve.drain().then_inc(phase1, 1)
            halvings(near, 0, ITERS - sum(EARLY.values()))
            middle = prompt_group((5,))
            run(bound(middle, 3))
            halvings(middle, 3, ITERS)
            take(dve, "2a", "TR", (SB - 1, 1))
            admit_group(near, 0)
            admit_group(middle, 3)
            dve.wait_ge(phase1, 4)
            dve.wait_ge(phase2a, 3)
            link(v.memset(ASUM[:, :], 0.0))
            for k in range(2):
                link(v.tensor_scalar(behind[:, :, k], const("tokid"), float(NBLK * CAP + k * NTOK), None, ALU.add))
            link(v.memset(G8[:, NG:8], -BIG))
            link(v.memset(A[:, :], 0.0))
            link(v.memset(RK[:, :, :], 0.0))
            link(v.memset(EF[:, :, :], 0.0))
            dve.wait_ge(init_done, 6)

            def route(i):
                r = rows(i)
                v.tensor_tensor(L[0:r, :], ps[0:r, 7, 0:36], bias36[0:r, :], ALU.add).then_inc(emptied["2bM"], 1)
                copied(dve, "2b", "M", ("LG", i))
                link(v.tensor_copy(G8[0:r, 0:NG], L[0:r, 0:NG]))
                link(v.max(gm8[0:r, :], G8[0:r, :]))
                link(v.max_index(gi8[0:r, :], gm8[0:r, :], G8[0:r, :]))
                link(v.tensor_copy(r1[0:r, 4:5], gi8[0:r, 0:1]))
                link(v.tensor_scalar(oh4[0:r, :], const("iota", r)[:, 0:NG], r1[0:r, 4:5], None, ALU.is_equal))
                link(v.tensor_scalar(oh4[0:r, :], oh4[0:r, :], -1.0, BIG, ALU.add, ALU.mult))
                pen = oh4[0:r, :].unsqueeze(2).broadcast_to([r, NG, EPG])
                link(v.tensor_tensor(E32[0:r, :].rearrange("p (g e) -> p g e", g=NG), L[0:r, NG:36].rearrange("p (g e) -> p g e", g=NG),
                                     pen, ALU.add))
                link(v.max(em8[0:r, :], E32[0:r, :]))
                link(v.max_index(ei8[0:r, :], em8[0:r, :], E32[0:r, :]))
                link(v.tensor_scalar(r1[0:r, 0:1], gm8[0:r, 0:1], -1.0, None, ALU.mult))
                v.tensor_tensor(r1[0:r, 1:2], em8[0:r, 1:2], em8[0:r, 0:1], ALU.subtract).then_inc(logits_split, 1)
                link(v.tensor_copy(EF[0:r, i, :], ei8[0:r, 0:2]))
                for k in range(2):
                    link(v.tensor_scalar(OH[0:r, k, :], const("iota", r), EF[0:r, i, k:k + 1], None, ALU.is_equal))
                v.tensor_tensor(A[0:r, :], OH[0:r, 0, :], OH[0:r, 1, :], ALU.add).then_inc(A_ready, 1)

            def weigh(i):
                r = rows(i)
                dve.wait_ge(gexp_ready, i + 1)
                link(v.tensor_scalar(r1[0:r, 5:6], r1[0:r, 3:4], 1.0, None, ALU.add))
                link(v.tensor_tensor(r1[0:r, 5:6], r1[0:r, 5:6], r1[0:r, 2:3], ALU.mult))
                link(v.reciprocal(CW[0:r, i, 0:1], r1[0:r, 5:6]))
                link(v.tensor_tensor(CW[0:r, i, 1:2], CW[0:r, i, 0:1], r1[0:r, 3:4], ALU.mult))

            def rank(i):
                r = rows(i)
                for k in range(2):
                    ins = v.tensor_tensor_reduce(out=rkt[0:r, :], in0=ps[0:r, 7, 0:NE], in1=OH[0:r, k, :], scale=1.0, scalar=0.0,
                                                 op0=ALU.mult, op1=ALU.add, accum_out=RK[0:r, i, k:k + 1])
                    if k == 0:
                        link(ins)
                ins.then_inc(emptied["2bM"], 1)
                copied(dve, "2b", "M", ("RK", i))
                v.tensor_tensor(ASUM[0:r, :], ASUM[0:r, :], A[0:r, :], ALU.add).then_inc(ASUM_ready, 1)
                dve.wait_ge(ASUM_ready, i + 1)
                link(v.tensor_scalar(FF[0:r, :], RK[0:r, i, :], float(CAP), float(NBLK * CAP + 2 * NTOK), ALU.is_ge, ALU.mult))
                link(v.tensor_tensor(FF[0:r, :], FF[0:r, :], RK[0:r, i, :], ALU.add))
                link(v.scalar_tensor_tensor(out=FF[0:r, :], in0=EF[0:r, i, :], scalar=float(CAP), in1=FF[0:r, :],
                                            op0=ALU.mult, op1=ALU.add))
                link(v.tensor_tensor(FF[0:r, :], FF[0:r, :], behind[0:r, i, :], ALU.min))
                v.tensor_copy(first[0:r, i, :], FF[0:r, :]).then_inc(first_ready, 1)

            def tail(t):
                kind, i = t[0], t[1]
                r, s = rows(i), i % 2
                if kind == "OP":
                    take(dve, "2b", "M", t)
                    dve.wait_ge(xr_in[s], 16 * (i // 2 + 1))
                    half = hb[0:r, s, 512 * t[2]:512 * t[2] + 512]
                    v.tensor_tensor(half, ps[0:r, 7, :], half, ALU.add).then_inc(emptied["2bM"], 1)
                elif kind == "NM":
                    dve.wait_ge(std2_ready, i + 1)
                    if i == 0:
                        dve.wait_ge(gb_in, 16)
                    link(v.reciprocal(rstd2[0:r, i:i + 1], std2[0:r, i:i + 1]))
                    v.scalar_tensor_tensor(out=x2[0:r, s, :], in0=hb[0:r, s, :], scalar=rstd2[0:r, i:i + 1], in1=gb[0:r, :],
                                           op0=ALU.mult, op1=ALU.mult).then_inc(x2_ready, 1)
                elif kind == "LG":
                    take(dve, "2b", "M", t)
                    if i == 0:
                        dve.wait_ge(rw_in, 64)
                    route(i)
                elif kind == "RK":
                    weigh(i)
                    take(dve, "2b", "M", t)
                    rank(i)

            def last_chunk(i, h):
                return ("T", i, h, 4 if i >= 4 else 0)

            far_tiles = begin(far, 4, far_step, masks_ready)
            samples = begin([(SCs[0:SR, :], LS, SR, const("tailmask", SR), smask[0:SR, :], (sJ, sG, sT))], 6, sample_step, smask_ready)
            for t in tasks:
                kind, i = t[0], t[1]
                if t == ("S", NT - 2, 0):
                    assert not far_tiles
                if kind == "S":
                    h, w, idx = t[2], P * (i + 1), i * NH + t[2]
                    take(dve, "2b", f"A{h % 2}", t)
                    if idx >= 3:
                        key = last_chunk(*divmod(idx - 3, NH))
                        take(dve, "2b", f"PT{pt_use[key]}", key)
                    sc2 = ps[:, 2 * (h % 2):2 * (h % 2) + 2, :].rearrange("p b n -> p (b n)")[:, 0:w]
                    v.tensor_tensor_reduce(out=Sm[:, idx % 3, 0:w], in0=sc2, in1=maskv(i), scale=1.0, scalar=-3e38, op0=ALU.add,
                                           op1=ALU.max, accum_out=mx[:, h:h + 1]).then_inc(emptied[f"2bA{h % 2}"], 1)
                    copied(dve, "2b", f"A{h % 2}", t)
                    v.tensor_scalar(nb[:, h:h + 1], mx[:, h:h + 1], -SCALE, None, ALU.mult).then_inc(s_masked, 1)
                elif kind == "T":
                    h = t[2]
                    if i >= 4:
                        part = pt_use[t + (4,)]
                        n = i + 1 - 4
                        take(dve, "2b", f"PT{part}", t + (4,))
                        if i * NH + h >= 2:
                            dve.wait_ge(av_done, i * NH + h - 1)
                        v.tensor_copy(PT[:, h % 2, 4:4 + n, :], ps[:, 4 + part, 0:n * P].rearrange("p (j q) -> p j q", q=P))\
                            .then_inc(emptied[f"2bPT{part}"], 1)
                elif kind == "V":
                    if t[2] == NH - 1:
                        take(dve, "2b", "O", ("V", i))
                        if i:
                            take(dve, "2b", "M", ("OT", i - 1))
                        dve.wait_ge(s_exp, (i + 1) * NH)
                        e8 = slice(8 * (i % 2), 8 * (i % 2) + 8)
                        link(v.reciprocal(einv[:, e8], esum[:, e8]))
                        inv = einv[:, e8].rearrange("p (g b) -> p g b", g=NKV).unsqueeze(3).broadcast_to([P, NKV, GH, HD])
                        v.tensor_tensor(Osb[:, :].rearrange("p (b g d) -> p g b d", g=NKV, b=GH),
                                        ps[:, 6, :].rearrange("p (g b d) -> p g b d", g=NKV, b=GH), inv, ALU.mult)\
                            .then_inc(emptied["2bO"], 1)
                else:
                    tail(t)
                if kind in PIECES and t[1:] != (NT - 1, NH - 1):
                    pieces, long = PIECES[kind]
                    long = long and t[2] < NH - 1 or kind == "T" and i >= 3 and t[2] == 3
                    advance(far_tiles, pieces, long)
                    if (i, t[2]) >= SAMPLES_FROM:
                        advance(samples, pieces, long)
            assert not samples
            dve.drain().then_inc(prompts_done, 1)
            dve.wait_ge(prompts_done, 3)
            flat = ps[:, :, :].rearrange("p b n -> p (b n)")
            def keep_keys(b):
                for c in (0, 1):
                    part = tk_use["k", b, c]
                    take(dve, "2c", f"TK{part}", ("k", b, c))
                    v.tensor_copy(KTs[:, 512 * c:512 * (c + 1)], ps[:, 5 + part, :]).then_inc(emptied[f"2cTK{part}"], 1)

            keep_keys(0)
            for b in range(SB):
                take(dve, "2c", "SS", b)
                link(v.tensor_reduce(smx[:, b:b + 1], flat[0:SR, 0:LS], AX.X, ALU.max))
                v.tensor_scalar(snb[:, b:b + 1], smx[:, b:b + 1], -SCALE, None, ALU.mult).then_inc(smax_ready, 1)
                if b + 1 < SB:
                    keep_keys(b + 1)
                copied(dve, "2c", "SS", b)
                v.reciprocal(seinv[:, b:b + 1], sesum[:, b:b + 1]).then_inc(sinv_ready, 1)
            for t in tail_tasks(NT):
                tail(t)
            take(dve, "2b", "M", "count")
            v.tensor_copy(cntE[:, :], ps[:, 7, 0:NE]).then_inc(emptied["2bM"], 1)
            copied(dve, "2b", "M", "count")
            dve.drain().then_inc(phase2, 1)
            link(v.tensor_scalar(ovT[:, :], const("iota"), float(CAP), float(CAP), ALU.mult, ALU.add))
            many = NTOK // CAP
            wide = sG.bitcast(F32)[:, 0:NE * many].rearrange("p (e j) -> p e j", e=NE)
            link(v.tensor_tensor(wide, cntE[:, :].unsqueeze(2).broadcast_to([P, NE, many]),
                                 ovT[:, 0:many].unsqueeze(1).broadcast_to([P, NE, many]), ALU.is_gt))
            link(v.tensor_reduce(ovE[:, :], wide, AX.X, ALU.add))
            link(v.memset(ovT[:, :], 0.0))
            link(v.tensor_tensor_scan(ovX[:, :], ovE[:, :], ovT[:, :], 0.0, ALU.add, ALU.add))
            link(v.tensor_tensor(ovS[:, :], ovX[:, :], ovE[:, :], ALU.subtract))
            efl, rkf = EF[:, :, :].rearrange("p i k -> p (i k)"), RK[:, :, :].rearrange("p i k -> p (i k)")
            n = 2 * TILES
            wide = sG.bitcast(F32)[:, 0:n * NE].rearrange("p (a e) -> p a e", e=NE)
            link(v.tensor_tensor(wide, const("iota").unsqueeze(1).broadcast_to([P, n, NE]),
                                 efl.unsqueeze(2).broadcast_to([P, n, NE]), ALU.is_equal))
            link(v.tensor_tensor(wide, wide, ovS[:, :].unsqueeze(1).broadcast_to([P, n, NE]), ALU.mult))
            link(v.tensor_reduce(OS[:, :], wide, AX.X, ALU.add))
            link(v.scalar_tensor_tensor(out=DF[:, :], in0=OS[:, :], scalar=1.0, in1=efl, op0=ALU.mult, op1=ALU.subtract))
            link(v.tensor_scalar(DF[:, :], DF[:, :], float(CAP), float((NE - 1) * CAP), ALU.mult, ALU.add))
            link(v.tensor_scalar(DB[:, :], rkf, float(CAP), None, ALU.is_ge))
            link(v.tensor_tensor(DF[:, :], DF[:, :], DB[:, :], ALU.mult))
            link(v.tensor_tensor(DF[:, :], DF[:, :], rkf, ALU.add))
            link(v.scalar_tensor_tensor(out=DF[:, :], in0=efl, scalar=float(CAP), in1=DF[:, :], op0=ALU.mult, op1=ALU.add))
            link(v.tensor_copy(dest[:, :, :].rearrange("p i k -> p (i k)"), DF[:, :]))
            wide = sG.bitcast(F32)[:, 0:OVB * NE].rearrange("p (j e) -> p j e", e=NE)
            link(v.tensor_tensor(wide, ovX[:, :].unsqueeze(1).broadcast_to([P, OVB, NE]),
                                 const("iota")[:, 0:OVB].unsqueeze(2).broadcast_to([P, OVB, NE]), ALU.is_le))
            link(v.tensor_reduce(ovf[:, 0:OVB], wide, AX.X, ALU.add))
            link(v.tensor_copy(ovf[:, OVB:OVB + 1], ovX[:, NE - 1:NE]))
            link(v.tensor_scalar(ovf[:, 0:OVB], ovf[:, 0:OVB], float(NE - 1), None, ALU.min))
            v.tensor_copy(ovb[:, :], ovf[:, :]).then_inc(dest_ready, 1)
            dve.wait_ge(phase2, 4)

            def gated(s):
                return v.tensor_tensor(hT[:, s].rearrange("p c t -> p (c t)"), sg[:, s, :], ps[:, 2 + s, 2 * CAP:4 * CAP], ALU.mult)

            def gate(q, u):
                dve.wait_ge(silu_ready, q * WSLOTS + (u + 1))
                gated(u % 2).then_inc(hid_ready, 1)

            def keep_xgT(q, u):
                dve.wait_ge(xT_filled[1], q * WSLOTS + (u + 1))
                v.tensor_copy(xgT[:, u % 2, 4:8, :], ps[:, 1, 0:4 * CAP].rearrange("p (j t) -> p j t", j=4)).then_inc(xT_emptied[1], 1)

            def keep_out(q, u):
                e, s = q * WSLOTS + u, u % 2
                dve.wait_ge(dn_filled[1], e + 1)
                if above(e, 1):
                    dve.wait_ge(eo_out[s], pair(q, u) * 16)
                v.tensor_copy(ob[0:CAP, s, 512:1024], ps[0:CAP, 6, :]).then_inc(dn_emptied[1], 1)

            def experts(q, last=False):
                for u in range(WSLOTS):
                    gate(q, u)
                    if u < WSLOTS - 1 or not last:
                        keep_xgT(q, u + 1) if u < WSLOTS - 1 else keep_xgT(q + 1, 0)
                    keep_out(q, u)

            keep_xgT(0, 0)
            experts(0)
            with dve.Fori(1, NE // WSLOTS - 1) as q:
                experts(q)
            experts(NE // WSLOTS - 1, last=True)
            for s in range(2):
                dve.wait_ge(eo_out[s], 16 * (NE // 2))
            dve.wait_ge(dest_ready, 1)
            some = dve.value_load(ovb[0:1, OVB:OVB + 1], min_val=0, max_val=OVB)
            with dve.If(some > 0):
                dve.nop().then_inc(ov_dve, 3)
                with dve.Fori(0, OVB) as j:
                    dve.wait_ge(ov_pe, j * 3 + 4)
                    v.tensor_copy(xgT[:, 0].rearrange("p (a j) t -> p a (j t)", a=2), ps[:, 0:2, 0:4 * CAP]).then_inc(ov_dve, 1)
                    dve.wait_ge(ov_act, j + 1)
                    gated(0).then_inc(ov_dve, 1)
                    dve.wait_ge(ov_pe, j * 3 + 6)
                    dve.wait_ge(ov_out, j * 16 + 16)
                    v.tensor_copy(ob[0:CAP, 0, :], flat[0:CAP, 5 * 512:7 * 512]).then_inc(ov_dve, 1)
                dve.nop()
            with dve.Else():
                dve.nop()
            dve.wait_ge(hc_in, 16 * (TILES + 1))

            def finish(i):
                r = rows(i)
                dve.wait_ge(std3_ready, i + 1)
                link(v.reciprocal(rstd3[0:r, i:i + 1], std3[0:r, i:i + 1]))
                v.scalar_tensor_tensor(out=hc[0:r, i, :], in0=hc[0:r, i, :], scalar=rstd3[0:r, i:i + 1], in1=gb[0:r, :],
                                       op0=ALU.mult, op1=ALU.mult).then_inc(y_ready, 1)

            for i in range(TILES):
                r, s = rows(i), i % OSLOTS
                dve.wait_ge(o_in[i % OQ], 32 * (i // OQ + 1))
                v.scalar_tensor_tensor(out=hc[0:r, i, :], in0=o1[0:r, s, :], scalar=CW[0:r, i, 0:1], in1=hc[0:r, i, :],
                                       op0=ALU.mult, op1=ALU.add).then_inc(ysum_ready, 1)
                dve.wait_ge(ysum_ready, 2 * i + 1)
                v.scalar_tensor_tensor(out=hc[0:r, i, :], in0=o2[0:r, s, :], scalar=CW[0:r, i, 1:2], in1=hc[0:r, i, :],
                                       op0=ALU.mult, op1=ALU.add).then_inc(ysum_ready, 1)
                if i:
                    finish(i - 1)
            finish(TILES - 1)


_INS = ['x_prompt', 'x_sample', 'cache_k', 'cache_v', 'cache_idx_k', 'state_pool', 'page_table', 'norm_mix_g', 'w_in',
        'pool_w', 'pool_scale', 'w_out', 'norm_ffn_g', 'router_group_w', 'router_group_b', 'router_expert_w',
        'router_expert_b', 'expert_w_gate', 'expert_w_up', 'expert_w_down', 'final_norm_g']
_OUTS = [(1, SEQ, D), (SB, ST, D), (1, 1, SEQ, NKV, HD), (1, 1, SEQ, NKV, HD), (1, 1, SEQ, HD), (1, 1, HALO, 512),
         (1, SB, ST, NKV, HD), (1, SB, ST, NKV, HD), (1, SB, ST, HD), (1, SB, HALO, 512)]


def kernel(**inputs):
    import concourse.bacc as bacc
    from concourse.bass_utils import run_bass_kernel_spmd

    nc = bacc.Bacc("TRN2", target_bir_lowering=False, num_devices=1)
    arrays, args = {}, []
    table, spread = constants()
    values = [(name, np.ascontiguousarray(inputs[name])) for name in _INS] + [("const_table", table), ("head_select", spread)]
    for name, a in values:
        arrays[f"in_{name}"] = a
        args.append(nc.dram_tensor(f"in_{name}", a.shape, mybir.dt.from_np(a.dtype), kind="ExternalInput").ap())
    for i, shape in enumerate(_OUTS):
        args.append(nc.dram_tensor(f"out_{i}", shape, F32, kind="ExternalOutput").ap())
    program(nc, *args)
    r = run_bass_kernel_spmd(nc, [arrays], core_ids=[0])
    return tuple(r.results[0][f"out_{i}"] for i in range(len(_OUTS)))
```
